# Optimizing a Trainium2 kernel written in Bass

```python
import math
import jax, jax.numpy as jnp
from jax import lax
import numpy as np
import jax
import jax.numpy as jnp

D_MODEL = 1024
BATCH = 1
SEQ = 256
DEPTH = 2

HEAD_DIM = 64
MIX_WIDTH = D_MODEL
DIFF_WIDTH = MIX_WIDTH // 2
DIFF_HEADS = DIFF_WIDTH // (2 * HEAD_DIM)
SWA_WIDTH = MIX_WIDTH - DIFF_WIDTH
SWA_Q_HEADS = SWA_WIDTH // HEAD_DIM
SWA_KV_HEADS = 2
SWA_GROUP = SWA_Q_HEADS // SWA_KV_HEADS
WINDOW = 128
BLOCK = 128
D_FF = ((8 * D_MODEL // 3 + 127) // 128) * 128
ROPE_THETA = 10000.0
ALPHA = (2.0 * DEPTH) ** 0.25
BETA = (8.0 * DEPTH) ** -0.25
LN_EPS = 1e-5
RMS_EPS = 1e-5

DQ = DIFF_HEADS * 2 * HEAD_DIM
DK = DIFF_HEADS * 2 * HEAD_DIM
DV = DIFF_HEADS * 2 * HEAD_DIM
SQ = SWA_Q_HEADS * HEAD_DIM
SK = SWA_KV_HEADS * HEAD_DIM
SV = SWA_KV_HEADS * HEAD_DIM
IN_COLS = DQ + DK + DV + SQ + SK + SV


def layer_norm(x, g, b):
    xf = x.astype(jnp.float32)
    mu = jnp.mean(xf, axis=-1, keepdims=True)
    var = jnp.mean(jnp.square(xf - mu), axis=-1, keepdims=True)
    y = (xf - mu) * lax.rsqrt(var + LN_EPS) * g.astype(jnp.float32) + b.astype(jnp.float32)
    return y.astype(x.dtype)

def swiglu(x, w_in, w_out):
    h = x @ w_in
    gate, up = h[..., :D_FF], h[..., D_FF:]
    return (jax.nn.silu(gate) * up) @ w_out

def rope_tables(positions):
    inv = jnp.power(ROPE_THETA, -jnp.arange(0, HEAD_DIM, 2, dtype=jnp.float32) / HEAD_DIM)
    ang = positions.astype(jnp.float32)[..., None] * inv
    ang = jnp.concatenate([ang, ang], axis=-1)[:, :, None, :]
    return jnp.cos(ang), jnp.sin(ang)

def apply_rope(t, cos, sin):
    half = HEAD_DIM // 2
    t1, t2 = t[..., :half], t[..., half:]
    rot = jnp.concatenate([-t2, t1], axis=-1)
    return (t * cos.astype(t.dtype) + rot * sin.astype(t.dtype)).astype(t.dtype)

def diff_attention(q, k, v, lam, subln_g, lambda_init):
    B, S = q.shape[0], q.shape[1]
    nb = S // BLOCK
    scale = HEAD_DIM ** -0.5
    qb = q.reshape(B, nb, BLOCK, DIFF_HEADS, 2, HEAD_DIM).transpose(1, 0, 2, 3, 4, 5)

    def one_block(q_blk):
        s = jnp.einsum('bqhcd,bkhcd->bhcqk', q_blk, k).astype(jnp.float32) * scale
        p = jax.nn.softmax(s, axis=-1)
        a = p[:, :, 0] - lam * p[:, :, 1]
        return jnp.einsum('bhqk,bkhe->bqhe', a.astype(v.dtype), v)

    o = lax.map(one_block, qb)
    o = o.transpose(1, 0, 2, 3, 4).reshape(B, S, DIFF_HEADS, 2 * HEAD_DIM)
    of = o.astype(jnp.float32)
    of = of * lax.rsqrt(jnp.mean(jnp.square(of), axis=-1, keepdims=True) + RMS_EPS)
    of = of * subln_g.astype(jnp.float32) * (1.0 - lambda_init)
    return of.astype(v.dtype).reshape(B, S, DIFF_WIDTH)

def band_mask(S):
    nb = S // BLOCK
    qpos = jnp.arange(nb)[:, None, None] * BLOCK + jnp.arange(BLOCK)[None, :, None]
    kpos = (jnp.arange(nb)[:, None, None] - 1) * BLOCK + jnp.arange(3 * BLOCK)[None, None, :]
    return (jnp.abs(qpos - kpos) <= WINDOW) & (kpos >= 0) & (kpos < S)

def swa_sink_attention(q, k, v, sink, mask):
    B, S = q.shape[0], q.shape[1]
    nb = S // BLOCK
    scale = HEAD_DIM ** -0.5
    qb = q.reshape(B, nb, BLOCK, SWA_KV_HEADS, SWA_GROUP, HEAD_DIM)

    def band(t):
        tp = jnp.pad(t, ((0, 0), (BLOCK, BLOCK), (0, 0), (0, 0)))
        tp = tp.reshape(B, nb + 2, BLOCK, SWA_KV_HEADS, HEAD_DIM)
        return jnp.concatenate([tp[:, :-2], tp[:, 1:-1], tp[:, 2:]], axis=2)

    kb, vb = band(k), band(v)
    s = jnp.einsum('bnqhgd,bnkhd->bnhgqk', qb, kb).astype(jnp.float32) * scale
    s = jnp.where(mask[None, :, None, None, :, :], s, -jnp.inf)
    sk = sink.astype(jnp.float32).reshape(1, 1, SWA_KV_HEADS, SWA_GROUP, 1, 1)
    m = jnp.maximum(jnp.max(s, axis=-1, keepdims=True), sk)
    e = jnp.exp(s - m)
    p = e / (jnp.sum(e, axis=-1, keepdims=True) + jnp.exp(sk - m))
    o = jnp.einsum('bnhgqk,bnkhd->bnqhgd', p.astype(v.dtype), vb)
    return o.reshape(B, S, SWA_WIDTH)

def hybrid_mixer(x, cos, sin, mask, w_in, w_out, lam_vec, subln_g, sink, lambda_init):
    B, S = x.shape[0], x.shape[1]
    h = x @ w_in
    o0 = 0
    dq = h[..., o0:o0 + DQ]; o0 += DQ
    dk = h[..., o0:o0 + DK]; o0 += DK
    dv = h[..., o0:o0 + DV]; o0 += DV
    sq = h[..., o0:o0 + SQ]; o0 += SQ
    sk = h[..., o0:o0 + SK]; o0 += SK
    sv = h[..., o0:o0 + SV]

    dq = apply_rope(dq.reshape(B, S, 2 * DIFF_HEADS, HEAD_DIM), cos, sin)
    dk = apply_rope(dk.reshape(B, S, 2 * DIFF_HEADS, HEAD_DIM), cos, sin)
    dq = dq.reshape(B, S, DIFF_HEADS, 2, HEAD_DIM)
    dk = dk.reshape(B, S, DIFF_HEADS, 2, HEAD_DIM)
    dv = dv.reshape(B, S, DIFF_HEADS, 2 * HEAD_DIM)
    lv = lam_vec.astype(jnp.float32)
    lam = jnp.exp(jnp.sum(lv[0] * lv[1])) - jnp.exp(jnp.sum(lv[2] * lv[3])) + lambda_init
    y_diff = diff_attention(dq, dk, dv, lam, subln_g, lambda_init)

    sq = apply_rope(sq.reshape(B, S, SWA_Q_HEADS, HEAD_DIM), cos, sin)
    sk = apply_rope(sk.reshape(B, S, SWA_KV_HEADS, HEAD_DIM), cos, sin)
    sv = sv.reshape(B, S, SWA_KV_HEADS, HEAD_DIM)
    y_swa = swa_sink_attention(sq, sk, sv, sink, mask)

    return jnp.concatenate([y_diff, y_swa], axis=-1) @ w_out

def first_inputs(seed: int = 0) -> dict:
    key = jax.random.key(seed)
    ks = jax.random.split(key, 14)
    f32 = jnp.float32
    x = jax.random.normal(ks[0], (BATCH, SEQ, D_MODEL), f32)
    positions = jnp.broadcast_to(jnp.arange(SEQ, dtype=jnp.int32)[None, :], (BATCH, SEQ))
    col_scale = jnp.concatenate([
        jnp.ones((DQ + DK,), f32), jnp.full((DV,), BETA, f32),
        jnp.ones((SQ + SK,), f32), jnp.full((SV,), BETA, f32)])
    w_in = jax.random.normal(ks[1], (DEPTH, D_MODEL, IN_COLS), f32) * (D_MODEL ** -0.5) * col_scale
    w_out = jax.random.normal(ks[2], (DEPTH, MIX_WIDTH, D_MODEL), f32) * (MIX_WIDTH ** -0.5) * BETA
    diff_lambda = jax.random.normal(ks[3], (DEPTH, 4, HEAD_DIM), f32) * 0.1
    diff_subln_g = 1.0 + 0.02 * jax.random.normal(ks[4], (DEPTH, 2 * HEAD_DIM), f32)
    swa_sink = 0.5 * jax.random.normal(ks[5], (DEPTH, SWA_Q_HEADS), f32)
    ffn1_w_in = jax.random.normal(ks[6], (DEPTH, D_MODEL, 2 * D_FF), f32) * (D_MODEL ** -0.5)
    ffn1_w_out = jax.random.normal(ks[7], (DEPTH, D_FF, D_MODEL), f32) * (D_FF ** -0.5) * BETA
    ffn2_w_in = jax.random.normal(ks[8], (DEPTH, D_MODEL, 2 * D_FF), f32) * (D_MODEL ** -0.5)
    ffn2_w_out = jax.random.normal(ks[9], (DEPTH, D_FF, D_MODEL), f32) * (D_FF ** -0.5) * BETA
    ln_g = 1.0 + 0.02 * jax.random.normal(ks[10], (DEPTH, 3, D_MODEL), f32)
    ln_b = 0.02 * jax.random.normal(ks[11], (DEPTH, 3, D_MODEL), f32)
    return {"x": x, "positions": positions, "w_in": w_in, "w_out": w_out,
            "diff_lambda": diff_lambda, "diff_subln_g": diff_subln_g, "swa_sink": swa_sink,
            "ffn1_w_in": ffn1_w_in, "ffn1_w_out": ffn1_w_out,
            "ffn2_w_in": ffn2_w_in, "ffn2_w_out": ffn2_w_out,
            "ln_g": ln_g, "ln_b": ln_b}

def first_block(x, positions, w_in, w_out, diff_lambda, diff_subln_g, swa_sink,
              ffn1_w_in, ffn1_w_out, ffn2_w_in, ffn2_w_out, ln_g, ln_b):
    S = x.shape[1]
    cos, sin = rope_tables(positions)
    mask = band_mask(S)
    for l in range(DEPTH):
        lambda_init = 0.8 - 0.6 * math.exp(-0.3 * l)
        x = layer_norm(ALPHA * x + 0.5 * swiglu(x, ffn1_w_in[l], ffn1_w_out[l]), ln_g[l, 0], ln_b[l, 0])
        mix = hybrid_mixer(x, cos, sin, mask, w_in[l], w_out[l], diff_lambda[l],
                           diff_subln_g[l], swa_sink[l], lambda_init)
        x = layer_norm(ALPHA * x + mix, ln_g[l, 1], ln_b[l, 1])
        x = layer_norm(ALPHA * x + 0.5 * swiglu(x, ffn2_w_in[l], ffn2_w_out[l]), ln_g[l, 2], ln_b[l, 2])
    return x


CHUNK = 64

D_A = D_MODEL // 2
S5_H = 16
S5_G = D_A // S5_H
S5_P = 64
DT_MIN = 1e-3
DT_MAX = 1e-1
D_B = D_MODEL - D_A
POOL_WINDOWS = (2, 4, 8, 16)
POOL_GROUPS = len(POOL_WINDOWS)
POOL_C = D_B // POOL_GROUPS
SB_HEADS = 16
SB_HEAD_DIM = D_MODEL // SB_HEADS
SB_BLOCK = 128
N_EXPERTS = 16
N_EXPERT_GROUPS = 4
EXPERTS_PER_GROUP = N_EXPERTS // N_EXPERT_GROUPS
TOP_K = 2
D_EXPERT = 512
PLE_DIM = 256
DEEPNORM_ALPHA = (2 * DEPTH) ** 0.25
DEEPNORM_BETA = (8 * DEPTH) ** -0.25
N_EVEN = (DEPTH + 1) // 2
N_ODD = DEPTH // 2


F32 = jnp.float32

def layer_norm_2(x, g, b):
    x32 = x.astype(F32)
    mu = jnp.mean(x32, axis=-1, keepdims=True)
    var = jnp.mean(jnp.square(x32 - mu), axis=-1, keepdims=True)
    return ((x32 - mu) * lax.rsqrt(var + LN_EPS) * g.astype(F32) + b.astype(F32)).astype(x.dtype)

def _complex_linear_combine(e1, e2):
    a1r, a1i, b1r, b1i = e1
    a2r, a2i, b2r, b2i = e2
    ar = a2r * a1r - a2i * a1i
    ai = a2r * a1i + a2i * a1r
    br = a2r * b1r - a2i * b1i + b2r
    bi = a2r * b1i + a2i * b1r + b2i
    return (ar, ai, br, bi)

def s5_mixer(u, lam_re, lam_im, log_dt, b_re, b_im, c_re, c_im, d_skip, w_glu):
    bsz, s, _ = u.shape
    u32 = u.astype(F32).reshape(bsz, s, S5_G, S5_H)
    lam_re = lam_re.astype(F32)
    lam_im = lam_im.astype(F32)
    dt = jnp.exp(log_dt.astype(F32))[:, None]
    mag = jnp.exp(lam_re * dt)
    ang = lam_im * dt
    lb_re = mag * jnp.cos(ang)
    lb_im = mag * jnp.sin(ang)
    den = lam_re * lam_re + lam_im * lam_im
    num_re = lb_re - 1.0
    f_re = (num_re * lam_re + lb_im * lam_im) / den
    f_im = (lb_im * lam_re - num_re * lam_im) / den
    b_re = b_re.astype(F32)
    b_im = b_im.astype(F32)
    bb_re = f_re[..., None] * b_re - f_im[..., None] * b_im
    bb_im = f_re[..., None] * b_im + f_im[..., None] * b_re
    bu_re = jnp.einsum('bsgh,gph->sbgp', u32, bb_re)
    bu_im = jnp.einsum('bsgh,gph->sbgp', u32, bb_im)
    a_re = jnp.broadcast_to(lb_re[None, None], (s, 1, S5_G, S5_P))
    a_im = jnp.broadcast_to(lb_im[None, None], (s, 1, S5_G, S5_P))
    _, _, st_re, st_im = lax.associative_scan(
        _complex_linear_combine, (a_re, a_im, bu_re, bu_im), axis=0)
    y = (jnp.einsum('sbgp,ghp->bsgh', st_re, c_re.astype(F32))
         - jnp.einsum('sbgp,ghp->bsgh', st_im, c_im.astype(F32))
         + d_skip.astype(F32) * u32)
    y = jax.nn.gelu(y.reshape(bsz, s, D_A))
    out = y * jax.nn.sigmoid(y @ w_glu.astype(F32))
    return out.astype(u.dtype)

def pool_mixer(v, pool_w, pool_scale):
    bsz, s, _ = v.shape
    v32 = v.astype(F32).reshape(bsz, s, POOL_GROUPS, POOL_C)
    csum = jnp.cumsum(v32, axis=1)
    t = jnp.arange(s)
    means = []
    for gi, w in enumerate(POOL_WINDOWS):
        c = csum[:, :, gi]
        lagged = jnp.pad(c, ((0, 0), (w, 0), (0, 0)))[:, :s]
        count = jnp.minimum(t + 1, w).astype(F32)[None, :, None]
        means.append((c - lagged) / count)
    pooled = jnp.stack(means, axis=2) - v32
    mixed = jnp.einsum('bsgc,gcd->bsgd', pooled, pool_w.astype(F32))
    return (mixed.reshape(bsz, s, D_B) * pool_scale.astype(F32)).astype(v.dtype)

def stick_breaking_attention(qkv):
    bsz, s, _ = qkv.shape
    q, k, v = jnp.split(qkv.astype(F32), 3, axis=-1)
    to_heads = lambda z: z.reshape(bsz, s, SB_HEADS, SB_HEAD_DIM).transpose(0, 2, 1, 3)
    q, k, v = to_heads(q), to_heads(k), to_heads(v)
    scale = SB_HEAD_DIM ** -0.5
    outs = []
    for blk in range(s // SB_BLOCK):
        q0 = blk * SB_BLOCK
        end = q0 + SB_BLOCK
        z = jnp.einsum('bhqd,bhkd->bhqk', q[:, :, q0:end], k[:, :, :end]) * scale
        t_pos = q0 + jnp.arange(SB_BLOCK)
        s_pos = jnp.arange(end)
        causal = s_pos[None, :] < t_pos[:, None]
        log_keep = jnp.where(causal, jax.nn.log_sigmoid(-z), 0.0)
        log_after = lax.cumsum(log_keep, axis=3, reverse=True) - log_keep
        wts = jnp.where(causal, jnp.exp(jax.nn.log_sigmoid(z) + log_after), 0.0)
        outs.append(jnp.einsum('bhqk,bhkd->bhqd', wts, v[:, :, :end]))
    o = jnp.concatenate(outs, axis=2)
    return o.transpose(0, 2, 1, 3).reshape(bsz, s, D_MODEL).astype(qkv.dtype)

def grouped_moe(x, router_w, router_bias, w1, w3, w2):
    bsz, s, d = x.shape
    xt = x.reshape(-1, d)
    scores = jax.nn.sigmoid((xt @ router_w).astype(F32))
    sel = scores + router_bias.astype(F32)
    grp = sel.reshape(-1, N_EXPERT_GROUPS, EXPERTS_PER_GROUP)
    grp_score = jnp.sum(lax.top_k(grp, TOP_K)[0], axis=-1)
    top_group = jnp.argmax(grp_score, axis=-1)
    in_group = (jnp.arange(N_EXPERTS) // EXPERTS_PER_GROUP)[None, :] == top_group[:, None]
    _, idx = lax.top_k(jnp.where(in_group, sel, -jnp.inf), TOP_K)
    w = jnp.take_along_axis(scores, idx, axis=-1)
    w = w / jnp.sum(w, axis=-1, keepdims=True)
    gates = jnp.sum(jax.nn.one_hot(idx, N_EXPERTS, dtype=F32) * w[..., None], axis=1)
    h = jax.nn.silu(jnp.einsum('td,edf->etf', xt, w1)) * jnp.einsum('td,edf->etf', xt, w3)
    h = h * gates.T[:, :, None].astype(h.dtype)
    y = jnp.einsum('etf,efd->td', h, w2)
    return y.reshape(bsz, s, d).astype(x.dtype)

def second_inputs(seed: int = 0) -> dict:
    key = jax.random.key(seed)
    ks = jax.random.split(key, 32)
    nrm = lambda k, shape, sc: jax.random.normal(k, shape, F32) * sc
    n_idx = jnp.arange(S5_P, dtype=F32)
    return {
        'x': nrm(ks[0], (BATCH, SEQ, D_MODEL), 1.0),
        'p': nrm(ks[1], (DEPTH, BATCH, SEQ, PLE_DIM), 1.0),
        'ab_w_in': nrm(ks[2], (N_EVEN, D_MODEL, D_A + D_B), D_MODEL ** -0.5),
        's5_lambda_re': -0.5 + nrm(ks[3], (N_EVEN, S5_G, S5_P), 0.01),
        's5_lambda_im': math.pi * n_idx + nrm(ks[4], (N_EVEN, S5_G, S5_P), 0.01),
        's5_log_dt': jax.random.uniform(ks[5], (N_EVEN, S5_G), F32, math.log(DT_MIN), math.log(DT_MAX)),
        's5_b_re': nrm(ks[6], (N_EVEN, S5_G, S5_P, S5_H), (2 * S5_H) ** -0.5),
        's5_b_im': nrm(ks[7], (N_EVEN, S5_G, S5_P, S5_H), (2 * S5_H) ** -0.5),
        's5_c_re': nrm(ks[8], (N_EVEN, S5_G, S5_H, S5_P), S5_P ** -0.5),
        's5_c_im': nrm(ks[9], (N_EVEN, S5_G, S5_H, S5_P), S5_P ** -0.5),
        's5_d': nrm(ks[10], (N_EVEN, S5_G, S5_H), 1.0),
        's5_w_glu': nrm(ks[11], (N_EVEN, D_A, D_A), D_A ** -0.5),
        'pool_w': nrm(ks[12], (N_EVEN, POOL_GROUPS, POOL_C, POOL_C), POOL_C ** -0.5),
        'pool_scale': 1.0 + nrm(ks[13], (N_EVEN, D_B), 0.1),
        'ab_w_out': nrm(ks[14], (N_EVEN, D_A + D_B, D_MODEL), (D_A + D_B) ** -0.5 * DEEPNORM_BETA),
        'sb_w_qkv': nrm(ks[15], (N_ODD, D_MODEL, 3 * D_MODEL), D_MODEL ** -0.5),
        'sb_w_out': nrm(ks[16], (N_ODD, D_MODEL, D_MODEL), D_MODEL ** -0.5 * DEEPNORM_BETA),
        'ln_mix_g': 1.0 + nrm(ks[17], (DEPTH, D_MODEL), 0.01),
        'ln_mix_b': nrm(ks[18], (DEPTH, D_MODEL), 0.01),
        'ln_ffn_g': 1.0 + nrm(ks[19], (DEPTH, D_MODEL), 0.01),
        'ln_ffn_b': nrm(ks[20], (DEPTH, D_MODEL), 0.01),
        'router_w': nrm(ks[21], (D_MODEL, N_EXPERTS), D_MODEL ** -0.5),
        'router_bias': nrm(ks[22], (N_EXPERTS,), 0.01),
        'moe_w1': nrm(ks[23], (DEPTH, N_EXPERTS, D_MODEL, D_EXPERT), D_MODEL ** -0.5),
        'moe_w3': nrm(ks[24], (DEPTH, N_EXPERTS, D_MODEL, D_EXPERT), D_MODEL ** -0.5),
        'moe_w2': nrm(ks[25], (DEPTH, N_EXPERTS, D_EXPERT, D_MODEL), D_EXPERT ** -0.5 * DEEPNORM_BETA),
        'ple_w_proj': nrm(ks[26], (DEPTH, PLE_DIM, D_MODEL), PLE_DIM ** -0.5 * DEEPNORM_BETA),
        'ple_w_gate': nrm(ks[27], (DEPTH, D_MODEL, D_MODEL), D_MODEL ** -0.5),
    }

def second_block(x, p, ab_w_in, s5_lambda_re, s5_lambda_im, s5_log_dt, s5_b_re, s5_b_im,
              s5_c_re, s5_c_im, s5_d, s5_w_glu, pool_w, pool_scale, ab_w_out,
              sb_w_qkv, sb_w_out, ln_mix_g, ln_mix_b, ln_ffn_g, ln_ffn_b,
              router_w, router_bias, moe_w1, moe_w3, moe_w2, ple_w_proj, ple_w_gate):
    for i in range(DEPTH):
        j = i // 2
        if i % 2 == 0:
            h = x @ ab_w_in[j]
            out_a = s5_mixer(h[..., :D_A], s5_lambda_re[j], s5_lambda_im[j], s5_log_dt[j],
                             s5_b_re[j], s5_b_im[j], s5_c_re[j], s5_c_im[j], s5_d[j], s5_w_glu[j])
            out_b = pool_mixer(h[..., D_A:], pool_w[j], pool_scale[j])
            mix = jnp.concatenate([out_a, out_b], axis=-1) @ ab_w_out[j]
        else:
            mix = stick_breaking_attention(x @ sb_w_qkv[j]) @ sb_w_out[j]
        x = layer_norm_2(DEEPNORM_ALPHA * x + mix, ln_mix_g[i], ln_mix_b[i])
        ple = (p[i] @ ple_w_proj[i]) * jax.nn.sigmoid(x @ ple_w_gate[i])
        ffn = grouped_moe(x, router_w, router_bias, moe_w1[i], moe_w3[i], moe_w2[i])
        x = layer_norm_2(DEEPNORM_ALPHA * x + ffn + ple, ln_ffn_g[i], ln_ffn_b[i])
    return x


def setup_inputs(seed=0):
    out = dict(first_inputs(seed))
    for name, value in second_inputs(seed + 1).items():
        if name != "x":
            out[name + "_2"] = value
    return out


def reference(
    x, positions, w_in, w_out, diff_lambda, diff_subln_g, swa_sink, ffn1_w_in, ffn1_w_out,
    ffn2_w_in, ffn2_w_out, ln_g, ln_b, p_2, ab_w_in_2, s5_lambda_re_2, s5_lambda_im_2,
    s5_log_dt_2, s5_b_re_2, s5_b_im_2, s5_c_re_2, s5_c_im_2, s5_d_2, s5_w_glu_2, pool_w_2,
    pool_scale_2, ab_w_out_2, sb_w_qkv_2, sb_w_out_2, ln_mix_g_2, ln_mix_b_2, ln_ffn_g_2,
    ln_ffn_b_2, router_w_2, router_bias_2, moe_w1_2, moe_w3_2, moe_w2_2, ple_w_proj_2,
    ple_w_gate_2,
):
    x = first_block(
        x, positions, w_in, w_out, diff_lambda, diff_subln_g, swa_sink, ffn1_w_in, ffn1_w_out,
        ffn2_w_in, ffn2_w_out, ln_g, ln_b,
    )
    return second_block(
        x, p_2, ab_w_in_2, s5_lambda_re_2, s5_lambda_im_2, s5_log_dt_2, s5_b_re_2, s5_b_im_2,
        s5_c_re_2, s5_c_im_2, s5_d_2, s5_w_glu_2, pool_w_2, pool_scale_2, ab_w_out_2,
        sb_w_qkv_2, sb_w_out_2, ln_mix_g_2, ln_mix_b_2, ln_ffn_g_2, ln_ffn_b_2, router_w_2,
        router_bias_2, moe_w1_2, moe_w3_2, moe_w2_2, ple_w_proj_2, ple_w_gate_2,
    )


_drawn_inputs = setup_inputs


def setup_inputs(seed=0):
    import zlib

    import numpy as np

    out = dict(_drawn_inputs(seed))
    spreads = {}
    factors = {'swa_sink': 8.0,
     's5_lambda_re_2': 8.0,
     's5_b_im_2': 2.894,
     's5_c_re_2': 2.69,
     's5_c_im_2': 3.368,
     'ln_ffn_g_2': 3.963}
    for name, (base, spread) in spreads.items():
        noise = np.random.default_rng([zlib.crc32(name.encode()), seed]).standard_normal(out[name].shape)
        drawn = base * np.exp(spread * noise) if base else spread * noise
        out[name] = jnp.asarray(drawn.astype(out[name].dtype))
    for name, factor in factors.items():
        out[name] = (out[name] * factor).astype(out[name].dtype)
    return out
```

```python
import math
from contextlib import ExitStack, contextmanager

import numpy as np
import concourse.bass as bass
from concourse import mybir

ALU = mybir.AluOpType
ACT = mybir.ActivationFunctionType
F32 = mybir.dt.float32
F32R = mybir.dt.float32r
I32 = mybir.dt.int32
AX_X = mybir.AxisListType.X

P = 128
T = 256
TT = T // P
D = 1024
KD = D // P
DEPTH = 2
D_FF = ((8 * D // 3 + 127) // 128) * 128
HALF = 256
FF_STEPS = D_FF // HALF
UNIT = 2048
RAW = 6
SPLIT = 3
AHEAD = 2
ALPHA = (2.0 * DEPTH) ** 0.25
LN_EPS = 1e-5
RMS_EPS = 1e-5
HD = 64
SCALE = HD ** -0.5
FAR = -1e30
DIFF_HEADS = 4
SWA_Q = 8
WINDOW = 128
N_EXPERTS = 16
D_EXPERT = 512
EXPERT_STEPS = D_EXPERT // HALF
MOE_STEPS = N_EXPERTS * EXPERT_STEPS
N_GROUPS = 4
PLE = 256
G5, P5, H5 = 32, 64, 16
S5_TILES = G5 * P5 // P
POOL_WINDOWS = (2, 4, 8, 16)
TWO_PI = 2.0 * math.pi
PI_IN = 3.1415925
ROUND = 1.5 * 2.0 ** 23
TP_HI = 6.28125
TP_MID = float(np.float32(TWO_PI - TP_HI) * 1.0)
TP_MID = math.floor((TWO_PI - TP_HI) * 2.0 ** 21) / 2.0 ** 21
TP_LO = TWO_PI - TP_HI - TP_MID
GELU_C = 2.0 * math.sqrt(2.0 / math.pi)

C_FREQ, C_TIME, C_COUNT, C_PAR, C_END = 0, 32, 288, 352, 354


class Tally:

    def __init__(self, engine):
        self.engine, self.n, self.term = engine, {}, {}

    def __call__(self, sem, k=1):
        self.n[id(sem)] = self.n.get(id(sem), 0) + k
        return self.n[id(sem)] + self.term.get(id(sem), 0)

    def ahead(self, sem, k):
        return self.n.get(id(sem), 0) + k + self.term.get(id(sem), 0)

    @contextmanager
    def loop(self, rounds, per_round):
        start = {id(s): self.n.get(id(s), 0) for s, _ in per_round}
        before = dict(self.n)
        with self.engine.Fori(0, rounds) as i:
            self.term = {id(s): i * k for s, k in per_round}
            yield i
        for s, k in per_round:
            assert self.n.get(id(s), 0) - start[id(s)] == k, (s, k, self.n.get(id(s), 0) - start[id(s)])
            self.n[id(s)] = start[id(s)] + rounds * k
        for key, n in self.n.items():
            assert key in start or n == before.get(key), "a semaphore waited for, but not named"
        self.term = {}


class Gated:

    def __init__(self, gate, up, down, steps, peeled):
        self.gate_v, self.up_v, self.down_v, self.steps, self.peeled = gate, up, down, steps, peeled
        self.rounds = (steps - 1 - peeled) // 2
        assert peeled + 1 + 2 * self.rounds == steps


class FeedForward(Gated):
    def __init__(self, w_in, w_out):
        v = w_in.rearrange("(u k p) (g j c) -> g u j p k c", p=P, u=2, g=2, c=HALF)
        super().__init__(v[0], v[1], w_out.rearrange("(j k p) c -> j p k c", p=P, k=2), FF_STEPS, 2)
        self.experts = False

    def gate_up(self, i, j, u):
        at = 2 * i + j
        if isinstance(at, int):
            return self.gate_v[u, at], self.up_v[u, at]
        return (self.gate_v[u, bass.ds(at, 1)].rearrange("o p k c -> (o p) k c"),
                self.up_v[u, bass.ds(at, 1)].rearrange("o p k c -> (o p) k c"))

    def down(self, i, j):
        at = 2 * i + j
        if isinstance(at, int):
            return self.down_v[at]
        return self.down_v[bass.ds(at, 1)].rearrange("o p k c -> (o p) k c")


class Experts(Gated):
    def __init__(self, w1, w3, w2):
        ins = [w.rearrange("e (u k p) (j c) -> u j e p k c", p=P, u=2, c=HALF) for w in (w1, w3)]
        super().__init__(*ins, w2.rearrange("e (j k p) c -> j e p k c", p=P, k=2), MOE_STEPS, 1)
        self.experts = True

    def pick(self, v, i, j):
        e, half = i + j // EXPERT_STEPS, j % EXPERT_STEPS
        if isinstance(e, int):
            return v[half, e]
        return v[half, bass.ds(e, 1)].rearrange("o p k c -> (o p) k c")

    def gate_up(self, i, j, u):
        return self.pick(self.gate_v[u], i, j), self.pick(self.up_v[u], i, j)

    def down(self, i, j):
        return self.pick(self.down_v, i, j)


def program(nc, a, out):
    with ExitStack() as ctx:
        def sb(name, shape, dt=F32):
            return ctx.enter_context(nc.sbuf_tensor(name, shape, dt))

        def bank(name):
            return ctx.enter_context(nc.psum_tensor(name, [P, 512], F32))

        def sem(name):
            return ctx.enter_context(nc.semaphore(name))

        raw = [sb(f"raw{i}", [P, UNIT]) for i in range(RAW)]
        hi = [sb(f"w_hi{i}", [P, UNIT], F32R) for i in range(SPLIT)]
        lo = [sb(f"w_lo{i}", [P, UNIT], F32R) for i in range(SPLIT)]
        x = sb("x_rows", [P, TT, D])
        xt_hi = sb("xt_hi", [P, KD, T], F32R)
        xt_lo = sb("xt_lo", [P, KD, T], F32R)
        gate_act = sb("gate_act", [P, TT, HALF])
        h = sb("h", [P, TT, HALF])
        ht_hi = sb("ht_hi", [P, 2, T], F32R)
        ht_lo = sb("ht_lo", [P, 2, T], F32R)
        ln_gb = sb("ln_gb", [P, 2, D])
        ident = sb("ident", [P, P])
        stats = sb("stats", [P, TT, 2, 6])
        moments = sb("moments", [P, TT, 2])
        rstd = sb("rstd", [P, TT, 1])
        minus_half = sb("minus_half", [P, 4])
        cst = sb("cst", [P, C_END])
        rope = sb("rope", [P, 2, TT, HD])
        swa_mask = sb("swa_mask", [P, TT, T])
        causal = sb("causal", [P, T])
        gates = sb("gates", [P, TT, N_EXPERTS])
        small = sb("small", [P, 384])
        params = sb("params", [P, 984])
        pool_w = sb("pool_w", [P, 4, P])
        rw_hi = sb("rw_hi", [P, KD, N_EXPERTS], F32R)
        rw_lo = sb("rw_lo", [P, KD, N_EXPERTS], F32R)
        before = sb("before", [P, N_EXPERTS, N_EXPERTS])
        half_pi = sb("half_pi", [P, 1])
        position = sb("position", [P, TT], I32)
        work = sb("work", [P, 14336])

        y_bank = [[bank(f"y{t}{c}") for c in range(2)] for t in range(TT)]
        h_bank = [bank(f"h{t}") for t in range(TT)]
        turn_bank = [bank(f"turn{t}") for t in range(TT)]

        unit_loaded = [sem(f"unit_loaded{i}") for i in range(RAW)]
        hi_ready = sem("hi_ready")
        lo_ready = sem("lo_ready")
        unit_used = sem("unit_used")
        const_loaded = sem("const_loaded")
        const_made = sem("const_made")
        gb_loaded = sem("gb_loaded")
        x_loaded = sem("x_loaded")
        first_half = sem("first_half")
        y_half = sem("y_half")
        gate_ready = sem("gate_ready")
        h_ready = sem("h_ready")
        h_turned = sem("h_turned")
        ht_hi_ready = sem("ht_hi_ready")
        ht_lo_ready = sem("ht_lo_ready")
        var_ready = sem("var_ready")
        rstd_ready = sem("rstd_ready")
        x_ready = sem("x_ready")
        x_turned = sem("x_turned")
        xt_hi_ready = sem("xt_hi_ready")
        xt_lo_ready = sem("xt_lo_ready")
        tile_taken = sem("tile_taken")
        dve_link = sem("dve_link")
        act_link = sem("act_link")
        pool_link = sem("pool_link")
        angles = sem("angles")
        sines = sem("sines")
        x_final = sem("x_final")
        stored = sem("stored")
        lam_sums = sem("lam_sums")
        lam_exps = sem("lam_exps")
        row_ready = sem("row_ready")
        row_turned = sem("row_turned")
        col_ready = sem("col_ready")
        scores_ready = sem("scores_ready")
        neg_ready = sem("neg_ready")
        exp_ready = sem("exp_ready")
        prob_ready = sem("prob_ready")
        prob_turned = sem("prob_turned")
        pt_ready = sem("pt_ready")
        pv_done = sem("pv_done")
        swa_out = sem("swa_out")
        squares = sem("squares")
        sub_rstd = sem("sub_rstd")
        mix_ready = sem("mix_ready")
        zm_ready = sem("zm_ready")
        sp_ready = sem("sp_ready")
        arg_ready = sem("arg_ready")
        w_ready = sem("w_ready")
        s5_loaded = sem("s5_loaded")
        s5_act = sem("s5_act")
        s5_dve = sem("s5_dve")
        wide_ready = sem("wide_ready")
        wide_turned = sem("wide_turned")
        wide_copied = sem("wide_copied")
        turns_ready = sem("turns_ready")
        trig_ready = sem("trig_ready")
        bu_ready = sem("bu_ready")
        scan_ready = sem("scan_ready")
        st_ready = sem("st_ready")
        y_part = sem("y_part")
        pooled = sem("pooled")
        pool_mixed = sem("pool_mixed")
        rw_hi_ready = sem("rw_hi_ready")
        rw_lo_ready = sem("rw_lo_ready")
        routed = sem("routed")
        route_sig = sem("route_sig")
        gates_ready = sem("gates_ready")
        p_loaded = sem("p_loaded")
        ple_sig = sem("ple_sig")

        block = ctx.enter_context(nc.Block())

        ff = [[FeedForward(a["ffn1_w_in"][l], a["ffn1_w_out"][l]), FeedForward(a["ffn2_w_in"][l], a["ffn2_w_out"][l])]
              for l in range(DEPTH)]
        moe = [Experts(a["moe_w1_2"][l], a["moe_w3_2"][l], a["moe_w2_2"][l]) for l in range(DEPTH)]

        def by_rows(w, rows, c0, c1):
            return w[rows[0] * P:rows[1] * P, c0:c1].rearrange("(k p) c -> p k c", p=P)

        @block.sync
        def _(sp):
            seen = Tally(sp)
            n = [0]

            def load(*pieces):
                s = n[0] % RAW
                if n[0] >= RAW:
                    sp.wait_ge(lo_ready, seen(lo_ready))
                k = pieces[0].shape[1]
                dst = raw[s][:, :].rearrange("p (k c) -> p k c", k=k)
                c = UNIT // k // len(pieces)
                for q, src in enumerate(pieces):
                    sp.dma_start(dst[:, :, q * c:(q + 1) * c], src).then_inc(unit_loaded[s], 32 // len(pieces))
                n[0] += 1

            def load_gated(w):
                def step(i, j):
                    load(*w.gate_up(i, j, 0))
                    load(*w.gate_up(i, j, 1))
                    if not isinstance(i, int) or j > 0:
                        load(w.down(i, j - 1))
                for j in range(w.peeled + 1):
                    step(0, j)
                with seen.loop(w.rounds, [(lo_ready, 6)]) as i:
                    step(i, w.peeled + 1)
                    step(i, w.peeled + 2)
                n[0] += 6 * (w.rounds - 1)
                load(w.down(0, w.steps - 1))

            def load_matrix(w, cols, c0=0):
                for c in range(c0, c0 + cols, 512):
                    for u in range(2):
                        load(by_rows(w, (4 * u, 4 * u + 4), c, c + 512))

            for l in range(DEPTH):
                load_gated(ff[l][0])
                load_matrix(a["w_in"][l], 1024)
                load_matrix(a["w_in"][l], 512, 1536)
                load(by_rows(a["w_in"][l], (0, 8), 2048, 2304))
                load_matrix(a["w_in"][l], 512, 1024)
                load_matrix(a["w_out"][l], 1024)
                load_gated(ff[l][1])
            load_matrix(a["ab_w_in_2"][0], 1024)
            load(by_rows(a["s5_w_glu_2"][0], (0, 4), 0, 512))
            load_matrix(a["ab_w_out_2"][0], 1024)
            load_matrix(a["ple_w_gate_2"][0], 1024)
            load(by_rows(a["ple_w_proj_2"][0], (0, 2), 0, 1024))
            load_gated(moe[0])
            load_matrix(a["sb_w_qkv_2"][0], 3072)
            load_matrix(a["sb_w_out_2"][0], 1024)
            load_matrix(a["ple_w_gate_2"][1], 1024)
            load(by_rows(a["ple_w_proj_2"][1], (0, 2), 0, 1024))
            load_gated(moe[1])
            s = n[0] % RAW
            sp.wait_ge(lo_ready, seen(lo_ready))
            sp.dma_start(raw[s][:, 0:P], a["p_2"][0, 0, 0:P, 0:P]).then_inc(unit_loaded[s], 32)
            sp.wait_ge(x_final, TT)
            sp.dma_start(out[0].rearrange("(t p) d -> p t d", p=P), x[:, :, :]).then_inc(stored, 16)
            sp.wait_ge(stored, 16)

        def carve(tensor, at, *dims):
            n = int(np.prod(dims))
            v = tensor[:, at:at + n]
            if len(dims) == 1:
                return v
            names = "abcd"[:len(dims)]
            return v.rearrange(f"p ({' '.join(names)}) -> p {' '.join(names)}",
                               **{k: d for k, d in zip(names[1:], dims[1:])})

        freq, time_row = cst[:, C_FREQ:C_FREQ + 32], cst[:, C_TIME:C_TIME + T]
        count_ratio = carve(cst, C_COUNT, 4, 16)
        parity = cst[:, C_PAR:C_PAR + 2]

        qk = carve(work, 0, TT, 1792)
        qz1 = carve(work, 3584, 8, 2, T)
        kt1 = carve(work, 7680, 6, T)
        v1 = carve(work, 9216, TT, 640)
        rot = carve(work, 10496, 2, 512)
        e1 = carve(work, 11520, 2, 2, T)
        p1 = carve(work, 12544, 2, 2, T)
        pt1 = carve(work, 2048, 2, 512)
        mix = carve(work, 0, TT, D)
        qz2 = carve(work, 0, 8, 2, T)
        kt2 = carve(work, 4096, 8, T)
        v2 = carve(work, 6144, TT, D)
        qk_row = carve(work, 8192, 2, TT, 512)
        zm = carve(work, 8192, 2, 2, T)
        sp_ = carve(work, 9216, 2, 2, T)
        soft = carve(work, 10240, 2, 2, T)
        w2 = carve(work, 11264, 2, 2, T)
        wt2 = carve(work, 12288, 2, 512)
        ab_row = carve(work, 2048, TT, D)
        ab_t = carve(work, 0, 8, T)
        bb_t = carve(work, 4096, 2, 4, P)
        c_t = carve(work, 5120, 2, 4, P)
        trig = carve(work, 6144, 2, 4, T)
        th = carve(work, 8192, 2, 4, T)
        m5 = carve(work, 10240, 2, 2, T)
        s5 = carve(work, 11264, 2, 2, T)
        n5 = carve(work, 12288, 2, 2, T)
        st5 = carve(work, 13312, 2, 2, T)
        b_nat = carve(work, 8192, 2, 16, 16)
        bb_wide = carve(work, 8704, 2, 16, 32)
        c_nat = carve(work, 9728, 2, 4, P5)
        c_wide = carve(work, 10240, 2, 4, P)
        bb_tmp = carve(work, 11264, 2, 16, 16)
        pool_pad = [carve(work, 6144 + 1088 * i, 4, 16 + T) for i in range(2)]
        y5 = carve(work, 8320, 4, T)
        g5 = carve(work, 9344, 4, T)

        lam_in = carve(params, 0, DEPTH, 4, HD)
        sub_g = carve(params, 512, DEPTH, P)
        sink = carve(params, 768, DEPTH, SWA_Q)
        router_w = carve(params, 784, KD, N_EXPERTS)
        router_b = carve(params, 912, N_EXPERTS)
        lam_re, lam_im, log_dt = (carve(params, 928 + 16 * i, S5_TILES) for i in range(3))
        pool_scale = carve(params, 976, 4)
        d_skip = carve(params, 980, 4)
        N_LOADS = 14
        lam = carve(small, 0, DEPTH)
        lam_e = carve(small, 2, DEPTH, 2)
        neg = carve(small, 8, 2, 2)
        sums = carve(small, 12, 2, 2)
        sink_e = carve(small, 16, 2, 2)
        inv = carve(small, 20, 2, 2)
        nmax = carve(small, 24, 2, 2)
        ssq = carve(small, 28, TT, DIFF_HEADS)
        srs = carve(small, 36, TT, DIFF_HEADS)
        neg_sink = carve(small, 44, DEPTH, SWA_Q)
        s5v = [carve(small, 64 + 16 * i, 16) for i in range(20)]
        (dt5, ang5, mag5, k5, r5, sin5, cos5, phi5, abs5, lbr, lbi, den, fre, fim, tmpa, tmpb) = s5v[:16]

        ple_gate = carve(work, 0, TT, D)
        r_s = carve(work, 4096, TT, N_EXPERTS)
        r_sel = carve(work, 4128, TT, N_EXPERTS)
        r_two = carve(work, 4160, 8, TT * N_GROUPS)
        r_grp = carve(work, 4224, TT, N_GROUPS)
        r_rank = carve(work, 4232, TT, N_EXPERTS)
        r_sum = carve(work, 4264, TT)
        r_gt = carve(work, 4352, N_EXPERTS, N_EXPERTS)
        r_eq = carve(work, 4608, N_EXPERTS, N_EXPERTS)

        @block.gpsimd
        def _(pool):
            seen = Tally(pool)

            def link(ins):
                ins.then_inc(pool_link, 1)
                pool.wait_ge(pool_link, seen(pool_link))

            def load(dst, src, to=const_loaded):
                pool.dma_start(dst, src, allow_slow_non_contiguous=True).then_inc(to, 16)

            def load_ln(g, b):
                load(ln_gb[:, 0, :], g.partition_broadcast(P), gb_loaded)
                load(ln_gb[:, 1, :], b.partition_broadcast(P), gb_loaded)

            load(x[:, :, :], a["x"][0].rearrange("(t p) d -> p t d", p=P), x_loaded)
            pool.memset(ident[:, :], 0.0).then_inc(pool_link, 1)
            pool.wait_ge(pool_link, seen(pool_link))
            pool.affine_select(out=ident[:, :], in_=ident[:, :], compare_op=ALU.not_equal, fill=1.0, base=0,
                               pattern=[[-1, P]], channel_multiplier=1).then_inc(const_made, 1)
            load_ln(a["ln_g"][0, 0], a["ln_b"][0, 0])
            load(cst[:, :], a["constants"])
            load(position[:, :], a["positions"][0].rearrange("(t p) -> p t", p=P))
            load(lam_in, a["diff_lambda"].partition_broadcast(P))
            load(sub_g, a["diff_subln_g"].partition_broadcast(P))
            load(sink, a["swa_sink"].partition_broadcast(P))
            load(router_w, a["router_w_2"].rearrange("(k p) e -> p k e", p=P))
            load(router_b, a["router_bias_2"].partition_broadcast(P))
            load(lam_re, a["s5_lambda_re_2"][0].rearrange("(i g) p -> (g p) i", g=2))
            load(lam_im, a["s5_lambda_im_2"][0].rearrange("(i g) p -> (g p) i", g=2))
            for g in range(2):
                load(log_dt[P5 * g:P5 * g + P5, :],
                     a["s5_log_dt_2"][0].rearrange("(i g) -> g i", g=2)[g].partition_broadcast(P5))
            load(pool_scale, a["pool_scale_2"][0].rearrange("(g d) -> d g", d=P))
            load(d_skip, a["s5_d_2"][0].rearrange("(c g) h -> (g h) c", c=4))
            load(pool_w[:, :, :], a["pool_w_2"][0].rearrange("g c d -> c g d"))
            pool.memset(minus_half[:, :], -0.5).then_inc(const_made, 1)
            pool.memset(half_pi[:, :], math.pi / 2).then_inc(const_made, 1)
            pool.memset(swa_mask[:, :, :], 0.0).then_inc(pool_link, 1)
            pool.memset(causal[:, :], 0.0).then_inc(pool_link, 1)
            pool.memset(before[:, :, :], 1.0).then_inc(pool_link, 1)
            pool.wait_ge(pool_link, seen(pool_link, 3))
            pool.affine_select(out=swa_mask[:, 0, :], in_=swa_mask[:, 0, :], compare_op=ALU.is_ge, fill=FAR,
                               base=WINDOW, pattern=[[-1, T]], channel_multiplier=1).then_inc(const_made, 1)
            pool.affine_select(out=swa_mask[:, 1, :], in_=swa_mask[:, 1, :], compare_op=ALU.is_ge, fill=FAR,
                               base=WINDOW - P, pattern=[[1, T]], channel_multiplier=-1).then_inc(const_made, 1)
            pool.affine_select(out=causal[:, P:T], in_=causal[:, P:T], compare_op=ALU.is_gt, fill=FAR, base=0,
                               pattern=[[-1, P]], channel_multiplier=1).then_inc(const_made, 1)
            pool.affine_select(out=before[:, :, :], in_=before[:, :, :], compare_op=ALU.is_gt, fill=0.0, base=0,
                               pattern=[[1, N_EXPERTS], [-1, N_EXPERTS]], channel_multiplier=0).then_inc(const_made, 1)

            def ln_rstd(eps):
                pool.wait_ge(const_made, 7)
                for t in range(TT):
                    pool.wait_ge(var_ready, seen(var_ready))
                    link(pool.tensor_scalar(rstd[:, t], moments[:, t, 1:2], eps, None, ALU.add))
                    pool.tensor_tensor(rstd[:, t], rstd[:, t], minus_half[:, 0:1], ALU.pow).then_inc(rstd_ready, 1)

            def next_ln(g, b):
                pool.wait_ge(x_ready, seen(x_ready, TT))
                load_ln(g, b)

            for l in range(DEPTH):
                ln_rstd(4 * LN_EPS)
                next_ln(a["ln_g"][l, 1], a["ln_b"][l, 1])
                pool.wait_ge(squares, seen(squares, TT))
                link(pool.tensor_scalar(srs, ssq, 1.0 / P, RMS_EPS, ALU.mult, ALU.add))
                pool.tensor_tensor(srs, srs, minus_half[:, 0:1].broadcast_to([P, TT, DIFF_HEADS]), ALU.pow)\
                    .then_inc(sub_rstd, 1)
                ln_rstd(LN_EPS)
                next_ln(a["ln_g"][l, 2], a["ln_b"][l, 2])
                if l == DEPTH - 1:
                    for i, n in enumerate(("re", "im")):
                        load(b_nat[:, i], a[f"s5_b_{n}_2"][0].rearrange("(i g) p h -> (g p) i h", g=2), s5_loaded)
                        load(c_nat[:, i], a[f"s5_c_{n}_2"][0].rearrange("(c g) h p -> (g h) c p", c=4), s5_loaded)
                ln_rstd(4 * LN_EPS)
                if l < DEPTH - 1:
                    next_ln(a["ln_g"][l + 1, 0], a["ln_b"][l + 1, 0])
                else:
                    next_ln(a["ln_mix_g_2"][0], a["ln_mix_b_2"][0])

            def load_p(l):
                load(h[:, :, :], a["p_2"][l, 0].rearrange("(t p) c -> p t c", p=P), p_loaded)

            load_p(0)
            for i in range(S5_TILES):
                q, b = i % 4, i % 2
                pool.wait_ge(scan_ready, seen(scan_ready))
                if i > 0:
                    pool.wait_ge(st_ready, 2 * i)
                for j in range(2):
                    pool.tensor_tensor(n5[:, j], s5[:, b], trig[:, j, q:q + 1, :].broadcast_to([P, 2, T]), ALU.mult)\
                        .then_inc(pool_link, 1)
                pool.wait_ge(pool_link, seen(pool_link, 2))
                if i >= 2:
                    pool.wait_ge(y_part, seen(y_part))
                pool.tensor_tensor(st5[:, b, 0], n5[:, 0, 0], n5[:, 1, 1], ALU.subtract).then_inc(st_ready, 1)
                pool.tensor_tensor(st5[:, b, 1], n5[:, 0, 1], n5[:, 1, 0], ALU.add).then_inc(st_ready, 1)
            for pad in pool_pad:
                pool.memset(pad[:, :, 0:16], 0.0).then_inc(pool_link, 1)
            pool.tensor_copy(pool_pad[0][:, :, 16:], ab_t[:, 4:8, :]).then_inc(pool_link, 1)
            pool.wait_ge(pool_link, seen(pool_link, 3))
            for g, w in enumerate(POOL_WINDOWS):
                src, dst = pool_pad[g % 2], pool_pad[(g + 1) % 2]
                link(pool.tensor_tensor(dst[:, g:4, 16:], src[:, g:4, 16:], src[:, g:4, 16 - w // 2:16 + T - w // 2], ALU.add))
            for g, w in enumerate(POOL_WINDOWS):
                s = pool_pad[(g + 1) % 2][:, g, 16:]
                link(pool.tensor_tensor(s[:, 0:16], s[:, 0:16], count_ratio[:, g], ALU.mult))
                link(pool.tensor_scalar(s, s, 1.0 / w, None, ALU.mult))
                pool.tensor_tensor(s, s, ab_t[:, 4 + g], ALU.subtract).then_inc(pooled, 1)

            ln_rstd(LN_EPS)
            next_ln(a["ln_ffn_g_2"][0], a["ln_ffn_b_2"][0])
            ln_rstd(LN_EPS)
            next_ln(a["ln_mix_g_2"][1], a["ln_mix_b_2"][1])
            load_p(1)
            ln_rstd(LN_EPS)
            next_ln(a["ln_ffn_g_2"][1], a["ln_ffn_b_2"][1])
            ln_rstd(LN_EPS)
            pool.wait_ge(gb_loaded, 2 * 16 * 10)

        def mm3(pe, dst, left, right, start, stop):
            pe.matmul(dst, left[0], right[0], start=start, stop=False)
            pe.matmul(dst, left[0], right[1], start=False, stop=False)
            return pe.matmul(dst, left[1], right[0], start=False, stop=stop)

        @block.tensor
        def _(pe):
            seen = Tally(pe)
            n = [0]

            def unit(k):
                s = n[0] % SPLIT
                n[0] += 1
                pe.wait_ge(lo_ready, seen(lo_ready))
                return [w[s][:, :].rearrange("p (k c) -> p k c", k=k) for w in (hi, lo)]

            def xt_part(k, t):
                return xt_hi[:, k, t * P:(t + 1) * P], xt_lo[:, k, t * P:(t + 1) * P]

            def tile(banks, parts=2, half=None):
                for u in range(parts):
                    w = unit(KD // parts)
                    width = UNIT // (KD // parts)
                    for t in range(TT):
                        for k in range(KD // parts):
                            mm = mm3(pe, banks[t][:, 0:width], xt_part(u * (KD // parts) + k, t), (w[0][:, k], w[1][:, k]),
                                     u == 0 and k == 0, u == parts - 1 and k == KD // parts - 1)
                        if t == 0 and u == parts - 1 and half is not None:
                            mm.then_inc(half, 1)
                    mm.then_inc(unit_used, 1)

            def matrix():
                tile([y_bank[t][0] for t in range(TT)])
                tile([y_bank[t][1] for t in range(TT)], half=y_half)

            def turn_h(p=False):
                if p:
                    pe.wait_ge(p_loaded, seen(p_loaded, 16))
                else:
                    pe.wait_ge(h_ready, seen(h_ready, TT))
                for k in range(2):
                    for t in range(TT):
                        mm = pe.transpose(turn_bank[0][:, k * T + t * P:k * T + (t + 1) * P], h[:, t, k * P:(k + 1) * P],
                                          ident[:, :])
                mm.then_inc(h_turned, 1)

            def down(first, last):
                w = unit(2)
                pe.wait_ge(ht_lo_ready, seen(ht_lo_ready))
                for t in range(TT):
                    for c in range(2):
                        for k in range(2):
                            left = ht_hi[:, k, t * P:(t + 1) * P], ht_lo[:, k, t * P:(t + 1) * P]
                            right = [v[:, k, c * 512:(c + 1) * 512] for v in w]
                            mm = mm3(pe, y_bank[t][c][:, :], left, right, first and k == 0, last and k == 1)
                    if t == 0 and last:
                        mm.then_inc(y_half, 1)
                mm.then_inc(unit_used, 1)

            def gated(w):
                def step(j):
                    tile(h_bank, half=first_half)
                    if j > 0:
                        down(j == 1, False)
                    turn_h()
                for j in range(w.peeled + 1):
                    step(j)
                with seen.loop(w.rounds, [(lo_ready, 6), (h_ready, 2 * TT), (ht_lo_ready, 2)]):
                    step(w.peeled + 1)
                    step(w.peeled + 2)
                n[0] += 6 * (w.rounds - 1)
                down(False, True)

            def turn_to_xt(src, ready, also=None):
                for t in range(TT):
                    if ready is not None:
                        pe.wait_ge(ready, seen(ready))
                    if also is not None:
                        pe.wait_ge(also, seen(also))
                    for b in range(2):
                        if t > 0:
                            pe.wait_ge(xt_lo_ready, seen(xt_lo_ready))
                        for k in range(4):
                            mm = pe.transpose(turn_bank[b][:, k * P:(k + 1) * P],
                                              src[:, t, (4 * b + k) * P:(4 * b + k + 1) * P], ident[:, :])
                        mm.then_inc(x_turned, 1)
                pe.wait_ge(xt_lo_ready, seen(xt_lo_ready, 2))

            def turn_rows(get, pairs, b0=0):
                for r in range(pairs):
                    b = (b0 + r) % 2
                    if r >= 2:
                        pe.wait_ge(col_ready, seen(col_ready))
                    for m in range(2):
                        for t in range(TT):
                            mm = pe.transpose(turn_bank[b][:, m * T + t * P:m * T + (t + 1) * P], get(2 * r + m, t),
                                              ident[:, :])
                    mm.then_inc(row_turned, 1)
                pe.wait_ge(col_ready, seen(col_ready, min(2, pairs)))

            def items(count, lag, scores, turn, pv):
                for i in range(count + lag + 1):
                    if i < count:
                        scores(i)
                    if lag <= i < count + lag:
                        turn(i - lag)
                    if i >= lag + 1:
                        pv(i - lag - 1)

            def hybrid(l):
                for j in range(5):
                    if j >= 2:
                        pe.wait_ge(tile_taken, seen(tile_taken, TT))
                    tile([y_bank[t][j % 2] for t in range(TT)], parts=1 if j == 3 else 2)
                pe.wait_ge(tile_taken, seen(tile_taken, 2 * TT))
                pe.wait_ge(row_ready, seen(row_ready, TT))
                turn_rows(lambda m, t: qk[:, t, m * P:(m + 1) * P], 7)

                def scores(i):
                    t = i % 2
                    k_tile = i // 2 if i < 8 else 4 + (i - 8) // 4
                    for c in range(2):
                        mm = pe.matmul(h_bank[i % 2][:, c * T:(c + 1) * T], qz1[:, i // 2, c, t * P:(t + 1) * P],
                                       kt1[:, k_tile, :], start=True, stop=True)
                    mm.then_inc(scores_ready, 1)

                def turn(i):
                    pe.wait_ge(prob_ready, seen(prob_ready))
                    for c in range(1 if i < 8 else 2):
                        for kt_ in range(2):
                            mm = pe.transpose(turn_bank[i % 2][:, c * T + kt_ * P:c * T + (kt_ + 1) * P],
                                              p1[:, i % 2, c, kt_ * P:(kt_ + 1) * P], ident[:, :])
                    mm.then_inc(prob_turned, 1)

                def pv(i):
                    pe.wait_ge(pt_ready, seen(pt_ready))
                    t = i % 2
                    for c in range(1 if i < 8 else 2):
                        if i < 8:
                            dst = y_bank[t][0][:, (i // 2) * P:(i // 2 + 1) * P]
                            cols = slice((i // 2) * P, (i // 2 + 1) * P)
                        else:
                            head = 2 * ((i - 8) // 2) + c
                            dst = y_bank[t][1][:, head * HD:(head + 1) * HD]
                            kv = head // (SWA_Q // 2)
                            cols = slice(512 + kv * HD, 512 + (kv + 1) * HD)
                        for kt_ in range(2):
                            mm = pe.matmul(dst, pt1[:, i % 2, c * T + kt_ * P:c * T + (kt_ + 1) * P], v1[:, kt_, cols],
                                           start=kt_ == 0, stop=kt_ == 1)
                    mm.then_inc(pv_done, 1)

                items(16, 1, scores, turn, pv)
                turn_to_xt(mix, mix_ready, swa_out)
                matrix()

            def stick_breaking():
                for j in range(6):
                    tile([y_bank[t][j % 2] for t in range(TT)])
                    if 1 <= j <= 4:
                        pe.wait_ge(row_ready, seen(row_ready, TT))
                        turn_rows(lambda m, t: qk_row[:, (j - 1) % 2, t, m * P:(m + 1) * P], 2)
                pe.wait_ge(tile_taken, seen(tile_taken, 2 * TT))
                banks = [y_bank[t][c] for t in range(TT) for c in range(2)]

                def scores(i):
                    t = i % 2
                    if i >= 2:
                        pe.wait_ge(zm_ready, seen(zm_ready))
                    for c in range(2):
                        mm = pe.matmul(h_bank[i % 2][:, c * T:c * T + (t + 1) * P], qz2[:, i // 2, c, t * P:(t + 1) * P],
                                       kt2[:, i // 2, 0:(t + 1) * P], start=True, stop=True)
                    mm.then_inc(scores_ready, 1)

                def turn(i):
                    pe.wait_ge(w_ready, seen(w_ready))
                    for c in range(2):
                        for k in range(i % 2 + 1):
                            mm = pe.transpose(turn_bank[i % 2][:, c * T + k * P:c * T + (k + 1) * P],
                                              w2[:, i % 2, c, k * P:(k + 1) * P], ident[:, :])
                    mm.then_inc(prob_turned, 1)

                def pv(i):
                    pe.wait_ge(pt_ready, seen(pt_ready))
                    pair, t = i // 2, i % 2
                    for c in range(2):
                        head = 2 * pair + c
                        at = (pair % 2) * T + t * P
                        for k in range(t + 1):
                            mm = pe.matmul(banks[pair // 2][HD * c:HD * c + HD, at:at + P],
                                           v2[:, k, head * HD:(head + 1) * HD],
                                           wt2[:, i % 2, c * T + k * P:c * T + (k + 1) * P], start=k == 0, stop=k == t)
                    mm.then_inc(pv_done, 1)

                items(16, 2, scores, turn, pv)
                pe.wait_ge(zm_ready, seen(zm_ready, 2))
                pe.wait_ge(xt_lo_ready, seen(xt_lo_ready, 4))
                matrix()

            def s5_and_pool():
                for j in range(2):
                    tile([y_bank[t][j] for t in range(TT)])
                pe.wait_ge(wide_ready, 4)
                for r in range(4):
                    src = (bb_wide, c_wide)[r // 2]
                    if r >= 2:
                        pe.wait_ge(wide_copied, seen(wide_copied))
                    for c in range(4):
                        if r < 2:
                            block = bb_wide[:, r % 2, 4 * c:4 * c + 4, :].rearrange("p i h -> p (i h)")
                        else:
                            block = c_wide[:, r % 2, c, :]
                        mm = pe.transpose(turn_bank[r % 2][:, c * P:(c + 1) * P], block, ident[:, :])
                    mm.then_inc(wide_turned, 1)
                pe.wait_ge(wide_copied, seen(wide_copied, 2))
                pe.wait_ge(row_ready, seen(row_ready, 2 * TT))
                turn_rows(lambda m, t: ab_row[:, t, m * P:(m + 1) * P], 4)

                def inputs(i):
                    c, q = i // 4, i % 4
                    if i >= 2:
                        pe.wait_ge(scan_ready, seen(scan_ready))
                    for ri in range(2):
                        mm = pe.matmul(h_bank[i % 2][:, ri * T:(ri + 1) * T], bb_t[32 * q:32 * q + 32, ri, c, :],
                                       ab_t[32 * q:32 * q + 32, c, :], start=True, stop=True)
                    mm.then_inc(bu_ready, 1)

                def outputs(i):
                    c, q = i // 4, i % 4
                    pe.wait_ge(st_ready, seen(st_ready, 2))
                    for ri in range(2):
                        mm = pe.matmul(y_bank[0][c // 2][32 * q:32 * q + 32, (c % 2) * T:(c % 2 + 1) * T],
                                       c_t[:, ri, c, 32 * q:32 * q + 32], st5[:, i % 2, ri], start=ri == 0, stop=ri == 1)
                    mm.then_inc(y_part, 1)

                for i in range(S5_TILES + 1):
                    if i < S5_TILES:
                        inputs(i)
                    if i > 0:
                        outputs(i - 1)
                for g in range(4):
                    pe.wait_ge(pooled, seen(pooled))
                    mm = pe.matmul(turn_bank[g // 2][:, (g % 2) * T:(g % 2 + 1) * T], pool_w[:, g, :],
                                   pool_pad[(g + 1) % 2][:, g, 16:], start=True, stop=True)
                mm.then_inc(pool_mixed, 1)
                w = unit(4)
                pe.wait_ge(xt_lo_ready, seen(xt_lo_ready))
                for m in range(4):
                    for k in range(4):
                        mm = mm3(pe, h_bank[m // 2][:, (m % 2) * T:(m % 2 + 1) * T],
                                 [v[:, k, m * P:(m + 1) * P] for v in w], (xt_hi[:, k, :], xt_lo[:, k, :]), k == 0, k == 3)
                mm.then_inc(unit_used, 1)
                pe.wait_ge(xt_lo_ready, seen(xt_lo_ready, 2))
                matrix()

            def before_experts():
                pe.wait_ge(rw_lo_ready, 1)
                for t in range(TT):
                    for k in range(KD):
                        mm = mm3(pe, h_bank[t][:, 0:N_EXPERTS], xt_part(k, t), (rw_hi[:, k, :], rw_lo[:, k, :]),
                                 k == 0, k == KD - 1)
                    mm.then_inc(routed, 1)
                for j in range(2):
                    tile([y_bank[t][j] for t in range(TT)])
                turn_h(p=True)
                pe.wait_ge(ple_sig, seen(ple_sig, 2 * TT))
                down(True, True)
                pe.wait_ge(gates_ready, seen(gates_ready))
                pe.wait_ge(tile_taken, seen(tile_taken, TT))

            pe.wait_ge(const_made, 1)
            pe.wait_ge(x_loaded, 16)
            turn_to_xt(x, None)
            for l in range(DEPTH):
                gated(ff[l][0])
                turn_to_xt(x, x_ready)
                hybrid(l)
                turn_to_xt(x, x_ready)
                gated(ff[l][1])
                turn_to_xt(x, x_ready)
            for l in range(DEPTH):
                (s5_and_pool, stick_breaking)[l]()
                turn_to_xt(x, x_ready)
                before_experts()
                gated(moe[l])
                if l < DEPTH - 1:
                    turn_to_xt(x, x_ready)

        @block.scalar
        def _(act):
            seen = Tally(act)
            n = [0]

            def link(ins):
                ins.then_inc(act_link, 1)
                act.wait_ge(act_link, seen(act_link))

            def split(times=1):
                for _ in range(times):
                    s, r = n[0] % SPLIT, n[0] % RAW
                    act.wait_ge(unit_loaded[r], seen(unit_loaded[r], 32))
                    if n[0] >= SPLIT:
                        act.wait_ge(unit_used, seen(unit_used))
                    act.activation(hi[s][:, :], raw[r][:, :], ACT.Copy).then_inc(hi_ready, 1)
                    n[0] += 1

            def wait_units():
                act.wait_ge(unit_used, n[0] - AHEAD)

            def gated(w):
                def silu(t):
                    act.activation(gate_act[:, t], h_bank[t][:, 0:HALF], ACT.Silu).then_inc(gate_ready, 1)

                def step(j):
                    split(1 if j == 0 else 2)
                    act.wait_ge(first_half, seen(first_half))
                    silu(0)
                    act.wait_ge(unit_used, seen.ahead(unit_used, 2 if j == 0 else 1))
                    silu(1)
                    split()
                    act.wait_ge(h_turned, seen(h_turned))
                    act.activation(ht_hi[:, :, :].rearrange("p k t -> p (k t)"), turn_bank[0][:, :], ACT.Copy)\
                        .then_inc(ht_hi_ready, 1)
                for j in range(w.peeled + 1):
                    step(j)
                with seen.loop(w.rounds, [(s, 32) for s in unit_loaded] + [(unit_used, 6), (first_half, 2), (h_turned, 2)]):
                    step(1)
                    step(1)
                n[0] += 6 * (w.rounds - 1)
                if w is not moe[-1]:
                    split()

            def turned_to_xt():
                for t in range(TT):
                    for b in range(2):
                        act.wait_ge(x_turned, seen(x_turned))
                        act.activation(xt_hi[:, 4 * b:4 * b + 4, t * P:(t + 1) * P],
                                       turn_bank[b][:, :].rearrange("p (k t) -> p k t", k=4), ACT.Copy)\
                            .then_inc(xt_hi_ready, 1)

            def turned_rows(dsts):
                for r, dst in enumerate(dsts):
                    act.wait_ge(row_turned, seen(row_turned))
                    src = turn_bank[r % 2][:, :].rearrange("p (m t) -> p m t", m=2)
                    if len(dst.shape) == 3:
                        ins = act.activation(dst, src, ACT.Copy)
                    else:
                        for c in range(2):
                            rows = slice(HD * c, HD * c + HD)
                            ins = act.activation(dst[rows, :, c], src[rows], ACT.Copy)
                    ins.then_inc(col_ready, 1)

            def make_rope():
                act.wait_ge(angles, seen(angles))
                act.activation(rope[:, 1], rope[:, 0], ACT.Sin).then_inc(act_link, 1)
                link(act.activation(rot[:, 0, 0:TT * HD].rearrange("p (t d) -> p t d", t=TT), rope[:, 0], ACT.Abs))
                act.wait_ge(act_link, seen(act_link))
                act.activation(rope[:, 0], rot[:, 0, 0:TT * HD].rearrange("p (t d) -> p t d", t=TT), ACT.Sin,
                               bias=half_pi[:, 0:1], scale=-1.0).then_inc(sines, 1)

            def hybrid(l):
                split(9)
                turned_rows([qz1[:, 0:2], qz1[:, 2:4], kt1[:, 0:2], kt1[:, 2:4], qz1[:, 4:6], qz1[:, 6:8], kt1[:, 4:6]])

                def exps(i):
                    b = i % 2
                    act.wait_ge(neg_ready, seen(neg_ready))
                    for c in range(2):
                        src = h_bank[b][:, c * T:(c + 1) * T] if i < 8 else e1[:, b, c]
                        ins = act.activation(e1[:, b, c], src, ACT.Exp, bias=neg[:, b, c:c + 1], scale=SCALE,
                                             accum_out=sums[:, b, c:c + 1])
                    if i >= 8:
                        ins = act.activation(sink_e[:, b], sink_e[:, b], ACT.Exp)
                    ins.then_inc(exp_ready, 1)

                def copies(i):
                    act.wait_ge(prob_turned, seen(prob_turned))
                    width = T if i < 8 else 2 * T
                    act.activation(pt1[:, i % 2, 0:width], turn_bank[i % 2][:, 0:width], ACT.Copy).then_inc(pt_ready, 1)

                for i in range(17):
                    if i < 16:
                        exps(i)
                    if i >= 1:
                        copies(i - 1)
                act.wait_ge(pv_done, seen(pv_done, 16))
                for t in range(TT):
                    for d in range(DIFF_HEADS):
                        ins = act.activation(e1[:, t, d // 2, (d % 2) * P:(d % 2 + 1) * P], y_bank[t][0][:, d * P:(d + 1) * P], ACT.Square,
                                             accum_out=ssq[:, t, d:d + 1])
                    ins.then_inc(squares, 1)
                for t in range(TT):
                    act.activation(mix[:, t, 512:D], y_bank[t][1][:, :], ACT.Copy).then_inc(swa_out, 1)
                turned_to_xt()
                split(4)

            def stick_breaking():
                for j in range(6):
                    split(2)
                    if 1 <= j <= 4:
                        dst = (qz2, kt2)[(j - 1) // 2]
                        k = 4 * ((j - 1) % 2)
                        turned_rows([dst[:, k + 2 * r:k + 2 * r + 2] for r in range(2)])

                def logs(i):
                    b, n_keys = i % 2, (i % 2 + 1) * P
                    act.wait_ge(zm_ready, seen(zm_ready))
                    v = sp_[:, b, :, 0:n_keys]
                    link(act.activation(v, zm[:, b, :, 0:n_keys], ACT.Abs))
                    link(act.activation(v, v, ACT.Exp, scale=-1.0))
                    act.activation(v, v, ACT.Ln, bias=1.0).then_inc(sp_ready, 1)

                def weights(i):
                    b, n_keys = i % 2, (i % 2 + 1) * P
                    act.wait_ge(arg_ready, seen(arg_ready))
                    act.activation(w2[:, b, :, 0:n_keys], zm[:, b, :, 0:n_keys], ACT.Exp).then_inc(w_ready, 1)

                def copies(i):
                    act.wait_ge(prob_turned, seen(prob_turned))
                    for c in range(2):
                        at = slice(c * T, c * T + (i % 2 + 1) * P)
                        ins = act.activation(wt2[:, i % 2, at], turn_bank[i % 2][:, at], ACT.Copy)
                    ins.then_inc(pt_ready, 1)

                for i in range(18):
                    if i < 16:
                        logs(i)
                    if 1 <= i < 17:
                        weights(i - 1)
                    if i >= 2:
                        copies(i - 2)
                act.wait_ge(pv_done, seen(pv_done, 16))
                for b in range(4):
                    act.activation(xt_hi[:, 2 * b:2 * b + 2, :],
                                   y_bank[b // 2][b % 2][:, :].rearrange("p (k t) -> p k t", k=2), ACT.Copy)\
                        .then_inc(xt_hi_ready, 1)
                split(4)

            def s5_and_pool():
                split(4)
                act.wait_ge(s5_loaded, 16 * 4)
                act.activation(dt5, log_dt, ACT.Exp).then_inc(s5_act, 1)
                act.wait_ge(s5_dve, seen(s5_dve))
                act.activation(mag5, tmpa, ACT.Exp).then_inc(s5_act, 1)
                act.wait_ge(s5_dve, seen(s5_dve))
                act.activation(sin5, r5, ACT.Sin).then_inc(s5_act, 1)
                link(act.activation(abs5, r5, ACT.Abs))
                act.activation(cos5, abs5, ACT.Sin, bias=half_pi[:, 0:1], scale=-1.0).then_inc(s5_act, 1)
                for r in range(4):
                    act.wait_ge(wide_turned, seen(wide_turned))
                    dst = (bb_t, c_t)[r // 2][:, r % 2]
                    act.activation(dst, turn_bank[r % 2][:, :].rearrange("p (c m) -> p c m", c=4), ACT.Copy,
                                   scale=-1.0 if r == 3 else 1.0).then_inc(wide_copied, 1)
                turned_rows([ab_t[:, 2 * r:2 * r + 2, :] for r in range(4)])
                for c in range(4):
                    act.wait_ge(turns_ready, seen(turns_ready))
                    if c > 0:
                        act.wait_ge(st_ready, 8 * c)
                    act.activation(trig[:, 1], th[:, 0], ACT.Sin, scale=6.283185).then_inc(act_link, 1)
                    link(act.activation(th[:, 1], th[:, 0], ACT.Abs))
                    act.wait_ge(act_link, seen(act_link))
                    act.activation(trig[:, 0], th[:, 1], ACT.Sin, bias=half_pi[:, 0:1], scale=-6.283185)\
                        .then_inc(trig_ready, 1)
                act.wait_ge(s5_dve, seen(s5_dve))
                act.activation(g5, y5, ACT.Square).then_inc(s5_act, 1)
                act.wait_ge(s5_dve, seen(s5_dve))
                act.activation(g5, g5, ACT.Sigmoid, scale=GELU_C).then_inc(s5_act, 1)
                act.wait_ge(s5_dve, seen(s5_dve))
                act.activation(xt_hi[:, 0:4, :], y5, ACT.Copy).then_inc(xt_hi_ready, 1)
                split()
                wait_units()
                for b in range(2):
                    act.activation(g5[:, 2 * b:2 * b + 2, :], h_bank[b][:, :].rearrange("p (m t) -> p m t", m=2),
                                   ACT.Sigmoid).then_inc(s5_act, 1)
                act.wait_ge(s5_dve, seen(s5_dve))
                act.activation(xt_hi[:, 0:4, :], y5, ACT.Copy).then_inc(xt_hi_ready, 1)
                act.wait_ge(pool_mixed, 1)
                for g in range(4):
                    ins = act.activation(xt_hi[:, 4 + g, :], turn_bank[g // 2][:, (g % 2) * T:(g % 2 + 1) * T], ACT.Copy,
                                         scale=pool_scale[:, g:g + 1])
                ins.then_inc(xt_hi_ready, 1)
                split(4)

            def before_experts(l):
                if l == 0:
                    act.activation(rw_hi[:, :, :], router_w, ACT.Copy).then_inc(rw_hi_ready, 1)
                for t in range(TT):
                    act.wait_ge(routed, seen(routed))
                    act.activation(r_s[:, t], h_bank[t][:, 0:N_EXPERTS], ACT.Sigmoid).then_inc(route_sig, 1)
                for j in range(2):
                    split(2)
                    wait_units()
                    for t in range(TT):
                        act.activation(ple_gate[:, t, j * 512:(j + 1) * 512], y_bank[t][j][:, :], ACT.Sigmoid)\
                            .then_inc(ple_sig, 1)
                act.wait_ge(h_turned, seen(h_turned))
                act.activation(ht_hi[:, :, :].rearrange("p k t -> p (k t)"), turn_bank[0][:, :], ACT.Copy)\
                    .then_inc(ht_hi_ready, 1)
                split()

            split(AHEAD)
            turned_to_xt()
            act.wait_ge(const_loaded, 16 * N_LOADS)
            act.wait_ge(const_made, 7)
            act.wait_ge(lam_sums, 1)
            act.activation(lam_e, lam_e, ACT.Exp).then_inc(lam_exps, 1)
            make_rope()
            for l in range(DEPTH):
                gated(ff[l][0])
                turned_to_xt()
                hybrid(l)
                turned_to_xt()
                gated(ff[l][1])
                turned_to_xt()
            for l in range(DEPTH):
                (s5_and_pool, stick_breaking)[l]()
                turned_to_xt()
                before_experts(l)
                gated(moe[l])
                if l < DEPTH - 1:
                    turned_to_xt()

        @block.vector
        def _(dve):
            seen = Tally(dve)
            n = [0]

            def link(ins):
                ins.then_inc(dve_link, 1)
                dve.wait_ge(dve_link, seen(dve_link))

            def split(times=1):
                for _ in range(times):
                    s, r = n[0] % SPLIT, n[0] % RAW
                    dve.wait_ge(hi_ready, seen(hi_ready))
                    dve.tensor_tensor(lo[s][:, :], raw[r][:, :], hi[s][:, :].bitcast(F32), ALU.subtract)\
                        .then_inc(lo_ready, 1)
                    n[0] += 1

            def wait_units():
                dve.wait_ge(unit_used, n[0] - AHEAD)

            def low_h():
                dve.wait_ge(ht_hi_ready, seen(ht_hi_ready))
                dve.tensor_tensor(ht_lo[:, :, :].rearrange("p k t -> p (k t)"), turn_bank[0][:, :],
                                  ht_hi[:, :, :].bitcast(F32).rearrange("p k t -> p (k t)"), ALU.subtract)\
                    .then_inc(ht_lo_ready, 1)

            def gated(w):
                def step(i, j):
                    split(1 if j == 0 else 2)
                    for t in range(TT):
                        dve.wait_ge(gate_ready, seen(gate_ready))
                        up = h_bank[t][:, HALF:2 * HALF]
                        if w.experts:
                            e = i + j // EXPERT_STEPS
                            g = gates[:, t, e:e + 1] if isinstance(e, int) else gates[:, t, bass.ds(e, 1)]
                            ins = dve.scalar_tensor_tensor(out=h[:, t], in0=up, scalar=g, in1=gate_act[:, t],
                                                           op0=ALU.mult, op1=ALU.mult)
                        else:
                            ins = dve.tensor_tensor(h[:, t], up, gate_act[:, t], ALU.mult)
                        ins.then_inc(h_ready, 1)
                    split()
                    low_h()
                for j in range(w.peeled + 1):
                    step(0, j)
                with seen.loop(w.rounds, [(hi_ready, 6), (gate_ready, 2 * TT), (ht_hi_ready, 2)]) as i:
                    step(i, w.peeled + 1)
                    step(i, w.peeled + 2)
                n[0] += 6 * (w.rounds - 1)
                if w is not moe[-1]:
                    split()

            def norm(k, coef, done, split_ahead=AHEAD):
                for t in range(TT):
                    if t == 0:
                        dve.wait_ge(y_half, seen(y_half))
                    else:
                        dve.wait_ge(unit_used, n[0] - split_ahead)
                    for c in range(2):
                        v = x[:, t, c * 512:(c + 1) * 512]
                        dve.scalar_tensor_tensor(out=v, in0=v, scalar=coef, in1=y_bank[t][c][:, :],
                                                 op0=ALU.mult, op1=ALU.add).then_inc(dve_link, 1)
                    dve.wait_ge(dve_link, seen(dve_link, 2))
                    for c in range(2):
                        dve.bn_stats(stats[:, t, c, :], x[:, t, c * 512:(c + 1) * 512]).then_inc(dve_link, 1)
                    dve.wait_ge(dve_link, seen(dve_link, 2))
                    dve.bn_aggr(moments[:, t, :], stats[:, t].rearrange("p c s -> p (c s)")).then_inc(var_ready, 1)
                dve.wait_ge(gb_loaded, 32 * (k + 1))
                for t in range(TT):
                    dve.wait_ge(rstd_ready, seen(rstd_ready))
                    v = x[:, t, :]
                    link(dve.tensor_scalar(v, v, moments[:, t, 0:1], rstd[:, t, 0:1], ALU.subtract, ALU.mult))
                    link(dve.tensor_tensor(v, v, ln_gb[:, 0, :], ALU.mult))
                    dve.tensor_tensor(v, v, ln_gb[:, 1, :], ALU.add).then_inc(done, 1)

            def low_xt():
                for t in range(TT):
                    for b in range(2):
                        dve.wait_ge(xt_hi_ready, seen(xt_hi_ready))
                        at = (slice(None), slice(4 * b, 4 * b + 4), slice(t * P, (t + 1) * P))
                        dve.tensor_tensor(xt_lo[at], turn_bank[b][:, :].rearrange("p (k t) -> p k t", k=4),
                                          xt_hi[at].bitcast(F32), ALU.subtract).then_inc(xt_lo_ready, 1)

            def reduce_angle(dst, src, whole):
                link(dve.tensor_scalar(whole, src, 1.0 / TWO_PI, ROUND, ALU.mult, ALU.add))
                link(dve.tensor_scalar(whole, whole, ROUND, None, ALU.subtract))
                for part, first in ((TP_HI, src), (TP_MID, dst), (TP_LO, dst)):
                    link(dve.scalar_tensor_tensor(out=dst, in0=whole, scalar=-part, in1=first, op0=ALU.mult, op1=ALU.add))
                return dve.tensor_scalar(dst, dst, PI_IN, -PI_IN, ALU.min, ALU.max)

            def make_tables():
                dve.wait_ge(const_loaded, 16 * N_LOADS)
                prod = rot[:, 0, 0:DEPTH * 2 * HD].rearrange("p (l i d) -> p l i d", l=DEPTH, i=2)
                for l in range(DEPTH):
                    v = lam_in[:, l].rearrange("p (i j) d -> p j i d", j=2)
                    link(dve.tensor_tensor(prod[:, l], v[:, 0], v[:, 1], ALU.mult))
                dve.tensor_reduce(lam_e, prod, AX_X, ALU.add).then_inc(lam_sums, 1)
                dve.wait_ge(lam_exps, 1)
                for l in range(DEPTH):
                    link(dve.tensor_tensor(lam[:, l:l + 1], lam_e[:, l, 0:1], lam_e[:, l, 1:2], ALU.subtract))
                    link(dve.tensor_scalar(lam[:, l:l + 1], lam[:, l:l + 1], lambda_init(l), None, ALU.add))
                    link(dve.tensor_scalar(sub_g[:, l], sub_g[:, l], 1.0 - lambda_init(l), None, ALU.mult))
                link(dve.tensor_scalar(neg_sink, sink, -1.0, None, ALU.mult))
                pos = small[:, 52:54]
                link(dve.tensor_copy(pos, position[:, :]))
                ang = rot[:, 1, 0:TT * 32].rearrange("p (t f) -> p t f", t=TT)
                whole = rot[:, 1, 64:64 + TT * 32].rearrange("p (t f) -> p t f", t=TT)
                red = rot[:, 1, 128:128 + TT * 32].rearrange("p (t f) -> p t f", t=TT)
                for t in range(TT):
                    link(dve.tensor_scalar(ang[:, t], freq, pos[:, t:t + 1], None, ALU.mult))
                link(reduce_angle(red, ang, whole))
                link(dve.tensor_copy(rope[:, 0, :, 0:32], red))
                dve.tensor_copy(rope[:, 0, :, 32:64], red).then_inc(angles, 1)
                dve.wait_ge(sines, 1)
                link(dve.tensor_scalar(rope[:, 1, :, 0:32], rope[:, 1, :, 0:32], -1.0, None, ALU.mult))

            def rotate(t, src, heads, dsts, done):
                cos = rope[:, 0, t:t + 1, :].broadcast_to([P, heads, HD])
                sin = rope[:, 1, t:t + 1, :].broadcast_to([P, heads, HD])
                by_cos = rot[:, 0, 0:heads * HD].rearrange("p (h d) -> p h d", h=heads)
                by_sin = rot[:, 1, 0:heads * HD].rearrange("p (h d) -> p h d", h=heads)
                dve.tensor_tensor(by_sin[:, :, 0:32], src[:, :, 32:64], sin[:, :, 0:32], ALU.mult).then_inc(dve_link, 1)
                dve.tensor_tensor(by_sin[:, :, 32:64], src[:, :, 0:32], sin[:, :, 32:64], ALU.mult).then_inc(dve_link, 1)
                dve.tensor_tensor(by_cos, src, cos, ALU.mult).then_inc(tile_taken, 1)
                dve.wait_ge(dve_link, seen(dve_link, 2))
                dve.wait_ge(tile_taken, seen(tile_taken))
                for dst in dsts:
                    ins = dve.tensor_tensor(dst, by_cos, by_sin, ALU.add)
                ins.then_inc(done, 1)
                if done is dve_link:
                    dve.wait_ge(dve_link, seen(dve_link))

            def hybrid(l):
                link(dve.memset(qz1, 0.0))
                for j in range(5):
                    split(1 if j == 3 else 2)
                    wait_units()
                    for t in range(TT):
                        bank_ = y_bank[t][j % 2]
                        if j < 3:
                            rotate(t, bank_[:, :].rearrange("p (h d) -> p h d", h=8), 8,
                                   [qk[:, t, j * 512:(j + 1) * 512].rearrange("p (h d) -> p h d", h=8)], dve_link)
                        elif j == 3:
                            link(dve.tensor_copy(v1[:, t, 512:640], bank_[:, P:2 * P]))
                            twice = qk[:, t, 1536:1792].rearrange("p (h two d) -> p two h d", h=2, two=2)
                            rotate(t, bank_[:, 0:P].rearrange("p (h d) -> p h d", h=2), 2, [twice[:, 0], twice[:, 1]],
                                   row_ready)
                        else:
                            dve.tensor_copy(v1[:, t, 0:512], bank_[:, :]).then_inc(tile_taken, 1)
                            dve.wait_ge(tile_taken, seen(tile_taken))

                def maxima(i):
                    b = i % 2
                    dve.wait_ge(scores_ready, seen(scores_ready))
                    s = h_bank[b][:, :].rearrange("p (c k) -> p c k", c=2)
                    if i >= 8:
                        pair, t = (i - 8) // 2, i % 2
                        mask = swa_mask[:, t:t + 1, :].broadcast_to([P, 2, T])
                        link(dve.tensor_tensor(e1[:, b], s, mask, ALU.add))
                        s = e1[:, b]
                    link(dve.tensor_reduce(nmax[:, b], s, AX_X, ALU.max, negate=True))
                    if i < 8:
                        dve.tensor_scalar(neg[:, b], nmax[:, b], SCALE, None, ALU.mult).then_inc(neg_ready, 1)
                    else:
                        two = slice(2 * pair, 2 * pair + 2)
                        link(dve.scalar_tensor_tensor(out=neg[:, b], in0=nmax[:, b], scalar=SCALE,
                                                      in1=neg_sink[:, l, two], op0=ALU.mult, op1=ALU.min))
                        dve.tensor_tensor(sink_e[:, b], sink[:, l, two], neg[:, b], ALU.add).then_inc(neg_ready, 1)

                def probs(i):
                    b = i % 2
                    dve.wait_ge(exp_ready, seen(exp_ready))
                    if i < 8:
                        link(dve.reciprocal(inv[:, b], sums[:, b]))
                        link(dve.tensor_scalar(p1[:, b, 1], e1[:, b, 1], inv[:, b, 1:2], lam[:, l:l + 1], ALU.mult, ALU.mult))
                        dve.scalar_tensor_tensor(out=p1[:, b, 0], in0=e1[:, b, 0], scalar=inv[:, b, 0:1], in1=p1[:, b, 1],
                                                 op0=ALU.mult, op1=ALU.subtract).then_inc(prob_ready, 1)
                    else:
                        link(dve.tensor_tensor(sums[:, b], sums[:, b], sink_e[:, b], ALU.add))
                        link(dve.reciprocal(inv[:, b], sums[:, b]))
                        for c in range(2):
                            ins = dve.tensor_scalar(p1[:, b, c], e1[:, b, c], inv[:, b, c:c + 1], None, ALU.mult)
                        ins.then_inc(prob_ready, 1)

                for i in range(17):
                    if i < 16:
                        maxima(i)
                    if i >= 1:
                        probs(i - 1)
                dve.wait_ge(sub_rstd, seen(sub_rstd))
                for t in range(TT):
                    for d in range(DIFF_HEADS):
                        ins = dve.scalar_tensor_tensor(out=mix[:, t, d * P:(d + 1) * P], in0=y_bank[t][0][:, d * P:(d + 1) * P],
                                                       scalar=srs[:, t, d:d + 1], in1=sub_g[:, l], op0=ALU.mult, op1=ALU.mult)
                    ins.then_inc(mix_ready, 1)
                low_xt()
                split(4)

            def stick_breaking():
                link(dve.memset(qz2, 0.0))
                for j in range(6):
                    split(2)
                    wait_units()
                    for t in range(TT):
                        if j < 4:
                            dve.tensor_copy(qk_row[:, j % 2, t], y_bank[t][j % 2][:, :]).then_inc(row_ready, 1)
                        else:
                            dve.tensor_copy(v2[:, t, (j - 4) * 512:(j - 3) * 512], y_bank[t][j % 2][:, :])\
                                .then_inc(tile_taken, 1)
                seen(tile_taken, 2 * TT)

                def masked(i):
                    b, n_keys = i % 2, (i % 2 + 1) * P
                    if i >= 2:
                        dve.wait_ge(w_ready, seen(w_ready))
                    dve.wait_ge(scores_ready, seen(scores_ready))
                    mask = causal[:, T - n_keys:T].rearrange("p (o k) -> p o k", o=1).broadcast_to([P, 2, n_keys])
                    s = h_bank[b][:, :].rearrange("p (c k) -> p c k", c=2)[:, :, 0:n_keys]
                    dve.scalar_tensor_tensor(out=zm[:, b, :, 0:n_keys], in0=s, scalar=SCALE, in1=mask,
                                             op0=ALU.mult, op1=ALU.add).then_inc(zm_ready, 1)

                def exponents(i):
                    b, n_keys = i % 2, (i % 2 + 1) * P
                    dve.wait_ge(sp_ready, seen(sp_ready))
                    if i >= 2:
                        dve.wait_ge(prob_turned, 16 * DEPTH + i - 1)
                    z, keep = zm[:, b, :, 0:n_keys], soft[:, b, :, 0:n_keys]
                    link(dve.scalar_tensor_tensor(out=keep, in0=z, scalar=0.0, in1=sp_[:, b, :, 0:n_keys],
                                                  op0=ALU.max, op1=ALU.add))
                    for c in range(2):
                        dve.tensor_tensor_scan(w2[:, b, c, 0:n_keys][:, ::-1], before[:, 1, 0:1].broadcast_to([P, n_keys]),
                                               soft[:, b, c, 0:n_keys][:, ::-1], 0.0, ALU.mult, ALU.add).then_inc(dve_link, 1)
                    dve.wait_ge(dve_link, seen(dve_link, 2))
                    dve.tensor_tensor(z, z, w2[:, b, :, 0:n_keys], ALU.subtract).then_inc(arg_ready, 1)

                for i in range(17):
                    if i < 16:
                        masked(i)
                    if i >= 1:
                        exponents(i - 1)
                for b in range(4):
                    dve.wait_ge(xt_hi_ready, seen(xt_hi_ready))
                    dve.tensor_tensor(xt_lo[:, 2 * b:2 * b + 2, :],
                                      y_bank[b // 2][b % 2][:, :].rearrange("p (k t) -> p k t", k=2),
                                      xt_hi[:, 2 * b:2 * b + 2, :].bitcast(F32), ALU.subtract).then_inc(xt_lo_ready, 1)
                split(4)

            def s5_and_pool():
                split(4)
                dve.wait_ge(s5_act, seen(s5_act))
                link(dve.tensor_tensor(ang5, lam_im, dt5, ALU.mult))
                dve.tensor_tensor(tmpa, lam_re, dt5, ALU.mult).then_inc(s5_dve, 1)
                reduce_angle(r5, ang5, k5).then_inc(s5_dve, 1)
                dve.wait_ge(s5_dve, 2)
                link(dve.tensor_scalar(phi5, r5, 1.0 / TWO_PI, None, ALU.mult))
                link(dve.tensor_tensor(den, lam_re, lam_re, ALU.mult))
                link(dve.tensor_tensor(tmpb, lam_im, lam_im, ALU.mult))
                link(dve.tensor_tensor(den, den, tmpb, ALU.add))
                link(dve.reciprocal(den, den))
                dve.wait_ge(s5_act, seen(s5_act, 3))
                link(dve.tensor_tensor(lbr, mag5, cos5, ALU.mult))
                link(dve.tensor_tensor(lbi, mag5, sin5, ALU.mult))
                link(dve.tensor_scalar(lbr, lbr, 1.0, None, ALU.subtract))
                for f, (u, v), op in ((fre, (lam_re, lam_im), ALU.add), (fim, (lam_im, lam_re), ALU.subtract)):
                    link(dve.tensor_tensor(tmpa, lbr, u, ALU.mult))
                    link(dve.tensor_tensor(tmpb, lbi, v, ALU.mult))
                    first, second = (tmpa, tmpb) if op is ALU.add else (tmpb, tmpa)
                    link(dve.tensor_tensor(f, first, second, op))
                    link(dve.tensor_tensor(f, f, den, ALU.mult))
                dve.wait_ge(s5_loaded, 16 * 4)
                link(dve.memset(bb_wide, 0.0))
                f_re = fre.rearrange("p (i o) -> p i o", o=1).broadcast_to([P, 16, 16])
                f_im = fim.rearrange("p (i o) -> p i o", o=1).broadcast_to([P, 16, 16])
                for ri in range(2):
                    link(dve.tensor_tensor(bb_tmp[:, 0], b_nat[:, ri], f_re, ALU.mult))
                    link(dve.tensor_tensor(bb_tmp[:, 1], b_nat[:, 1 - ri], f_im, ALU.mult))
                    for g in range(2):
                        r = slice(P5 * g, P5 * g + P5)
                        link(dve.tensor_tensor(bb_wide[r, ri, :, 16 * g:16 * g + 16], bb_tmp[r, 0], bb_tmp[r, 1],
                                               ALU.subtract if ri == 0 else ALU.add))
                    for g in range(2):
                        ins = dve.tensor_scalar(c_wide[:, ri, :, P5 * g:P5 * g + P5], c_nat[:, ri], parity[:, g:g + 1],
                                                None, ALU.mult)
                        ins.then_inc(wide_ready, 1)
                wait_units()
                for j in range(2):
                    for t in range(TT):
                        dve.tensor_copy(ab_row[:, t, j * 512:(j + 1) * 512], y_bank[t][j][:, :]).then_inc(row_ready, 1)
                dve.wait_ge(wide_turned, 4)
                for c in range(4):
                    if c > 0:
                        dve.wait_ge(trig_ready, c)
                    phi = phi5[:, 4 * c:4 * c + 4].rearrange("p (i o) -> p i o", o=1).broadcast_to([P, 4, T])
                    time = time_row.rearrange("p (o t) -> p o t", o=1).broadcast_to([P, 4, T])
                    link(dve.tensor_tensor(th[:, 0], phi, time, ALU.mult))
                    link(dve.tensor_scalar(th[:, 1], th[:, 0], ROUND, ROUND, ALU.add, ALU.subtract))
                    dve.tensor_tensor(th[:, 0], th[:, 0], th[:, 1], ALU.subtract).then_inc(turns_ready, 1)
                    dve.wait_ge(trig_ready, c + 1)
                    for q in range(4):
                        i = 4 * c + q
                        dve.wait_ge(bu_ready, seen(bu_ready))
                        if i > 0:
                            dve.wait_ge(scan_ready, i)
                        bu = h_bank[i % 2][:, :].rearrange("p (c t) -> p c t", c=2)
                        for j in range(2):
                            dve.tensor_tensor(m5[:, j], bu, trig[:, j, q:q + 1, :].broadcast_to([P, 2, T]), ALU.mult)\
                                .then_inc(dve_link, 1)
                        dve.wait_ge(dve_link, seen(dve_link, 2))
                        dve.tensor_tensor(m5[:, 0, 0], m5[:, 0, 0], m5[:, 1, 1], ALU.add).then_inc(dve_link, 1)
                        dve.tensor_tensor(m5[:, 0, 1], m5[:, 0, 1], m5[:, 1, 0], ALU.subtract).then_inc(dve_link, 1)
                        dve.wait_ge(dve_link, seen(dve_link, 2))
                        if i >= 2:
                            dve.wait_ge(st_ready, 2 * (i - 1))
                        for ri in range(2):
                            ins = dve.tensor_tensor_scan(s5[:, i % 2, ri], mag5[:, i:i + 1].broadcast_to([P, T]),
                                                         m5[:, 0, ri], 0.0, ALU.mult, ALU.add)
                        ins.then_inc(scan_ready, 1)
                dve.wait_ge(y_part, S5_TILES)
                for c in range(4):
                    ins = dve.scalar_tensor_tensor(out=y5[:, c], in0=ab_t[:, c], scalar=d_skip[:, c:c + 1],
                                                   in1=y_bank[0][c // 2][:, (c % 2) * T:(c % 2 + 1) * T],
                                                   op0=ALU.mult, op1=ALU.add)
                ins.then_inc(s5_dve, 1)
                dve.wait_ge(s5_act, seen(s5_act))
                link(dve.tensor_scalar(g5, g5, 0.044715, 1.0, ALU.mult, ALU.add))
                dve.tensor_tensor(g5, g5, y5, ALU.mult).then_inc(s5_dve, 1)
                dve.wait_ge(s5_act, seen(s5_act))
                dve.tensor_tensor(y5, y5, g5, ALU.mult).then_inc(s5_dve, 1)
                dve.wait_ge(xt_hi_ready, seen(xt_hi_ready))
                dve.tensor_tensor(xt_lo[:, 0:4, :], y5, xt_hi[:, 0:4, :].bitcast(F32), ALU.subtract).then_inc(xt_lo_ready, 1)
                split()
                dve.wait_ge(s5_act, seen(s5_act, 2))
                dve.tensor_tensor(y5, y5, g5, ALU.mult).then_inc(s5_dve, 1)
                dve.wait_ge(xt_hi_ready, seen(xt_hi_ready))
                dve.tensor_tensor(xt_lo[:, 0:4, :], y5, xt_hi[:, 0:4, :].bitcast(F32), ALU.subtract).then_inc(xt_lo_ready, 1)
                dve.wait_ge(xt_hi_ready, seen(xt_hi_ready))
                for g in range(4):
                    ins = dve.scalar_tensor_tensor(out=xt_lo[:, 4 + g, :], in0=turn_bank[g // 2][:, (g % 2) * T:(g % 2 + 1) * T],
                                                   scalar=pool_scale[:, g:g + 1], in1=xt_hi[:, 4 + g, :].bitcast(F32),
                                                   op0=ALU.mult, op1=ALU.subtract)
                ins.then_inc(xt_lo_ready, 1)
                split(4)

            def before_experts(l):
                if l == 0:
                    dve.wait_ge(rw_hi_ready, 1)
                    dve.tensor_tensor(rw_lo[:, :, :], router_w, rw_hi[:, :, :].bitcast(F32), ALU.subtract)\
                        .then_inc(rw_lo_ready, 1)
                split(1)
                dve.wait_ge(route_sig, seen(route_sig, TT))
                bias = router_b.rearrange("p (o e) -> p o e", o=1).broadcast_to([P, TT, N_EXPERTS])
                link(dve.tensor_tensor(r_sel, r_s, bias, ALU.add))
                four = r_sel.rearrange("p t (g e) -> p (t g) e", g=N_GROUPS)
                for i, (u, v, op) in enumerate(((0, 1, ALU.max), (0, 1, ALU.min), (2, 3, ALU.max), (2, 3, ALU.min))):
                    dve.tensor_tensor(r_two[:, i], four[:, :, u], four[:, :, v], op).then_inc(dve_link, 1)
                dve.wait_ge(dve_link, seen(dve_link, 4))
                dve.tensor_tensor(r_two[:, 4], r_two[:, 0], r_two[:, 2], ALU.max).then_inc(dve_link, 1)
                dve.tensor_tensor(r_two[:, 5], r_two[:, 0], r_two[:, 2], ALU.min).then_inc(dve_link, 1)
                dve.tensor_tensor(r_two[:, 6], r_two[:, 1], r_two[:, 3], ALU.max).then_inc(dve_link, 1)
                dve.wait_ge(dve_link, seen(dve_link, 3))
                link(dve.tensor_tensor(r_two[:, 5], r_two[:, 5], r_two[:, 6], ALU.max))
                link(dve.tensor_tensor(r_two[:, 7], r_two[:, 4], r_two[:, 5], ALU.add))
                score = r_two[:, 7].rearrange("p (t g) -> p t g", t=TT)

                def rank(values, t, n_values, dst):
                    mine = values.rearrange("p (e o) -> p e o", o=1).broadcast_to([P, n_values, n_values])
                    others = values.rearrange("p (o e) -> p o e", o=1).broadcast_to([P, n_values, n_values])
                    g, q = r_gt[:, 0:n_values, 0:n_values], r_eq[:, 0:n_values, 0:n_values]
                    dve.tensor_tensor(g, others, mine, ALU.is_gt).then_inc(dve_link, 1)
                    dve.tensor_tensor(q, others, mine, ALU.is_equal).then_inc(dve_link, 1)
                    dve.wait_ge(dve_link, seen(dve_link, 2))
                    link(dve.tensor_tensor(q, q, before[:, 0:n_values, 0:n_values], ALU.mult))
                    link(dve.tensor_tensor(g, g, q, ALU.add))
                    link(dve.tensor_reduce(dst, g, AX_X, ALU.add))

                for t in range(TT):
                    rank(score[:, t], t, N_GROUPS, r_grp[:, t])
                    link(dve.tensor_scalar(r_grp[:, t], r_grp[:, t], 0.5, FAR, ALU.is_gt, ALU.mult))
                    away = r_grp[:, t].rearrange("p (g o) -> p g o", o=1).broadcast_to([P, N_GROUPS, 4])
                    link(dve.tensor_tensor(r_sel[:, t].rearrange("p (g e) -> p g e", g=N_GROUPS),
                                           r_sel[:, t].rearrange("p (g e) -> p g e", g=N_GROUPS), away, ALU.add))
                    rank(r_sel[:, t], t, N_EXPERTS, r_rank[:, t])
                    link(dve.tensor_scalar(r_rank[:, t], r_rank[:, t], 1.5, None, ALU.is_lt))
                    link(dve.tensor_tensor(r_rank[:, t], r_rank[:, t], r_s[:, t], ALU.mult))
                    link(dve.tensor_reduce(r_sum[:, t:t + 1], r_rank[:, t], AX_X, ALU.add))
                    link(dve.reciprocal(r_sum[:, t:t + 1], r_sum[:, t:t + 1]))
                    ins = dve.tensor_scalar(gates[:, t], r_rank[:, t], r_sum[:, t:t + 1], None, ALU.mult)
                    if t == 0:
                        link(ins)
                ins.then_inc(gates_ready, 1)
                split(3)
                low_h()
                split()
                for t in range(TT):
                    if t == 0:
                        dve.wait_ge(y_half, seen(y_half))
                    else:
                        wait_units()
                    for c in range(2):
                        at = slice(c * 512, (c + 1) * 512)
                        ins = dve.tensor_tensor(ple_gate[:, t, at], y_bank[t][c][:, :], ple_gate[:, t, at], ALU.mult)
                        if c == 0:
                            link(ins)
                    ins.then_inc(tile_taken, 1)
                    dve.wait_ge(tile_taken, seen(tile_taken))
                    link(dve.scalar_tensor_tensor(out=x[:, t, :], in0=x[:, t, :], scalar=ALPHA, in1=ple_gate[:, t, :],
                                                  op0=ALU.mult, op1=ALU.add))

            split(AHEAD)
            low_xt()
            make_tables()
            for l in range(DEPTH):
                gated(ff[l][0])
                norm(3 * l, 2 * ALPHA, x_ready)
                low_xt()
                hybrid(l)
                norm(3 * l + 1, ALPHA, x_ready)
                low_xt()
                gated(ff[l][1])
                norm(3 * l + 2, 2 * ALPHA, x_ready)
                low_xt()
            for l in range(DEPTH):
                (s5_and_pool, stick_breaking)[l]()
                norm(6 + 2 * l, ALPHA, x_ready)
                low_xt()
                before_experts(l)
                gated(moe[l])
                if l < DEPTH - 1:
                    norm(7 + 2 * l, 1.0, x_ready)
                    low_xt()
                else:
                    norm(7 + 2 * l, 1.0, x_final, split_ahead=1)


def lambda_init(l):
    return 0.8 - 0.6 * math.exp(-0.3 * l)


def constants():
    c = np.zeros((P, C_END), np.float32)
    c[:, C_FREQ:C_FREQ + 32] = np.power(np.float32(10000.0), -np.arange(0, HD, 2, dtype=np.float32) / np.float32(HD))
    c[:, C_TIME:C_TIME + T] = np.arange(T)
    for g, w in enumerate(POOL_WINDOWS):
        c[:, C_COUNT + 16 * g:C_COUNT + 16 * g + 16] = w / np.minimum(np.arange(16) + 1, w).astype(np.float32)
    for g in range(2):
        c[:, C_PAR + g] = (np.arange(P) // H5) % 2 == g
    return c


_NAMES = ["x", "positions", "w_in", "w_out", "diff_lambda", "diff_subln_g", "swa_sink", "ffn1_w_in", "ffn1_w_out",
          "ffn2_w_in", "ffn2_w_out", "ln_g", "ln_b", "p_2", "ab_w_in_2", "s5_lambda_re_2", "s5_lambda_im_2",
          "s5_log_dt_2", "s5_b_re_2", "s5_b_im_2", "s5_c_re_2", "s5_c_im_2", "s5_d_2", "s5_w_glu_2", "pool_w_2",
          "pool_scale_2", "ab_w_out_2", "sb_w_qkv_2", "sb_w_out_2", "ln_mix_g_2", "ln_mix_b_2", "ln_ffn_g_2",
          "ln_ffn_b_2", "router_w_2", "router_bias_2", "moe_w1_2", "moe_w3_2", "moe_w2_2", "ple_w_proj_2",
          "ple_w_gate_2"]


def kernel(**inputs):
    import concourse.bacc as bacc
    from concourse.bass_utils import run_bass_kernel_spmd

    nc = bacc.Bacc("TRN2", target_bir_lowering=False, num_devices=1)
    inputs = {**inputs, "constants": constants()}
    arrays, aps = {}, {}
    for name in _NAMES + ["constants"]:
        arrays[name] = np.ascontiguousarray(inputs[name])
        aps[name] = nc.dram_tensor(name, arrays[name].shape, mybir.dt.from_np(arrays[name].dtype), kind="ExternalInput").ap()
    out = nc.dram_tensor("out", (1, T, D), F32, kind="ExternalOutput").ap()
    program(nc, aps, out)
    r = run_bass_kernel_spmd(nc, [arrays], core_ids=[0])
    return r.results[0]["out"]
```

```python
import math
from contextlib import ExitStack, contextmanager

import numpy as np
import concourse.bass as bass
from concourse import mybir

ALU = mybir.AluOpType
ACT = mybir.ActivationFunctionType
F32 = mybir.dt.float32
F32R = mybir.dt.float32r
I32 = mybir.dt.int32
AX_X = mybir.AxisListType.X

P = 128
T = 256
TT = T // P
D = 1024
KD = D // P
DEPTH = 2
D_FF = ((8 * D // 3 + 127) // 128) * 128
HALF = 256
FF_STEPS = D_FF // HALF
UNIT = 2048
RAW = 6
SPLIT = 3
AHEAD = 2
ALPHA = (2.0 * DEPTH) ** 0.25
LN_EPS = 1e-5
RMS_EPS = 1e-5
HD = 64
SCALE = HD ** -0.5
FAR = -1e30
DIFF_HEADS = 4
SWA_Q = 8
WINDOW = 128
N_EXPERTS = 16
D_EXPERT = 512
EXPERT_STEPS = D_EXPERT // HALF
MOE_STEPS = N_EXPERTS * EXPERT_STEPS
N_GROUPS = 4
SLOT_ROUNDS = (N_EXPERTS - 4) // 2
PLE = 256
G5, P5, H5 = 32, 64, 16
S5_TILES = G5 * P5 // P
POOL_WINDOWS = (2, 4, 8, 16)
SLOTS = P
ELSEWHERE = 4096.0
TWO_PI = 2.0 * math.pi
PI_IN = 3.1415925
ROUND = 1.5 * 2.0 ** 23
TP_HI = 6.28125
TP_MID = float(np.float32(TWO_PI - TP_HI) * 1.0)
TP_MID = math.floor((TWO_PI - TP_HI) * 2.0 ** 21) / 2.0 ** 21
TP_LO = TWO_PI - TP_HI - TP_MID
GELU_C = 2.0 * math.sqrt(2.0 / math.pi)

WORK_AT = 171968

C_FREQ, C_TIME, C_PAR, C_END = 0, 32, 288, 290


class Tally:

    def __init__(self, engine):
        self.engine, self.n, self.term = engine, {}, {}

    def __call__(self, sem, k=1):
        self.n[id(sem)] = self.n.get(id(sem), 0) + k
        return self.n[id(sem)] + self.term.get(id(sem), 0)

    def ahead(self, sem, k):
        return self.n.get(id(sem), 0) + k + self.term.get(id(sem), 0)

    @contextmanager
    def loop(self, rounds, per_round):
        start = {id(s): self.n.get(id(s), 0) for s, _ in per_round}
        before = dict(self.n)
        with self.engine.Fori(0, rounds) as i:
            self.term = {id(s): i * k for s, k in per_round}
            yield i
        for s, k in per_round:
            assert self.n.get(id(s), 0) - start[id(s)] == k, (s, k, self.n.get(id(s), 0) - start[id(s)])
            self.n[id(s)] = start[id(s)] + rounds * k
        for key, n in self.n.items():
            assert key in start or n == before.get(key), "a semaphore waited for, but not named"
        self.term = {}


class Gated:

    def __init__(self, gate, up, down, steps, peeled):
        self.gate_v, self.up_v, self.down_v, self.steps, self.peeled = gate, up, down, steps, peeled
        self.rounds = (steps - 1 - peeled) // 2
        assert peeled + 1 + 2 * self.rounds == steps


class FeedForward(Gated):
    def __init__(self, w_in, w_out):
        v = w_in.rearrange("(u k p) (g j c) -> g u j p k c", p=P, u=2, g=2, c=HALF)
        super().__init__(v[0], v[1], w_out.rearrange("(j k p) c -> j p k c", p=P, k=2), FF_STEPS, 2)
        self.experts = False

    def gate_up(self, i, j, u):
        at = 2 * i + j
        if isinstance(at, int):
            return self.gate_v[u, at], self.up_v[u, at]
        return (self.gate_v[u, bass.ds(at, 1)].rearrange("o p k c -> (o p) k c"),
                self.up_v[u, bass.ds(at, 1)].rearrange("o p k c -> (o p) k c"))

    def down(self, i, j):
        at = 2 * i + j
        if isinstance(at, int):
            return self.down_v[at]
        return self.down_v[bass.ds(at, 1)].rearrange("o p k c -> (o p) k c")


class Experts(Gated):
    def __init__(self, w1, w3, w2):
        ins = [w.rearrange("e (u k p) (j c) -> u j e p k c", p=P, u=2, c=HALF) for w in (w1, w3)]
        super().__init__(*ins, w2.rearrange("e (j k p) c -> j e p k c", p=P, k=2), MOE_STEPS, 1)
        self.experts = True

    def pick(self, v, i, j):
        e, half = i + j // EXPERT_STEPS, j % EXPERT_STEPS
        if isinstance(e, int):
            return v[half, e]
        return v[half, bass.ds(e, 1)].rearrange("o p k c -> (o p) k c")

    def gate_up(self, i, j, u):
        return self.pick(self.gate_v[u], i, j), self.pick(self.up_v[u], i, j)

    def down(self, i, j):
        return self.pick(self.down_v, i, j)


def program(nc, a, out):
    with ExitStack() as ctx:
        def sb(name, shape, dt=F32):
            return ctx.enter_context(nc.sbuf_tensor(name, shape, dt))

        def bank(name):
            return ctx.enter_context(nc.psum_tensor(name, [P, 512], F32))

        def sem(name):
            return ctx.enter_context(nc.semaphore(name))

        raw = [sb(f"raw{i}", [P, UNIT]) for i in range(RAW)]
        hi = [sb(f"w_hi{i}", [P, UNIT], F32R) for i in range(SPLIT)]
        lo = [sb(f"w_lo{i}", [P, UNIT], F32R) for i in range(SPLIT)]
        x = sb("x_rows", [P, TT, D])
        xt_hi = sb("xt_hi", [P, KD, T], F32R)
        xt_lo = sb("xt_lo", [P, KD, T], F32R)
        gate_act = sb("gate_act", [P, TT, HALF])
        h = sb("h", [P, TT, HALF])
        ht_hi = sb("ht_hi", [P, 2, T], F32R)
        ht_lo = sb("ht_lo", [P, 2, T], F32R)
        ln_gb = sb("ln_gb", [P, 2, D])
        ident = sb("ident", [P, P])
        stats = sb("stats", [P, TT, 2, 6])
        moments = sb("moments", [P, TT, 2])
        rstd = sb("rstd", [P, TT, 1])
        minus_half = sb("minus_half", [P, 4])
        cst = sb("cst", [P, C_END])
        rope = sb("rope", [P, 2, TT, HD])
        swa_mask = sb("swa_mask", [P, TT, T])
        causal = sb("causal", [P, T])
        gates = sb("gates", [P, TT, N_EXPERTS])
        small = sb("small", [P, 384])
        params = sb("params", [P, 984])
        pool_w = sb("pool_w", [P, 4, P])
        rw_hi = sb("rw_hi", [P, KD, N_EXPERTS], F32R)
        rw_lo = sb("rw_lo", [P, KD, N_EXPERTS], F32R)
        before = sb("before", [P, N_EXPERTS, N_EXPERTS])
        half_pi = sb("half_pi", [P, 1])
        position = sb("position", [P, TT], I32)
        work = nc.alloc_sbuf_tensor_at("work", [P, 14336], F32, offset=WORK_AT)
        slot_mem = nc.alloc_sbuf_tensor_at("slot_mem", [P, 11744], F32R, offset=WORK_AT)
        overflow = sb("overflow", [P, 1], I32)

        y_bank = [[bank(f"y{t}{c}") for c in range(2)] for t in range(TT)]
        h_bank = [bank(f"h{t}") for t in range(TT)]
        turn_bank = [bank(f"turn{t}") for t in range(TT)]

        unit_loaded = [sem(f"unit_loaded{i}") for i in range(RAW)]
        hi_ready = sem("hi_ready")
        lo_ready = sem("lo_ready")
        unit_used = sem("unit_used")
        const_loaded = sem("const_loaded")
        const_made = sem("const_made")
        gb_loaded = sem("gb_loaded")
        x_loaded = sem("x_loaded")
        first_half = sem("first_half")
        y_half = sem("y_half")
        gate_ready = sem("gate_ready")
        h_ready = sem("h_ready")
        h_turned = sem("h_turned")
        ht_hi_ready = sem("ht_hi_ready")
        ht_lo_ready = sem("ht_lo_ready")
        var_ready = sem("var_ready")
        rstd_ready = sem("rstd_ready")
        x_ready = sem("x_ready")
        x_turned = sem("x_turned")
        xt_hi_ready = sem("xt_hi_ready")
        xt_lo_ready = sem("xt_lo_ready")
        tile_taken = sem("tile_taken")
        dve_link = sem("dve_link")
        act_link = sem("act_link")
        pool_link = sem("pool_link")
        angles = sem("angles")
        sines = sem("sines")
        x_final = sem("x_final")
        stored = sem("stored")
        lam_sums = sem("lam_sums")
        lam_exps = sem("lam_exps")
        row_ready = sem("row_ready")
        row_turned = sem("row_turned")
        col_ready = sem("col_ready")
        scores_ready = sem("scores_ready")
        neg_ready = sem("neg_ready")
        exp_ready = sem("exp_ready")
        prob_ready = sem("prob_ready")
        prob_turned = sem("prob_turned")
        pt_ready = sem("pt_ready")
        pv_done = sem("pv_done")
        swa_out = sem("swa_out")
        squares = sem("squares")
        sub_rstd = sem("sub_rstd")
        mix_ready = sem("mix_ready")
        zm_ready = sem("zm_ready")
        sp_ready = sem("sp_ready")
        arg_ready = sem("arg_ready")
        w_ready = sem("w_ready")
        s5_loaded = sem("s5_loaded")
        s5_act = sem("s5_act")
        s5_dve = sem("s5_dve")
        wide_ready = sem("wide_ready")
        wide_turned = sem("wide_turned")
        wide_copied = sem("wide_copied")
        turns_ready = sem("turns_ready")
        trig_ready = sem("trig_ready")
        bu_ready = sem("bu_ready")
        scan_ready = sem("scan_ready")
        st_ready = sem("st_ready")
        y_part = sem("y_part")
        pooled = sem("pooled")
        pooled_ready = sem("pooled_ready")
        pool_mixed = sem("pool_mixed")
        rw_hi_ready = sem("rw_hi_ready")
        rw_lo_ready = sem("rw_lo_ready")
        routed = sem("routed")
        route_sig = sem("route_sig")
        gates_ready = sem("gates_ready")
        p_loaded = sem("p_loaded")
        ple_sig = sem("ple_sig")

        placed = sem("placed")
        overflow_known = sem("overflow_known")
        x_high = sem("x_high")
        all_half = [sem(f"all_half{l}") for l in range(DEPTH)]
        slots_ready = [sem(f"slots_ready{l}") for l in range(DEPTH)]
        gathered = [sem(f"gathered{l}") for l in range(DEPTH)]
        xe_ready = [sem(f"xe_ready{l}") for l in range(DEPTH)]
        first_gates = [sem(f"first_gates{l}") for l in range(DEPTH)]
        turn_taken = [sem(f"turn_taken{l}") for l in range(DEPTH)]
        last_out = [sem(f"last_out{l}") for l in range(DEPTH)]
        ye_hi_ready = [sem(f"ye_hi_ready{l}") for l in range(DEPTH)]
        ye_lo_ready = [sem(f"ye_lo_ready{l}") for l in range(DEPTH)]

        block = ctx.enter_context(nc.Block())

        ff = [[FeedForward(a["ffn1_w_in"][l], a["ffn1_w_out"][l]), FeedForward(a["ffn2_w_in"][l], a["ffn2_w_out"][l])]
              for l in range(DEPTH)]
        moe = [Experts(a["moe_w1_2"][l], a["moe_w3_2"][l], a["moe_w2_2"][l]) for l in range(DEPTH)]

        def by_rows(w, rows, c0, c1):
            return w[rows[0] * P:rows[1] * P, c0:c1].rearrange("(k p) c -> p k c", p=P)

        @block.sync
        def _(sp):
            seen = Tally(sp)
            n = [0]

            def load(*pieces):
                s = n[0] % RAW
                if n[0] >= RAW:
                    sp.wait_ge(lo_ready, seen(lo_ready))
                k = pieces[0].shape[1]
                dst = raw[s][:, :].rearrange("p (k c) -> p k c", k=k)
                c = UNIT // k // len(pieces)
                for q, src in enumerate(pieces):
                    sp.dma_start(dst[:, :, q * c:(q + 1) * c], src).then_inc(unit_loaded[s], 32 // len(pieces))
                n[0] += 1

            def load_gated(w):
                def step(i, j):
                    load(*w.gate_up(i, j, 0))
                    load(*w.gate_up(i, j, 1))
                    if not isinstance(i, int) or j > 0:
                        load(w.down(i, j - 1))
                for j in range(w.peeled + 1):
                    step(0, j)
                with seen.loop(w.rounds, [(lo_ready, 6)]) as i:
                    step(i, w.peeled + 1)
                    step(i, w.peeled + 2)
                n[0] += 6 * (w.rounds - 1)
                load(w.down(0, w.steps - 1))

            def load_matrix(w, cols, c0=0):
                for c in range(c0, c0 + cols, 512):
                    for u in range(2):
                        load(by_rows(w, (4 * u, 4 * u + 4), c, c + 512))

            for l in range(DEPTH):
                load_gated(ff[l][0])
                load_matrix(a["w_in"][l], 1024)
                load_matrix(a["w_in"][l], 512, 1536)
                load(by_rows(a["w_in"][l], (0, 8), 2048, 2304))
                load_matrix(a["w_in"][l], 512, 1024)
                load_matrix(a["w_out"][l], 1024)
                load_gated(ff[l][1])
            load_matrix(a["ab_w_in_2"][0], 1024)
            load(by_rows(a["s5_w_glu_2"][0], (0, 4), 0, 512))
            load_matrix(a["ab_w_out_2"][0], 1024)
            load_matrix(a["ple_w_gate_2"][0], 1024)
            load(by_rows(a["ple_w_proj_2"][0], (0, 2), 0, 1024))
            load_gated(moe[0])
            load_matrix(a["sb_w_qkv_2"][0], 3072)
            load_matrix(a["sb_w_out_2"][0], 1024)
            load_matrix(a["ple_w_gate_2"][1], 1024)
            load(by_rows(a["ple_w_proj_2"][1], (0, 2), 0, 1024))
            load_gated(moe[1])
            s = n[0] % RAW
            sp.wait_ge(lo_ready, seen(lo_ready))
            sp.dma_start(raw[s][:, 0:P], a["p_2"][0, 0, 0:P, 0:P]).then_inc(unit_loaded[s], 32)
            sp.wait_ge(x_final, 2 * TT)
            sp.dma_start(out[0].rearrange("(t p) d -> p t d", p=P), x[:, :, :]).then_inc(stored, 16)
            sp.wait_ge(stored, 16)

        def carve(tensor, at, *dims):
            n = int(np.prod(dims))
            v = tensor[:, at:at + n]
            if len(dims) == 1:
                return v
            names = "abcd"[:len(dims)]
            return v.rearrange(f"p ({' '.join(names)}) -> p {' '.join(names)}",
                               **{k: d for k, d in zip(names[1:], dims[1:])})

        freq, time_row = cst[:, C_FREQ:C_FREQ + 32], cst[:, C_TIME:C_TIME + T]
        parity = cst[:, C_PAR:C_PAR + 2]

        qk = carve(work, 0, TT, 1792)
        qz1 = carve(work, 3584, 8, 2, T)
        kt1 = carve(work, 7680, 6, T)
        v1 = carve(work, 9216, TT, 640)
        rot = carve(work, 10496, 2, 512)
        e1 = carve(work, 11520, 2, 2, T)
        p1 = carve(work, 12544, 2, 2, T)
        pt1 = carve(work, 2048, 2, 512)
        mix = carve(work, 0, TT, D)
        qz2 = carve(work, 0, 8, 2, T)
        kt2 = carve(work, 4096, 8, T)
        v2 = carve(work, 6144, TT, D)
        qk_row = carve(work, 8192, 2, TT, 512)
        zm = carve(work, 8192, 2, 2, T)
        sp_ = carve(work, 9216, 2, 2, T)
        soft = carve(work, 10240, 2, 2, T)
        w2 = carve(work, 11264, 2, 2, T)
        wt2 = carve(work, 12288, 2, 512)
        ab_row = carve(work, 2048, TT, D)
        ab_t = carve(work, 0, 8, T)
        bb_t = carve(work, 4096, 2, 4, P)
        c_t = carve(work, 5120, 2, 4, P)
        trig = [carve(work, at, 2, 4, T) for at in (6144, 2048)]
        pool_mat = carve(work, 12288, 4, TT, T)
        th = carve(work, 8192, 2, 4, T)
        m5 = carve(work, 10240, 2, 2, T)
        s5 = carve(work, 11264, 2, 2, T)
        n5 = [carve(work, 12288 + 1024 * b, 2, 2, T) for b in range(2)]
        minus_c = carve(gate_act[:, :, :].rearrange("p t c -> p (t c)"), 0, 4, P)
        b_nat = carve(work, 8192, 2, 16, 16)
        bb_wide = carve(work, 8704, 2, 16, 32)
        c_nat = carve(work, 9728, 2, 4, P5)
        c_wide = carve(work, 10240, 2, 4, P)
        bb_tmp = carve(work, 11264, 2, 16, 16)
        y5 = carve(work, 8320, 4, T)
        g5 = carve(work, 9344, 4, T)

        lam_in = carve(params, 0, DEPTH, 4, HD)
        sub_g = carve(params, 512, DEPTH, P)
        sink = carve(params, 768, DEPTH, SWA_Q)
        router_w = carve(params, 784, KD, N_EXPERTS)
        router_b = carve(params, 912, N_EXPERTS)
        lam_re, lam_im, log_dt = (carve(params, 928 + 16 * i, S5_TILES) for i in range(3))
        pool_scale = carve(params, 976, 4)
        d_skip = carve(params, 980, 4)
        N_LOADS = 14
        lam = carve(small, 0, DEPTH)
        lam_e = carve(small, 2, DEPTH, 2)
        neg = carve(small, 8, 2, 2)
        sums = carve(small, 12, 2, 2)
        sink_e = carve(small, 16, 2, 2)
        inv = carve(small, 20, 2, 2)
        nmax = carve(small, 24, 2, 2)
        ssq = carve(small, 28, TT, DIFF_HEADS)
        srs = carve(small, 36, TT, DIFF_HEADS)
        neg_sink = carve(small, 44, DEPTH, SWA_Q)
        s5v = [carve(small, 64 + 16 * i, 16) for i in range(20)]
        (dt5, ang5, mag5, k5, r5, sin5, cos5, phi5, abs5, lbr, lbi, den, fre, fim, tmpa, tmpb) = s5v[:16]

        ple_gate = carve(work, 0, TT, D)
        r_s = carve(work, 11776, TT, N_EXPERTS)
        r_sel = carve(work, 11808, TT, N_EXPERTS)
        r_two = carve(work, 11840, 8, TT * N_GROUPS)
        r_grp = carve(work, 11904, TT, N_GROUPS)
        r_rank = carve(work, 11912, TT, N_EXPERTS)
        r_sum = carve(work, 11944, TT)
        r_gt = carve(work, 12032, N_EXPERTS, N_EXPERTS)
        r_eq = carve(work, 12288, N_EXPERTS, N_EXPERTS)

        ye = carve(slot_mem, 0, 2, D)
        xr = carve(slot_mem, 2048, 2, TT, D)
        xe = [carve(slot_mem, 6144 + 2048 * b, 4, 2, 2, SLOTS) for b in range(2)]
        pick = carve(slot_mem, 10240, 2, TT, SLOTS)
        pick_t = carve(slot_mem, 10752, 2, T)
        tri = carve(slot_mem, 11264, 2, P)
        ident_r = carve(slot_mem, 11520, P)
        chosen = carve(slot_mem, 11648, TT, N_EXPERTS)
        gates_r = carve(slot_mem, 11680, 2, TT, N_EXPERTS)
        tri_ones = swa_mask[:, 0, :]
        slot_of = carve(small, 64, TT, N_EXPERTS)
        slot_gate = carve(small, 96, 2)
        most = carve(small, 98, 1)
        slot_row = time_row[:, 0:SLOTS]

        @block.gpsimd
        def _(pool):
            seen = Tally(pool)

            def link(ins):
                ins.then_inc(pool_link, 1)
                pool.wait_ge(pool_link, seen(pool_link))

            def load(dst, src, to=const_loaded):
                pool.dma_start(dst, src, allow_slow_non_contiguous=True).then_inc(to, 16)

            def load_ln(g, b):
                load(ln_gb[:, 0, :], g.partition_broadcast(P), gb_loaded)
                load(ln_gb[:, 1, :], b.partition_broadcast(P), gb_loaded)

            load(x[:, :, :], a["x"][0].rearrange("(t p) d -> p t d", p=P), x_loaded)
            pool.memset(ident[:, :], 0.0).then_inc(pool_link, 1)
            pool.wait_ge(pool_link, seen(pool_link))
            pool.affine_select(out=ident[:, :], in_=ident[:, :], compare_op=ALU.not_equal, fill=1.0, base=0,
                               pattern=[[-1, P]], channel_multiplier=1).then_inc(const_made, 1)
            load_ln(a["ln_g"][0, 0], a["ln_b"][0, 0])
            load(cst[:, :], a["constants"])
            load(position[:, :], a["positions"][0].rearrange("(t p) -> p t", p=P))
            load(lam_in, a["diff_lambda"].partition_broadcast(P))
            load(sub_g, a["diff_subln_g"].partition_broadcast(P))
            load(sink, a["swa_sink"].partition_broadcast(P))
            load(router_w, a["router_w_2"].rearrange("(k p) e -> p k e", p=P))
            load(router_b, a["router_bias_2"].partition_broadcast(P))
            load(lam_re, a["s5_lambda_re_2"][0].rearrange("(i g) p -> (g p) i", g=2))
            load(lam_im, a["s5_lambda_im_2"][0].rearrange("(i g) p -> (g p) i", g=2))
            for g in range(2):
                load(log_dt[P5 * g:P5 * g + P5, :],
                     a["s5_log_dt_2"][0].rearrange("(i g) -> g i", g=2)[g].partition_broadcast(P5))
            load(pool_scale, a["pool_scale_2"][0].rearrange("(g d) -> d g", d=P))
            load(d_skip, a["s5_d_2"][0].rearrange("(c g) h -> (g h) c", c=4))
            load(pool_w[:, :, :], a["pool_w_2"][0].rearrange("g c d -> c g d"))
            pool.memset(minus_half[:, :], -0.5).then_inc(const_made, 1)
            pool.memset(half_pi[:, :], math.pi / 2).then_inc(const_made, 1)
            pool.memset(swa_mask[:, :, :], 0.0).then_inc(pool_link, 1)
            pool.memset(causal[:, :], 0.0).then_inc(pool_link, 1)
            pool.memset(before[:, :, :], 1.0).then_inc(pool_link, 1)
            pool.wait_ge(pool_link, seen(pool_link, 3))
            pool.affine_select(out=swa_mask[:, 0, :], in_=swa_mask[:, 0, :], compare_op=ALU.is_ge, fill=FAR,
                               base=WINDOW, pattern=[[-1, T]], channel_multiplier=1).then_inc(const_made, 1)
            pool.affine_select(out=swa_mask[:, 1, :], in_=swa_mask[:, 1, :], compare_op=ALU.is_ge, fill=FAR,
                               base=WINDOW - P, pattern=[[1, T]], channel_multiplier=-1).then_inc(const_made, 1)
            pool.affine_select(out=causal[:, P:T], in_=causal[:, P:T], compare_op=ALU.is_gt, fill=FAR, base=0,
                               pattern=[[-1, P]], channel_multiplier=1).then_inc(const_made, 1)
            pool.affine_select(out=before[:, :, :], in_=before[:, :, :], compare_op=ALU.is_gt, fill=0.0, base=0,
                               pattern=[[1, N_EXPERTS], [-1, N_EXPERTS]], channel_multiplier=0).then_inc(const_made, 1)

            def ln_rstd(eps):
                pool.wait_ge(const_made, 7)
                for t in range(TT):
                    pool.wait_ge(var_ready, seen(var_ready))
                    link(pool.tensor_scalar(rstd[:, t], moments[:, t, 1:2], eps, None, ALU.add))
                    pool.tensor_tensor(rstd[:, t], rstd[:, t], minus_half[:, 0:1], ALU.pow).then_inc(rstd_ready, 1)

            def next_ln(g, b):
                pool.wait_ge(x_ready, seen(x_ready, 2 * TT))
                load_ln(g, b)

            for l in range(DEPTH):
                ln_rstd(4 * LN_EPS)
                next_ln(a["ln_g"][l, 1], a["ln_b"][l, 1])
                pool.wait_ge(squares, seen(squares, TT))
                link(pool.tensor_scalar(srs, ssq, 1.0 / P, RMS_EPS, ALU.mult, ALU.add))
                pool.tensor_tensor(srs, srs, minus_half[:, 0:1].broadcast_to([P, TT, DIFF_HEADS]), ALU.pow)\
                    .then_inc(sub_rstd, 1)
                ln_rstd(LN_EPS)
                next_ln(a["ln_g"][l, 2], a["ln_b"][l, 2])
                if l == DEPTH - 1:
                    link(pool.memset(tri_ones, 1.0))
                    link(pool.affine_select(out=tri_ones[:, 0:P], in_=tri_ones[:, 0:P], compare_op=ALU.is_ge, fill=0.0,
                                            base=0, pattern=[[1, P]], channel_multiplier=-1))
                    pool.affine_select(out=tri_ones[:, 0:P], in_=tri_ones[:, 0:P], compare_op=ALU.not_equal,
                                       fill=-ELSEWHERE, base=0, pattern=[[-1, P]], channel_multiplier=1)\
                        .then_inc(const_made, 1)
                    for i, n in enumerate(("re", "im")):
                        load(b_nat[:, i], a[f"s5_b_{n}_2"][0].rearrange("(i g) p h -> (g p) i h", g=2), s5_loaded)
                        load(c_nat[:, i], a[f"s5_c_{n}_2"][0].rearrange("(c g) h p -> (g h) c p", c=4), s5_loaded)
                    load(pool_mat, a["window_matrices"], s5_loaded)
                ln_rstd(4 * LN_EPS)
                if l < DEPTH - 1:
                    next_ln(a["ln_g"][l + 1, 0], a["ln_b"][l + 1, 0])
                else:
                    next_ln(a["ln_mix_g_2"][0], a["ln_mix_b_2"][0])

            def load_p(l):
                load(h[:, :, :], a["p_2"][l, 0].rearrange("(t p) c -> p t c", p=P), p_loaded)

            load_p(0)
            for i in range(S5_TILES):
                q, b = i % 4, i % 2
                pool.wait_ge(scan_ready, seen(scan_ready))
                if i >= 2:
                    pool.wait_ge(y_part, seen(y_part))
                for j in range(2):
                    pool.tensor_tensor(n5[b][:, j], s5[:, b], trig[i // 4 % 2][:, j, q:q + 1, :].broadcast_to([P, 2, T]),
                                       ALU.mult).then_inc(st_ready, 1)

            ln_rstd(LN_EPS)
            next_ln(a["ln_ffn_g_2"][0], a["ln_ffn_b_2"][0])
            ln_rstd(LN_EPS)
            next_ln(a["ln_mix_g_2"][1], a["ln_mix_b_2"][1])
            load_p(1)
            ln_rstd(LN_EPS)
            next_ln(a["ln_ffn_g_2"][1], a["ln_ffn_b_2"][1])
            ln_rstd(LN_EPS)
            pool.wait_ge(gb_loaded, 2 * 16 * 10)

        def mm3(pe, dst, left, right, start, stop):
            pe.matmul(dst, left[0], right[0], start=start, stop=False)
            pe.matmul(dst, left[0], right[1], start=False, stop=False)
            return pe.matmul(dst, left[1], right[0], start=False, stop=stop)

        @block.tensor
        def _(pe):
            seen = Tally(pe)
            n = [0]

            def unit(k):
                s = n[0] % SPLIT
                n[0] += 1
                pe.wait_ge(lo_ready, seen(lo_ready))
                return [w[s][:, :].rearrange("p (k c) -> p k c", k=k) for w in (hi, lo)]

            def xt_part(k, t):
                return xt_hi[:, k, t * P:(t + 1) * P], xt_lo[:, k, t * P:(t + 1) * P]

            def tile(banks, parts=2, half=None, late=None):
                if late is not None:
                    w = [unit(4), unit(4)]
                    for t in range(TT):
                        if t == 1:
                            pe.wait_ge(xt_lo_ready, seen(xt_lo_ready, 2))
                        for u in range(2):
                            if t == 0 and u == 1:
                                late()
                            for k in range(4):
                                mm = mm3(pe, banks[t][:, :], xt_part(4 * u + k, t), (w[u][0][:, k], w[u][1][:, k]),
                                         u == 0 and k == 0, u == 1 and k == 3)
                            if t == 1:
                                mm.then_inc(unit_used, 1)
                        if t == 0 and half is not None:
                            mm.then_inc(half, 1)
                    return
                for u in range(parts):
                    w = unit(KD // parts)
                    width = UNIT // (KD // parts)
                    for t in range(TT):
                        for k in range(KD // parts):
                            mm = mm3(pe, banks[t][:, 0:width], xt_part(u * (KD // parts) + k, t), (w[0][:, k], w[1][:, k]),
                                     u == 0 and k == 0, u == parts - 1 and k == KD // parts - 1)
                        if t == 0 and u == parts - 1 and half is not None:
                            mm.then_inc(half, 1)
                    mm.then_inc(unit_used, 1)

            def matrix(late=None):
                tile([y_bank[t][0] for t in range(TT)], late=late)
                tile([y_bank[t][1] for t in range(TT)], half=y_half)

            def turn_h(p=False):
                if p:
                    pe.wait_ge(p_loaded, seen(p_loaded, 16))
                else:
                    pe.wait_ge(h_ready, seen(h_ready, TT))
                for k in range(2):
                    for t in range(TT):
                        mm = pe.transpose(turn_bank[0][:, k * T + t * P:k * T + (t + 1) * P], h[:, t, k * P:(k + 1) * P],
                                          ident[:, :])
                mm.then_inc(h_turned, 1)

            def down(first, last):
                w = unit(2)
                pe.wait_ge(ht_lo_ready, seen(ht_lo_ready))
                for t in range(TT):
                    for c in range(2):
                        for k in range(2):
                            left = ht_hi[:, k, t * P:(t + 1) * P], ht_lo[:, k, t * P:(t + 1) * P]
                            right = [v[:, k, c * 512:(c + 1) * 512] for v in w]
                            mm = mm3(pe, y_bank[t][c][:, :], left, right, first and k == 0, last and k == 1)
                    if t == 0 and last:
                        mm.then_inc(y_half, 1)
                mm.then_inc(unit_used, 1)

            def gated(w, half=first_half, late=None):
                def step(j):
                    tile(h_bank, half=half, late=late if j == 0 else None)
                    if j > 0:
                        down(j == 1, False)
                    turn_h()
                for j in range(w.peeled + 1):
                    step(j)
                with seen.loop(w.rounds, [(lo_ready, 6), (h_ready, 2 * TT), (ht_lo_ready, 2)]):
                    step(w.peeled + 1)
                    step(w.peeled + 2)
                n[0] += 6 * (w.rounds - 1)
                down(False, True)

            def turn_to_xt(src, ready, also=None):
                def turn(t):
                    if also is not None:
                        pe.wait_ge(also, seen(also))
                    for b in range(2):
                        if ready is x_ready or ready is not None and b == 0:
                            pe.wait_ge(ready, seen(ready))
                        for k in range(4):
                            mm = pe.transpose(turn_bank[b][:, k * P:(k + 1) * P],
                                              src[:, t, (4 * b + k) * P:(4 * b + k + 1) * P], ident[:, :])
                        mm.then_inc(x_turned, 1)
                turn(0)
                pe.wait_ge(xt_lo_ready, seen(xt_lo_ready, 2))
                return lambda: turn(1)

            def turn_rows(get, pairs, b0=0):
                for r in range(pairs):
                    b = (b0 + r) % 2
                    if r >= 2:
                        pe.wait_ge(col_ready, seen(col_ready))
                    for m in range(2):
                        for t in range(TT):
                            mm = pe.transpose(turn_bank[b][:, m * T + t * P:m * T + (t + 1) * P], get(2 * r + m, t),
                                              ident[:, :])
                    mm.then_inc(row_turned, 1)
                pe.wait_ge(col_ready, seen(col_ready, min(2, pairs)))

            def items(count, lag, scores, turn, pv):
                for i in range(count + lag + 1):
                    if i < count:
                        scores(i)
                    if lag <= i < count + lag:
                        turn(i - lag)
                    if i >= lag + 1:
                        pv(i - lag - 1)

            def hybrid(l, late):
                for j in range(5):
                    if j >= 2:
                        pe.wait_ge(tile_taken, seen(tile_taken, TT))
                    tile([y_bank[t][j % 2] for t in range(TT)], parts=1 if j == 3 else 2, late=late if j == 0 else None)
                pe.wait_ge(tile_taken, seen(tile_taken, 2 * TT))
                pe.wait_ge(row_ready, seen(row_ready, TT))
                turn_rows(lambda m, t: qk[:, t, m * P:(m + 1) * P], 7)

                def scores(i):
                    t = i % 2
                    k_tile = i // 2 if i < 8 else 4 + (i - 8) // 4
                    if i >= 2:
                        pe.wait_ge(exp_ready, seen(exp_ready))
                    for c in range(2):
                        mm = pe.matmul(h_bank[i % 2][:, c * T:(c + 1) * T], qz1[:, i // 2, c, t * P:(t + 1) * P],
                                       kt1[:, k_tile, :], start=True, stop=True)
                    mm.then_inc(scores_ready, 1)

                def turn(i):
                    pe.wait_ge(prob_ready, seen(prob_ready))
                    for c in range(1 if i < 8 else 2):
                        for kt_ in range(2):
                            mm = pe.transpose(turn_bank[i % 2][:, c * T + kt_ * P:c * T + (kt_ + 1) * P],
                                              p1[:, i % 2, c, kt_ * P:(kt_ + 1) * P], ident[:, :])
                    mm.then_inc(prob_turned, 1)

                def pv(i):
                    pe.wait_ge(pt_ready, seen(pt_ready))
                    t = i % 2
                    for c in range(1 if i < 8 else 2):
                        if i < 8:
                            dst = y_bank[t][0][:, (i // 2) * P:(i // 2 + 1) * P]
                            cols = slice((i // 2) * P, (i // 2 + 1) * P)
                        else:
                            head = 2 * ((i - 8) // 2) + c
                            dst = y_bank[t][1][:, head * HD:(head + 1) * HD]
                            kv = head // (SWA_Q // 2)
                            cols = slice(512 + kv * HD, 512 + (kv + 1) * HD)
                        for kt_ in range(2):
                            mm = pe.matmul(dst, pt1[:, i % 2, c * T + kt_ * P:c * T + (kt_ + 1) * P], v1[:, kt_, cols],
                                           start=kt_ == 0, stop=kt_ == 1)
                    mm.then_inc(pv_done, 1)

                items(16, 2, scores, turn, pv)
                seen(exp_ready, 2)
                matrix(late=turn_to_xt(mix, mix_ready, swa_out))

            def stick_breaking(late):
                for j in range(6):
                    tile([y_bank[t][j % 2] for t in range(TT)], late=late if j == 0 else None)
                    if 1 <= j <= 4:
                        pe.wait_ge(row_ready, seen(row_ready, TT))
                        turn_rows(lambda m, t: qk_row[:, (j - 1) % 2, t, m * P:(m + 1) * P], 2)
                pe.wait_ge(tile_taken, seen(tile_taken, 2 * TT))
                banks = [y_bank[t][c] for t in range(TT) for c in range(2)]

                def scores(i):
                    t = i % 2
                    if i >= 2:
                        pe.wait_ge(zm_ready, seen(zm_ready))
                    for c in range(2):
                        mm = pe.matmul(h_bank[i % 2][:, c * T:c * T + (t + 1) * P], qz2[:, i // 2, c, t * P:(t + 1) * P],
                                       kt2[:, i // 2, 0:(t + 1) * P], start=True, stop=True)
                    mm.then_inc(scores_ready, 1)

                def turn(i):
                    pe.wait_ge(w_ready, seen(w_ready))
                    for c in range(2):
                        for k in range(i % 2 + 1):
                            mm = pe.transpose(turn_bank[i % 2][:, c * T + k * P:c * T + (k + 1) * P],
                                              w2[:, i % 2, c, k * P:(k + 1) * P], ident[:, :])
                    mm.then_inc(prob_turned, 1)

                def pv(i):
                    pe.wait_ge(pt_ready, seen(pt_ready))
                    pair, t = i // 2, i % 2
                    for c in range(2):
                        head = 2 * pair + c
                        at = (pair % 2) * T + t * P
                        for k in range(t + 1):
                            mm = pe.matmul(banks[pair // 2][HD * c:HD * c + HD, at:at + P],
                                           v2[:, k, head * HD:(head + 1) * HD],
                                           wt2[:, i % 2, c * T + k * P:c * T + (k + 1) * P], start=k == 0, stop=k == t)
                    mm.then_inc(pv_done, 1)

                items(16, 2, scores, turn, pv)
                pe.wait_ge(zm_ready, seen(zm_ready, 2))
                pe.wait_ge(xt_lo_ready, seen(xt_lo_ready, 4))
                matrix()

            def s5_and_pool(late):
                tile([y_bank[t][0] for t in range(TT)], late=late)
                pe.wait_ge(wide_ready, 4)
                for r in range(4):
                    src = (bb_wide, c_wide)[r // 2]
                    if r >= 2:
                        pe.wait_ge(wide_copied, seen(wide_copied))
                    for c in range(4):
                        if r < 2:
                            block = bb_wide[:, r % 2, 4 * c:4 * c + 4, :].rearrange("p i h -> p (i h)")
                        else:
                            block = c_wide[:, r % 2, c, :]
                        mm = pe.transpose(turn_bank[r % 2][:, c * P:(c + 1) * P], block, ident[:, :])
                    mm.then_inc(wide_turned, 1)
                pe.wait_ge(wide_copied, seen(wide_copied, 2))
                tile([y_bank[t][1] for t in range(TT)])
                pe.wait_ge(row_ready, seen(row_ready, TT))
                turn_rows(lambda m, t: ab_row[:, t, m * P:(m + 1) * P], 2)
                pe.wait_ge(row_ready, seen(row_ready, TT))
                pe.wait_ge(s5_loaded, 16 * 5)
                for g in range(4):
                    for k in range(TT):
                        mm = pe.matmul(y_bank[1][g // 2][:, (g % 2) * T:(g % 2 + 1) * T],
                                       ab_row[:, k, (4 + g) * P:(5 + g) * P], pool_mat[:, g, k, :], start=k == 0,
                                       stop=k == TT - 1)
                mm.then_inc(pooled, 1)

                def inputs(i):
                    c, q = i // 4, i % 4
                    if i >= 2:
                        pe.wait_ge(scan_ready, seen(scan_ready))
                    for ri in range(2):
                        mm = pe.matmul(h_bank[i % 2][:, ri * T:(ri + 1) * T], bb_t[32 * q:32 * q + 32, ri, c, :],
                                       ab_t[32 * q:32 * q + 32, c, :], start=True, stop=True)
                    mm.then_inc(bu_ready, 1)

                def outputs(i):
                    c, q = i // 4, i % 4
                    pe.wait_ge(st_ready, seen(st_ready, 2))
                    n = n5[i % 2]
                    terms = ((c_t[:, 0], n[:, 0, 0]), (minus_c, n[:, 1, 1]), (c_t[:, 1], n[:, 0, 1]), (c_t[:, 1], n[:, 1, 0]))
                    for at, (left, right) in enumerate(terms):
                        mm = pe.matmul(y_bank[0][c // 2][32 * q:32 * q + 32, (c % 2) * T:(c % 2 + 1) * T],
                                       left[:, c, 32 * q:32 * q + 32], right, start=at == 0, stop=at == 3)
                    mm.then_inc(y_part, 1)

                for i in range(S5_TILES + 2):
                    if i < S5_TILES:
                        inputs(i)
                    if i >= 2:
                        outputs(i - 2)
                    if i == 1:
                        pe.wait_ge(pooled_ready, 2)
                        for g in range(4):
                            mm = pe.matmul(turn_bank[g // 2][:, (g % 2) * T:(g % 2 + 1) * T], pool_w[:, g, :],
                                           ab_t[:, 4 + g, :], start=True, stop=True)
                        mm.then_inc(pool_mixed, 1)
                w = unit(4)
                pe.wait_ge(xt_lo_ready, seen(xt_lo_ready, 2))
                for m in range(4):
                    for k in range(4):
                        mm = mm3(pe, h_bank[m // 2][:, (m % 2) * T:(m % 2 + 1) * T],
                                 [v[:, k, m * P:(m + 1) * P] for v in w], (xt_hi[:, k, :], xt_lo[:, k, :]), k == 0, k == 3)
                mm.then_inc(unit_used, 1)
                pe.wait_ge(xt_lo_ready, seen(xt_lo_ready))
                matrix()

            def before_experts(late):
                pe.wait_ge(rw_lo_ready, 1)
                for t in range(TT):
                    if t == 1:
                        late()
                        pe.wait_ge(xt_lo_ready, seen(xt_lo_ready, 2))
                    for k in range(KD):
                        mm = mm3(pe, h_bank[t][:, 0:N_EXPERTS], xt_part(k, t), (rw_hi[:, k, :], rw_lo[:, k, :]),
                                 k == 0, k == KD - 1)
                    mm.then_inc(routed, 1)
                for j in range(2):
                    tile([y_bank[t][j] for t in range(TT)])
                pe.wait_ge(gates_ready, seen(gates_ready))
                products = ((0, tri[:, 0], 0, True, True), (1, tri[:, 1], 0, True, False), (1, tri[:, 0], 1, False, True),
                            (2, tri[:, 1], 0, True, False), (2, tri[:, 1], 1, False, True))
                for at, left, t, start, stop in products:
                    mm = pe.matmul(h_bank[0][:, at * N_EXPERTS:(at + 1) * N_EXPERTS], left, chosen[:, t], start=start,
                                   stop=stop)
                mm.then_inc(placed, 1)
                turn_h(p=True)
                pe.wait_ge(ple_sig, seen(ple_sig, 2 * TT))
                down(True, True)
                pe.wait_ge(tile_taken, seen(tile_taken, TT))

            def experts(l):
                pe.wait_ge(overflow_known, l + 1)
                before, n_before = dict(seen.n), n[0]
                with pe.If(pe.value_load(overflow[0:1, 0:1], min_val=0, max_val=1) == 0):
                    gathered_experts(l)
                seen.n = dict(before)
                after, n[0] = n[0], n_before
                with pe.Else():
                    gated(moe[l], all_half[l])
                assert n[0] == after

            def gathered_experts(l):
                turn, into_h, z = turn_bank[0], h_bank[0], (h_bank[1], turn_bank[1])

                def gather(q, b, dst):
                    for part in range(2):
                        for m in range(2):
                            at = (2 * part + m) * SLOTS
                            for t in range(TT):
                                mm = pe.matmul(dst[:, at:at + SLOTS], xr[:, part, t, (2 * q + m) * P:(2 * q + m + 1) * P],
                                               pick[:, b, t, :], start=t == 0, stop=t == TT - 1)
                    mm.then_inc(gathered[l], 1)

                def gates_by_slot(b):
                    for t in range(TT):
                        for part in range(2):
                            mm = pe.matmul(turn[:, T:T + N_EXPERTS], pick[:, b, t, :], gates_r[:, part, t, :],
                                           start=t == 0 and part == 0, stop=t == TT - 1 and part == 1)
                    return mm

                def gate_up(b, u):
                    w = unit(4)
                    for k in range(4):
                        q, m = (4 * u + k) // 2, k % 2
                        mm = mm3(pe, into_h[:, :], (xe[b][:, q, 0, m, :], xe[b][:, q, 1, m, :]), (w[0][:, k], w[1][:, k]),
                                 u == 0 and k == 0, u == 1 and k == 3)
                    mm.then_inc(unit_used, 1)

                def down_slots(first, done):
                    w = unit(2)
                    pe.wait_ge(ht_lo_ready, seen(ht_lo_ready))
                    for c in range(2):
                        for k in range(2):
                            mm = mm3(pe, z[c][:, :], (ht_hi[:, k, 0:SLOTS], ht_lo[:, k, 0:SLOTS]),
                                     [v[:, k, c * 512:(c + 1) * 512] for v in w], first and k == 0, not first and k == 1)
                    mm.then_inc(done, 1)

                def scatter(b, first, last):
                    pe.wait_ge(ye_lo_ready[l], seen(ye_lo_ready[l], 2))
                    for t in range(TT):
                        for c in range(2):
                            for part in range(2):
                                mm = pe.matmul(y_bank[t][c][:, :], pick_t[:, b, t * P:(t + 1) * P],
                                               ye[:, part, c * 512:(c + 1) * 512], start=first and part == 0,
                                               stop=last and part == 1)
                        if t == 0 and last:
                            mm.then_inc(y_half, 1)
                    if last:
                        mm.then_inc(unit_used, 1)

                def step(e, s, prev=True, next_=True):
                    b = e % 2
                    gate_up(b, 0)
                    pe.wait_ge(turn_taken[l], seen(turn_taken[l]))
                    if next_:
                        if s == 0:
                            pe.wait_ge(slots_ready[l], seen(slots_ready[l]))
                        gather(2 * s, 1 - b, turn)
                    gate_up(b, 1)
                    if next_:
                        pe.wait_ge(xe_ready[l], seen(xe_ready[l]))
                        gather(2 * s + 1, 1 - b, turn)
                    if s == 1:
                        if prev:
                            scatter(1 - b, isinstance(prev, str), False)
                        down_slots(True, unit_used)
                    elif prev:
                        down_slots(False, unit_used)
                    pe.wait_ge(h_ready, seen(h_ready, TT))
                    if next_:
                        pe.wait_ge(xe_ready[l], seen(xe_ready[l]))
                    for k in range(2):
                        mm = pe.transpose(turn[:, k * P:(k + 1) * P], h[:, 0, k * P:(k + 1) * P], ident[:, :])
                    if s == 0:
                        for t in range(TT):
                            mm = pe.matmul(turn[:, T + t * P:T + (t + 1) * P], pick[:, b, t, :], ident_r, start=True,
                                           stop=True)
                    elif next_:
                        mm = gates_by_slot(1 - b)
                    mm.then_inc(h_turned, 1)

                pe.wait_ge(slots_ready[l], seen(slots_ready[l]))
                for q, dst in enumerate((turn, into_h) + z):
                    gather(q, 0, dst)
                pe.wait_ge(xe_ready[l], seen(xe_ready[l], 4))
                gates_by_slot(0).then_inc(first_gates[l], 1)
                for s in range(2):
                    step(0, s, prev=False)
                for s in range(2):
                    step(1, s, prev="first")
                with seen.loop(SLOT_ROUNDS, [(lo_ready, 12), (h_ready, 4 * TT), (ht_lo_ready, 4), (slots_ready[l], 2),
                                             (xe_ready[l], 8), (turn_taken[l], 4), (ye_lo_ready[l], 4)]):
                    for e in range(2, 4):
                        for s in range(2):
                            step(e, s)
                n[0] += 12 * (SLOT_ROUNDS - 1)
                for s in range(2):
                    step(14, s)
                for s in range(2):
                    step(15, s, next_=False)
                down_slots(False, last_out[l])
                scatter(1, False, True)

            pe.wait_ge(const_made, 1)
            pe.wait_ge(x_loaded, 16)
            late = turn_to_xt(x, None)
            for l in range(DEPTH):
                gated(ff[l][0], late=late)
                hybrid(l, turn_to_xt(x, x_ready))
                gated(ff[l][1], late=turn_to_xt(x, x_ready))
                late = turn_to_xt(x, x_ready)
            for l in range(DEPTH):
                (s5_and_pool, stick_breaking)[l](late)
                before_experts(turn_to_xt(x, x_ready))
                experts(l)
                if l < DEPTH - 1:
                    late = turn_to_xt(x, x_ready)

        @block.scalar
        def _(act):
            seen = Tally(act)
            n = [0]

            def link(ins):
                ins.then_inc(act_link, 1)
                act.wait_ge(act_link, seen(act_link))

            early = [0]

            def split_early():
                split()
                early[0] = 1

            def split(times=1):
                times, early[0] = times - early[0], 0
                for _ in range(times):
                    s, r = n[0] % SPLIT, n[0] % RAW
                    act.wait_ge(unit_loaded[r], seen(unit_loaded[r], 32))
                    if n[0] >= SPLIT:
                        act.wait_ge(unit_used, seen(unit_used))
                    act.activation(hi[s][:, :], raw[r][:, :], ACT.Copy).then_inc(hi_ready, 1)
                    n[0] += 1

            def wait_units():
                act.wait_ge(unit_used, n[0] - AHEAD)

            def gated(w, half=first_half, aside=None):
                def silu(t):
                    act.activation(gate_act[:, t], h_bank[t][:, 0:HALF], ACT.Silu).then_inc(gate_ready, 1)

                def step(j):
                    split(1 if j == 0 else 2)
                    act.wait_ge(half, seen(half))
                    silu(0)
                    act.wait_ge(unit_used, seen.ahead(unit_used, 2 if j == 0 else 1))
                    silu(1)
                    split()
                    act.wait_ge(h_turned, seen(h_turned))
                    act.activation(ht_hi[:, :, :].rearrange("p k t -> p (k t)"), turn_bank[0][:, :], ACT.Copy)\
                        .then_inc(ht_hi_ready, 1)
                for j in range(w.peeled + 1):
                    step(j)
                    if j == 1 and aside is not None:
                        aside()
                with seen.loop(w.rounds, [(s, 32) for s in unit_loaded] + [(unit_used, 6), (half, 2), (h_turned, 2)]):
                    step(1)
                    step(1)
                n[0] += 6 * (w.rounds - 1)
                if w is not moe[-1]:
                    split()

            def turned_to_xt(after_norm=True):
                for t in range(TT):
                    for b in range(2):
                        act.wait_ge(x_turned, seen(x_turned))
                        act.activation(xt_hi[:, 4 * b:4 * b + 4, t * P:(t + 1) * P],
                                       turn_bank[b][:, :].rearrange("p (k t) -> p k t", k=4), ACT.Copy)\
                            .then_inc(xt_hi_ready, 1)
                    if t == 0 and after_norm:
                        split_early()

            def turned_rows(dsts):
                for r, dst in enumerate(dsts):
                    act.wait_ge(row_turned, seen(row_turned))
                    src = turn_bank[r % 2][:, :].rearrange("p (m t) -> p m t", m=2)
                    if len(dst.shape) == 3:
                        ins = act.activation(dst, src, ACT.Copy)
                    else:
                        for c in range(2):
                            rows = slice(HD * c, HD * c + HD)
                            ins = act.activation(dst[rows, :, c], src[rows], ACT.Copy)
                    ins.then_inc(col_ready, 1)

            def make_tables():
                act.wait_ge(const_loaded, 16 * N_LOADS)
                act.wait_ge(const_made, 7)
                act.wait_ge(lam_sums, 1)
                act.activation(lam_e, lam_e, ACT.Exp).then_inc(lam_exps, 1)
                act.wait_ge(angles, seen(angles))
                act.activation(rope[:, 1], rope[:, 0], ACT.Sin).then_inc(act_link, 1)
                link(act.activation(rot[:, 0, 0:TT * HD].rearrange("p (t d) -> p t d", t=TT), rope[:, 0], ACT.Abs))
                act.wait_ge(act_link, seen(act_link))
                act.activation(rope[:, 0], rot[:, 0, 0:TT * HD].rearrange("p (t d) -> p t d", t=TT), ACT.Sin,
                               bias=half_pi[:, 0:1], scale=-1.0).then_inc(sines, 1)

            def hybrid(l):
                split(9)
                turned_rows([qz1[:, 0:2], qz1[:, 2:4], kt1[:, 0:2], kt1[:, 2:4], qz1[:, 4:6], qz1[:, 6:8], kt1[:, 4:6]])

                def exps(i):
                    b = i % 2
                    act.wait_ge(neg_ready, seen(neg_ready))
                    for c in range(2):
                        src = h_bank[b][:, c * T:(c + 1) * T] if i < 8 else e1[:, b, c]
                        ins = act.activation(e1[:, b, c], src, ACT.Exp, bias=neg[:, b, c:c + 1], scale=SCALE,
                                             accum_out=sums[:, b, c:c + 1])
                    if i >= 8:
                        ins = act.activation(sink_e[:, b], sink_e[:, b], ACT.Exp)
                    ins.then_inc(exp_ready, 1)

                def copies(i):
                    act.wait_ge(prob_turned, seen(prob_turned))
                    width = T if i < 8 else 2 * T
                    act.activation(pt1[:, i % 2, 0:width], turn_bank[i % 2][:, 0:width], ACT.Copy).then_inc(pt_ready, 1)

                for i in range(18):
                    if i < 16:
                        exps(i)
                    if i >= 2:
                        copies(i - 2)
                act.wait_ge(pv_done, seen(pv_done, 16))
                for t in range(TT):
                    for d in range(DIFF_HEADS):
                        ins = act.activation(e1[:, t, d // 2, (d % 2) * P:(d % 2 + 1) * P], y_bank[t][0][:, d * P:(d + 1) * P], ACT.Square,
                                             accum_out=ssq[:, t, d:d + 1])
                    ins.then_inc(squares, 1)
                for t in range(TT):
                    act.activation(mix[:, t, 512:D], y_bank[t][1][:, :], ACT.Copy).then_inc(swa_out, 1)
                turned_to_xt(after_norm=False)
                split(4)

            def stick_breaking():
                for j in range(6):
                    split(2)
                    if 1 <= j <= 4:
                        dst = (qz2, kt2)[(j - 1) // 2]
                        k = 4 * ((j - 1) % 2)
                        turned_rows([dst[:, k + 2 * r:k + 2 * r + 2] for r in range(2)])
                act.preload_act_table_set("natural_log_exp_and_others")

                def logs(i):
                    b, n_keys = i % 2, (i % 2 + 1) * P
                    act.wait_ge(zm_ready, seen(zm_ready))
                    v = sp_[:, b, :, 0:n_keys]
                    link(act.activation(v, zm[:, b, :, 0:n_keys], ACT.Abs))
                    link(act.activation(v, v, ACT.Exp, scale=-1.0))
                    act.activation(v, v, ACT.Ln, bias=1.0).then_inc(sp_ready, 1)

                def weights(i):
                    b, n_keys = i % 2, (i % 2 + 1) * P
                    act.wait_ge(arg_ready, seen(arg_ready))
                    act.activation(w2[:, b, :, 0:n_keys], zm[:, b, :, 0:n_keys], ACT.Exp).then_inc(w_ready, 1)

                def copies(i):
                    act.wait_ge(prob_turned, seen(prob_turned))
                    for c in range(2):
                        at = slice(c * T, c * T + (i % 2 + 1) * P)
                        ins = act.activation(wt2[:, i % 2, at], turn_bank[i % 2][:, at], ACT.Copy)
                    ins.then_inc(pt_ready, 1)

                for i in range(18):
                    if i < 16:
                        logs(i)
                    if 1 <= i < 17:
                        weights(i - 1)
                    if i >= 2:
                        copies(i - 2)
                act.wait_ge(pv_done, seen(pv_done, 16))
                for b in range(4):
                    act.activation(xt_hi[:, 2 * b:2 * b + 2, :],
                                   y_bank[b // 2][b % 2][:, :].rearrange("p (k t) -> p k t", k=2), ACT.Copy)\
                        .then_inc(xt_hi_ready, 1)
                split(4)

            def s5_parameters():
                act.activation(rw_hi[:, :, :], router_w, ACT.Copy).then_inc(rw_hi_ready, 1)
                act.activation(dt5, log_dt, ACT.Exp).then_inc(s5_act, 1)
                act.wait_ge(s5_dve, seen(s5_dve))
                act.activation(mag5, tmpa, ACT.Exp).then_inc(s5_act, 1)
                act.wait_ge(s5_dve, seen(s5_dve))
                act.activation(sin5, r5, ACT.Sin).then_inc(s5_act, 1)
                link(act.activation(abs5, r5, ACT.Abs))
                act.activation(cos5, abs5, ACT.Sin, bias=half_pi[:, 0:1], scale=-1.0).then_inc(s5_act, 1)

            def s5_and_pool():
                split()
                for r in range(4):
                    act.wait_ge(wide_turned, seen(wide_turned))
                    dst = (bb_t, c_t)[r // 2][:, r % 2]
                    if r == 2:
                        act.activation(minus_c, turn_bank[0][:, :].rearrange("p (c m) -> p c m", c=4), ACT.Copy, scale=-1.0)
                    act.activation(dst, turn_bank[r % 2][:, :].rearrange("p (c m) -> p c m", c=4), ACT.Copy,
                                   scale=-1.0 if r == 3 else 1.0).then_inc(wide_copied, 1)

                def sines_of(c):
                    act.wait_ge(turns_ready, seen(turns_ready))
                    if c >= 2:
                        act.wait_ge(st_ready, 8 * (c - 1))
                    act.activation(trig[c % 2][:, 1], th[:, 0], ACT.Sin, scale=6.283185).then_inc(act_link, 1)
                    link(act.activation(th[:, 1], th[:, 0], ACT.Abs))
                    act.wait_ge(act_link, seen(act_link))
                    act.activation(trig[c % 2][:, 0], th[:, 1], ACT.Sin, bias=half_pi[:, 0:1], scale=-6.283185)\
                        .then_inc(trig_ready, 1)

                split()
                sines_of(0)
                split(2)
                turned_rows([ab_t[:, 2 * r:2 * r + 2, :] for r in range(2)])
                act.wait_ge(pooled, 1)
                for b in range(2):
                    act.activation(ab_t[:, 4 + 2 * b:6 + 2 * b, :], y_bank[1][b][:, :].rearrange("p (g t) -> p g t", g=2),
                                   ACT.Copy).then_inc(pooled_ready, 1)
                sines_of(1)
                act.wait_ge(pool_mixed, 1)
                for g in range(4):
                    ins = act.activation(xt_hi[:, 4 + g, :], turn_bank[g // 2][:, (g % 2) * T:(g % 2 + 1) * T], ACT.Copy,
                                         scale=pool_scale[:, g:g + 1])
                ins.then_inc(xt_hi_ready, 1)
                for c in range(2, 4):
                    sines_of(c)
                act.wait_ge(s5_dve, seen(s5_dve))
                act.activation(g5, y5, ACT.Square).then_inc(s5_act, 1)
                act.wait_ge(s5_dve, seen(s5_dve))
                act.activation(g5, g5, ACT.Sigmoid, scale=GELU_C).then_inc(s5_act, 1)
                act.wait_ge(s5_dve, seen(s5_dve))
                act.activation(xt_hi[:, 0:4, :], y5, ACT.Copy).then_inc(xt_hi_ready, 1)
                split()
                wait_units()
                for b in range(2):
                    act.activation(g5[:, 2 * b:2 * b + 2, :], h_bank[b][:, :].rearrange("p (m t) -> p m t", m=2),
                                   ACT.Sigmoid).then_inc(s5_act, 1)
                act.wait_ge(s5_dve, seen(s5_dve))
                act.activation(xt_hi[:, 0:4, :], y5, ACT.Copy).then_inc(xt_hi_ready, 1)
                split(4)

            def before_experts(l):
                for t in range(TT):
                    act.wait_ge(routed, seen(routed))
                    act.activation(r_s[:, t], h_bank[t][:, 0:N_EXPERTS], ACT.Sigmoid).then_inc(route_sig, 1)
                for t in range(TT):
                    act.activation(xr[:, 0, t], x[:, t, :], ACT.Copy).then_inc(x_high, 1)
                for j in range(2):
                    split(2)
                    wait_units()
                    for t in range(TT):
                        act.activation(ple_gate[:, t, j * 512:(j + 1) * 512], y_bank[t][j][:, :], ACT.Sigmoid)\
                            .then_inc(ple_sig, 1)
                act.wait_ge(h_turned, seen(h_turned))
                act.activation(ht_hi[:, :, :].rearrange("p k t -> p (k t)"), turn_bank[0][:, :], ACT.Copy)\
                    .then_inc(ht_hi_ready, 1)
                split()

            def experts(l):
                act.wait_ge(overflow_known, l + 1)
                before, n_before = dict(seen.n), n[0]
                with act.If(act.value_load(overflow[0:1, 0:1], min_val=0, max_val=1) == 0):
                    gathered_experts(l)
                seen.n = dict(before)
                after, n[0] = n[0], n_before
                with act.Else():
                    gated(moe[l], all_half[l])
                assert n[0] == after

            def gathered_experts(l):
                z = h_bank[1], turn_bank[1]

                def copy_xe(b, q, src):
                    act.wait_ge(gathered[l], seen(gathered[l]))
                    act.activation(xe[b][:, q].rearrange("p a m c -> p (a m c)"), src[:, :], ACT.Copy)\
                        .then_inc(xe_ready[l], 1)

                def high_ye():
                    for c in range(2):
                        act.activation(ye[:, 0, c * 512:(c + 1) * 512], z[c][:, :], ACT.Copy).then_inc(ye_hi_ready[l], 1)

                def step(e, s, prev=True, next_=True):
                    b = e % 2
                    if s == 1 or prev:
                        split()
                    if next_:
                        copy_xe(1 - b, 2 * s, turn_bank[0])
                    split()
                    act.wait_ge(unit_used, seen.ahead(unit_used, 1 if s == 1 or prev else 2))
                    act.activation(gate_act[:, 0], h_bank[0][:, 0:HALF], ACT.Silu).then_inc(gate_ready, TT)
                    if next_:
                        copy_xe(1 - b, 2 * s + 1, turn_bank[0])
                    split()
                    act.wait_ge(h_turned, seen(h_turned))
                    act.activation(ht_hi[:, :, 0:SLOTS], turn_bank[0][:, 0:2 * SLOTS].rearrange("p (k c) -> p k c", k=2),
                                   ACT.Copy).then_inc(ht_hi_ready, 1)
                    if s == 0 and prev:
                        high_ye()

                for q, src in enumerate((turn_bank[0], h_bank[0]) + z):
                    copy_xe(0, q, src)
                for s in range(2):
                    step(0, s, prev=False)
                for s in range(2):
                    step(1, s)
                with seen.loop(SLOT_ROUNDS, [(s, 64) for s in unit_loaded] + [(unit_used, 12),
                                                                              (h_turned, 4), (gathered[l], 8)]):
                    for e in range(2, 4):
                        for s in range(2):
                            step(e, s)
                n[0] += 12 * (SLOT_ROUNDS - 1)
                for s in range(2):
                    step(14, s)
                for s in range(2):
                    step(15, s, next_=False)
                act.wait_ge(last_out[l], 1)
                high_ye()
                if l < DEPTH - 1:
                    split()

            split(AHEAD)
            turned_to_xt(after_norm=False)
            for l in range(DEPTH):
                gated(ff[l][0], aside=make_tables if l == 0 else None)
                turned_to_xt()
                hybrid(l)
                turned_to_xt()
                gated(ff[l][1], aside=s5_parameters if l == DEPTH - 1 else None)
                turned_to_xt()
            for l in range(DEPTH):
                (s5_and_pool, stick_breaking)[l]()
                turned_to_xt()
                before_experts(l)
                experts(l)
                if l < DEPTH - 1:
                    turned_to_xt()

        @block.vector
        def _(dve):
            seen = Tally(dve)
            n = [0]

            def link(ins):
                ins.then_inc(dve_link, 1)
                dve.wait_ge(dve_link, seen(dve_link))

            early = [0]

            def split_early():
                split()
                early[0] = 1

            def split(times=1):
                times, early[0] = times - early[0], 0
                for _ in range(times):
                    s, r = n[0] % SPLIT, n[0] % RAW
                    dve.wait_ge(hi_ready, seen(hi_ready))
                    dve.tensor_tensor(lo[s][:, :], raw[r][:, :], hi[s][:, :].bitcast(F32), ALU.subtract)\
                        .then_inc(lo_ready, 1)
                    n[0] += 1

            def wait_units():
                dve.wait_ge(unit_used, n[0] - AHEAD)

            def low_h():
                dve.wait_ge(ht_hi_ready, seen(ht_hi_ready))
                dve.tensor_tensor(ht_lo[:, :, :].rearrange("p k t -> p (k t)"), turn_bank[0][:, :],
                                  ht_hi[:, :, :].bitcast(F32).rearrange("p k t -> p (k t)"), ALU.subtract)\
                    .then_inc(ht_lo_ready, 1)

            def gated(w, aside=None):
                def step(i, j):
                    split(1 if j == 0 else 2)
                    for t in range(TT):
                        dve.wait_ge(gate_ready, seen(gate_ready))
                        up = h_bank[t][:, HALF:2 * HALF]
                        if w.experts:
                            e = i + j // EXPERT_STEPS
                            g = gates[:, t, e:e + 1] if isinstance(e, int) else gates[:, t, bass.ds(e, 1)]
                            ins = dve.scalar_tensor_tensor(out=h[:, t], in0=up, scalar=g, in1=gate_act[:, t],
                                                           op0=ALU.mult, op1=ALU.mult)
                        else:
                            ins = dve.tensor_tensor(h[:, t], up, gate_act[:, t], ALU.mult)
                        ins.then_inc(h_ready, 1)
                    split()
                    low_h()
                for j in range(w.peeled + 1):
                    step(0, j)
                    if j == 1 and aside is not None:
                        aside()
                with seen.loop(w.rounds, [(hi_ready, 6), (gate_ready, 2 * TT), (ht_hi_ready, 2)]) as i:
                    step(i, w.peeled + 1)
                    step(i, w.peeled + 2)
                n[0] += 6 * (w.rounds - 1)
                if w is not moe[-1]:
                    split()

            def norm(k, coef, done, split_ahead=AHEAD):
                def residual(t, c):
                    v = x[:, t, c * 512:(c + 1) * 512]
                    dve.scalar_tensor_tensor(out=v, in0=v, scalar=coef, in1=y_bank[t][c][:, :],
                                             op0=ALU.mult, op1=ALU.add).then_inc(dve_link, 1)

                def variance(t):
                    for c in range(2):
                        dve.bn_stats(stats[:, t, c, :], x[:, t, c * 512:(c + 1) * 512]).then_inc(dve_link, 1)
                    dve.wait_ge(dve_link, seen(dve_link, 2))
                    dve.bn_aggr(moments[:, t, :], stats[:, t].rearrange("p c s -> p (c s)")).then_inc(var_ready, 1)
                    dve.wait_ge(var_ready, seen(var_ready))

                def scaled(t):
                    link(dve.scalar_tensor_tensor(out=x[:, t, :], in0=x[:, t, :], scalar=moments[:, t, 0:1],
                                                  in1=ln_gb[:, 0, :], op0=ALU.subtract, op1=ALU.mult))
                    dve.wait_ge(rstd_ready, seen(rstd_ready))
                    for c in range(2):
                        v = x[:, t, c * 512:(c + 1) * 512]
                        dve.scalar_tensor_tensor(out=v, in0=v, scalar=rstd[:, t, 0:1], in1=ln_gb[:, 1, c * 512:(c + 1) * 512],
                                                 op0=ALU.mult, op1=ALU.add).then_inc(done, 1)

                dve.wait_ge(y_half, seen(y_half))
                for c in range(2):
                    residual(0, c)
                dve.wait_ge(dve_link, seen(dve_link, 2))
                variance(0)
                dve.wait_ge(unit_used, n[0] - split_ahead)
                residual(1, 0)
                dve.wait_ge(gb_loaded, 32 * (k + 1))
                dve.wait_ge(dve_link, seen(dve_link))
                scaled(0)
                residual(1, 1)
                dve.wait_ge(dve_link, seen(dve_link))
                variance(1)
                if done is x_ready:
                    low_xt(0)
                scaled(1)
                if done is x_ready:
                    split_early()
                    low_xt(1)

            def low_xt(t):
                for b in range(2):
                    dve.wait_ge(xt_hi_ready, seen(xt_hi_ready))
                    at = (slice(None), slice(4 * b, 4 * b + 4), slice(t * P, (t + 1) * P))
                    dve.tensor_tensor(xt_lo[at], turn_bank[b][:, :].rearrange("p (k t) -> p k t", k=4),
                                      xt_hi[at].bitcast(F32), ALU.subtract).then_inc(xt_lo_ready, 1)

            def reduce_angle(dst, src, whole):
                link(dve.tensor_scalar(whole, src, 1.0 / TWO_PI, ROUND, ALU.mult, ALU.add))
                link(dve.tensor_scalar(whole, whole, ROUND, None, ALU.subtract))
                for part, first in ((TP_HI, src), (TP_MID, dst), (TP_LO, dst)):
                    link(dve.scalar_tensor_tensor(out=dst, in0=whole, scalar=-part, in1=first, op0=ALU.mult, op1=ALU.add))
                return dve.tensor_scalar(dst, dst, PI_IN, -PI_IN, ALU.min, ALU.max)

            def make_tables():
                dve.wait_ge(const_loaded, 16 * N_LOADS)
                prod = rot[:, 0, 0:DEPTH * 2 * HD].rearrange("p (l i d) -> p l i d", l=DEPTH, i=2)
                for l in range(DEPTH):
                    v = lam_in[:, l].rearrange("p (i j) d -> p j i d", j=2)
                    link(dve.tensor_tensor(prod[:, l], v[:, 0], v[:, 1], ALU.mult))
                dve.tensor_reduce(lam_e, prod, AX_X, ALU.add).then_inc(lam_sums, 1)
                dve.wait_ge(lam_exps, 1)
                for l in range(DEPTH):
                    link(dve.tensor_tensor(lam[:, l:l + 1], lam_e[:, l, 0:1], lam_e[:, l, 1:2], ALU.subtract))
                    link(dve.tensor_scalar(lam[:, l:l + 1], lam[:, l:l + 1], lambda_init(l), None, ALU.add))
                    link(dve.tensor_scalar(sub_g[:, l], sub_g[:, l], 1.0 - lambda_init(l), None, ALU.mult))
                link(dve.tensor_scalar(neg_sink, sink, -1.0, None, ALU.mult))
                pos = small[:, 52:54]
                link(dve.tensor_copy(pos, position[:, :]))
                ang = rot[:, 1, 0:TT * 32].rearrange("p (t f) -> p t f", t=TT)
                whole = rot[:, 1, 64:64 + TT * 32].rearrange("p (t f) -> p t f", t=TT)
                red = rot[:, 1, 128:128 + TT * 32].rearrange("p (t f) -> p t f", t=TT)
                for t in range(TT):
                    link(dve.tensor_scalar(ang[:, t], freq, pos[:, t:t + 1], None, ALU.mult))
                link(reduce_angle(red, ang, whole))
                link(dve.tensor_copy(rope[:, 0, :, 0:32], red))
                dve.tensor_copy(rope[:, 0, :, 32:64], red).then_inc(angles, 1)
                dve.wait_ge(sines, 1)
                link(dve.tensor_scalar(rope[:, 1, :, 0:32], rope[:, 1, :, 0:32], -1.0, None, ALU.mult))

            def rotate(t, src, heads, dsts, done):
                cos = rope[:, 0, t:t + 1, :].broadcast_to([P, heads, HD])
                sin = rope[:, 1, t:t + 1, :].broadcast_to([P, heads, HD])
                by_cos = rot[:, 0, 0:heads * HD].rearrange("p (h d) -> p h d", h=heads)
                by_sin = rot[:, 1, 0:heads * HD].rearrange("p (h d) -> p h d", h=heads)
                dve.tensor_tensor(by_sin[:, :, 0:32], src[:, :, 32:64], sin[:, :, 0:32], ALU.mult).then_inc(dve_link, 1)
                dve.tensor_tensor(by_sin[:, :, 32:64], src[:, :, 0:32], sin[:, :, 32:64], ALU.mult).then_inc(dve_link, 1)
                dve.tensor_tensor(by_cos, src, cos, ALU.mult).then_inc(tile_taken, 1)
                dve.wait_ge(dve_link, seen(dve_link, 2))
                dve.wait_ge(tile_taken, seen(tile_taken))
                for dst in dsts:
                    ins = dve.tensor_tensor(dst, by_cos, by_sin, ALU.add)
                ins.then_inc(done, 1)
                if done is dve_link:
                    dve.wait_ge(dve_link, seen(dve_link))

            def hybrid(l):
                link(dve.memset(qz1, 0.0))
                for j in range(5):
                    split(1 if j == 3 else 2)
                    wait_units()
                    for t in range(TT):
                        bank_ = y_bank[t][j % 2]
                        if j < 3:
                            rotate(t, bank_[:, :].rearrange("p (h d) -> p h d", h=8), 8,
                                   [qk[:, t, j * 512:(j + 1) * 512].rearrange("p (h d) -> p h d", h=8)], dve_link)
                        elif j == 3:
                            link(dve.tensor_copy(v1[:, t, 512:640], bank_[:, P:2 * P]))
                            twice = qk[:, t, 1536:1792].rearrange("p (h two d) -> p two h d", h=2, two=2)
                            rotate(t, bank_[:, 0:P].rearrange("p (h d) -> p h d", h=2), 2, [twice[:, 0], twice[:, 1]],
                                   row_ready)
                        else:
                            dve.tensor_copy(v1[:, t, 0:512], bank_[:, :]).then_inc(tile_taken, 1)
                            dve.wait_ge(tile_taken, seen(tile_taken))

                def maxima(i):
                    b = i % 2
                    dve.wait_ge(scores_ready, seen(scores_ready))
                    if i >= 2:
                        dve.wait_ge(prob_ready, 16 * l + i - 1)
                    s = h_bank[b][:, :].rearrange("p (c k) -> p c k", c=2)
                    if i >= 8:
                        pair, t = (i - 8) // 2, i % 2
                        mask = swa_mask[:, t:t + 1, :].broadcast_to([P, 2, T])
                        link(dve.tensor_tensor(e1[:, b], s, mask, ALU.add))
                        s = e1[:, b]
                    link(dve.tensor_reduce(nmax[:, b], s, AX_X, ALU.max, negate=True))
                    if i < 8:
                        dve.tensor_scalar(neg[:, b], nmax[:, b], SCALE, None, ALU.mult).then_inc(neg_ready, 1)
                    else:
                        two = slice(2 * pair, 2 * pair + 2)
                        link(dve.scalar_tensor_tensor(out=neg[:, b], in0=nmax[:, b], scalar=SCALE,
                                                      in1=neg_sink[:, l, two], op0=ALU.mult, op1=ALU.min))
                        dve.tensor_tensor(sink_e[:, b], sink[:, l, two], neg[:, b], ALU.add).then_inc(neg_ready, 1)

                def probs(i):
                    b = i % 2
                    dve.wait_ge(exp_ready, seen(exp_ready))
                    if i >= 2:
                        dve.wait_ge(prob_turned, 16 * l + i - 1)
                    if i < 8:
                        link(dve.reciprocal(inv[:, b], sums[:, b]))
                        link(dve.tensor_scalar(p1[:, b, 1], e1[:, b, 1], inv[:, b, 1:2], lam[:, l:l + 1], ALU.mult, ALU.mult))
                        dve.scalar_tensor_tensor(out=p1[:, b, 0], in0=e1[:, b, 0], scalar=inv[:, b, 0:1], in1=p1[:, b, 1],
                                                 op0=ALU.mult, op1=ALU.subtract).then_inc(prob_ready, 1)
                    else:
                        link(dve.tensor_tensor(sums[:, b], sums[:, b], sink_e[:, b], ALU.add))
                        link(dve.reciprocal(inv[:, b], sums[:, b]))
                        for c in range(2):
                            ins = dve.tensor_scalar(p1[:, b, c], e1[:, b, c], inv[:, b, c:c + 1], None, ALU.mult)
                        ins.then_inc(prob_ready, 1)

                for i in range(17):
                    if i < 16:
                        maxima(i)
                    if i >= 1:
                        probs(i - 1)
                dve.wait_ge(sub_rstd, seen(sub_rstd))
                for t in range(TT):
                    for d in range(DIFF_HEADS):
                        ins = dve.scalar_tensor_tensor(out=mix[:, t, d * P:(d + 1) * P], in0=y_bank[t][0][:, d * P:(d + 1) * P],
                                                       scalar=srs[:, t, d:d + 1], in1=sub_g[:, l], op0=ALU.mult, op1=ALU.mult)
                    ins.then_inc(mix_ready, 1)
                for t in range(TT):
                    low_xt(t)
                split(4)

            def stick_breaking():
                link(dve.memset(qz2, 0.0))
                for j in range(6):
                    split(2)
                    wait_units()
                    for t in range(TT):
                        if j < 4:
                            dve.tensor_copy(qk_row[:, j % 2, t], y_bank[t][j % 2][:, :]).then_inc(row_ready, 1)
                        else:
                            dve.tensor_copy(v2[:, t, (j - 4) * 512:(j - 3) * 512], y_bank[t][j % 2][:, :])\
                                .then_inc(tile_taken, 1)
                seen(tile_taken, 2 * TT)

                def masked(i):
                    b, n_keys = i % 2, (i % 2 + 1) * P
                    if i >= 2:
                        dve.wait_ge(w_ready, seen(w_ready))
                    dve.wait_ge(scores_ready, seen(scores_ready))
                    mask = causal[:, T - n_keys:T].rearrange("p (o k) -> p o k", o=1).broadcast_to([P, 2, n_keys])
                    s = h_bank[b][:, :].rearrange("p (c k) -> p c k", c=2)[:, :, 0:n_keys]
                    dve.scalar_tensor_tensor(out=zm[:, b, :, 0:n_keys], in0=s, scalar=SCALE, in1=mask,
                                             op0=ALU.mult, op1=ALU.add).then_inc(zm_ready, 1)

                def exponents(i):
                    b, n_keys = i % 2, (i % 2 + 1) * P
                    dve.wait_ge(sp_ready, seen(sp_ready))
                    if i >= 2:
                        dve.wait_ge(prob_turned, 16 * DEPTH + i - 1)
                    z, keep = zm[:, b, :, 0:n_keys], soft[:, b, :, 0:n_keys]
                    link(dve.scalar_tensor_tensor(out=keep, in0=z, scalar=0.0, in1=sp_[:, b, :, 0:n_keys],
                                                  op0=ALU.max, op1=ALU.add))
                    for c in range(2):
                        dve.tensor_tensor_scan(w2[:, b, c, 0:n_keys][:, ::-1], before[:, 1, 0:1].broadcast_to([P, n_keys]),
                                               soft[:, b, c, 0:n_keys][:, ::-1], 0.0, ALU.mult, ALU.add).then_inc(dve_link, 1)
                    dve.wait_ge(dve_link, seen(dve_link, 2))
                    dve.tensor_tensor(z, z, w2[:, b, :, 0:n_keys], ALU.subtract).then_inc(arg_ready, 1)

                for i in range(17):
                    if i < 16:
                        masked(i)
                    if i >= 1:
                        exponents(i - 1)
                for b in range(4):
                    dve.wait_ge(xt_hi_ready, seen(xt_hi_ready))
                    dve.tensor_tensor(xt_lo[:, 2 * b:2 * b + 2, :],
                                      y_bank[b // 2][b % 2][:, :].rearrange("p (k t) -> p k t", k=2),
                                      xt_hi[:, 2 * b:2 * b + 2, :].bitcast(F32), ALU.subtract).then_inc(xt_lo_ready, 1)
                split(4)

            def s5_parameters():
                dve.wait_ge(rw_hi_ready, 1)
                dve.tensor_tensor(rw_lo[:, :, :], router_w, rw_hi[:, :, :].bitcast(F32), ALU.subtract)\
                    .then_inc(rw_lo_ready, 1)
                dve.wait_ge(s5_act, seen(s5_act))
                link(dve.tensor_tensor(ang5, lam_im, dt5, ALU.mult))
                dve.tensor_tensor(tmpa, lam_re, dt5, ALU.mult).then_inc(s5_dve, 1)
                reduce_angle(r5, ang5, k5).then_inc(s5_dve, 1)
                dve.wait_ge(s5_dve, 2)
                link(dve.tensor_scalar(phi5, r5, 1.0 / TWO_PI, None, ALU.mult))
                link(dve.tensor_tensor(den, lam_re, lam_re, ALU.mult))
                link(dve.tensor_tensor(tmpb, lam_im, lam_im, ALU.mult))
                link(dve.tensor_tensor(den, den, tmpb, ALU.add))
                link(dve.reciprocal(den, den))
                dve.wait_ge(s5_act, seen(s5_act, 3))
                link(dve.tensor_tensor(lbr, mag5, cos5, ALU.mult))
                link(dve.tensor_tensor(lbi, mag5, sin5, ALU.mult))
                link(dve.tensor_scalar(lbr, lbr, 1.0, None, ALU.subtract))
                for f, (u, v), op in ((fre, (lam_re, lam_im), ALU.add), (fim, (lam_im, lam_re), ALU.subtract)):
                    link(dve.tensor_tensor(tmpa, lbr, u, ALU.mult))
                    link(dve.tensor_tensor(tmpb, lbi, v, ALU.mult))
                    first, second = (tmpa, tmpb) if op is ALU.add else (tmpb, tmpa)
                    link(dve.tensor_tensor(f, first, second, op))
                    link(dve.tensor_tensor(f, f, den, ALU.mult))
                dve.wait_ge(s5_loaded, 16 * 5)
                link(dve.memset(bb_wide, 0.0))
                f_re = fre.rearrange("p (i o) -> p i o", o=1).broadcast_to([P, 16, 16])
                f_im = fim.rearrange("p (i o) -> p i o", o=1).broadcast_to([P, 16, 16])
                for ri in range(2):
                    link(dve.tensor_tensor(bb_tmp[:, 0], b_nat[:, ri], f_re, ALU.mult))
                    link(dve.tensor_tensor(bb_tmp[:, 1], b_nat[:, 1 - ri], f_im, ALU.mult))
                    for g in range(2):
                        r = slice(P5 * g, P5 * g + P5)
                        link(dve.tensor_tensor(bb_wide[r, ri, :, 16 * g:16 * g + 16], bb_tmp[r, 0], bb_tmp[r, 1],
                                               ALU.subtract if ri == 0 else ALU.add))
                    for g in range(2):
                        ins = dve.tensor_scalar(c_wide[:, ri, :, P5 * g:P5 * g + P5], c_nat[:, ri], parity[:, g:g + 1],
                                                None, ALU.mult)
                        ins.then_inc(wide_ready, 1)

            def s5_and_pool():
                def angles_of(c):
                    phi = phi5[:, 4 * c:4 * c + 4].rearrange("p (i o) -> p i o", o=1).broadcast_to([P, 4, T])
                    time = time_row.rearrange("p (o t) -> p o t", o=1).broadcast_to([P, 4, T])
                    link(dve.tensor_tensor(th[:, 0], phi, time, ALU.mult))
                    link(dve.tensor_scalar(th[:, 1], th[:, 0], ROUND, ROUND, ALU.add, ALU.subtract))
                    dve.tensor_tensor(th[:, 0], th[:, 0], th[:, 1], ALU.subtract).then_inc(turns_ready, 1)

                for j in range(2):
                    split(2)
                    if j == 0:
                        dve.wait_ge(wide_turned, 4)
                        angles_of(0)
                    wait_units()
                    for t in range(TT):
                        dve.tensor_copy(ab_row[:, t, j * 512:(j + 1) * 512], y_bank[t][j][:, :]).then_inc(row_ready, 1)
                for c in range(4):
                    dve.wait_ge(trig_ready, c + 1)
                    if c < 3:
                        angles_of(c + 1)
                    if c == 1:
                        dve.wait_ge(xt_hi_ready, seen(xt_hi_ready))
                        for g in range(4):
                            ins = dve.scalar_tensor_tensor(out=xt_lo[:, 4 + g, :],
                                                           in0=turn_bank[g // 2][:, (g % 2) * T:(g % 2 + 1) * T],
                                                           scalar=pool_scale[:, g:g + 1], in1=xt_hi[:, 4 + g, :].bitcast(F32),
                                                           op0=ALU.mult, op1=ALU.subtract)
                        ins.then_inc(xt_lo_ready, 1)
                    for q in range(4):
                        i = 4 * c + q
                        dve.wait_ge(bu_ready, seen(bu_ready))
                        if i > 0:
                            dve.wait_ge(scan_ready, i)
                        bu = h_bank[i % 2][:, :].rearrange("p (c t) -> p c t", c=2)
                        for j in range(2):
                            dve.tensor_tensor(m5[:, j], bu, trig[c % 2][:, j, q:q + 1, :].broadcast_to([P, 2, T]), ALU.mult)\
                                .then_inc(dve_link, 1)
                        dve.wait_ge(dve_link, seen(dve_link, 2))
                        dve.tensor_tensor(m5[:, 0, 0], m5[:, 0, 0], m5[:, 1, 1], ALU.add).then_inc(dve_link, 1)
                        dve.tensor_tensor(m5[:, 0, 1], m5[:, 0, 1], m5[:, 1, 0], ALU.subtract).then_inc(dve_link, 1)
                        dve.wait_ge(dve_link, seen(dve_link, 2))
                        if i >= 2:
                            dve.wait_ge(st_ready, 2 * (i - 1))
                        for ri in range(2):
                            ins = dve.tensor_tensor_scan(s5[:, i % 2, ri], mag5[:, i:i + 1].broadcast_to([P, T]),
                                                         m5[:, 0, ri], 0.0, ALU.mult, ALU.add)
                        ins.then_inc(scan_ready, 1)
                dve.wait_ge(y_part, S5_TILES)
                for c in range(4):
                    ins = dve.scalar_tensor_tensor(out=y5[:, c], in0=ab_t[:, c], scalar=d_skip[:, c:c + 1],
                                                   in1=y_bank[0][c // 2][:, (c % 2) * T:(c % 2 + 1) * T],
                                                   op0=ALU.mult, op1=ALU.add)
                ins.then_inc(s5_dve, 1)
                dve.wait_ge(s5_act, seen(s5_act))
                link(dve.tensor_scalar(g5, g5, 0.044715, 1.0, ALU.mult, ALU.add))
                dve.tensor_tensor(g5, g5, y5, ALU.mult).then_inc(s5_dve, 1)
                dve.wait_ge(s5_act, seen(s5_act))
                dve.tensor_tensor(y5, y5, g5, ALU.mult).then_inc(s5_dve, 1)
                dve.wait_ge(xt_hi_ready, seen(xt_hi_ready))
                dve.tensor_tensor(xt_lo[:, 0:4, :], y5, xt_hi[:, 0:4, :].bitcast(F32), ALU.subtract).then_inc(xt_lo_ready, 1)
                split()
                dve.wait_ge(s5_act, seen(s5_act, 2))
                dve.tensor_tensor(y5, y5, g5, ALU.mult).then_inc(s5_dve, 1)
                dve.wait_ge(xt_hi_ready, seen(xt_hi_ready))
                dve.tensor_tensor(xt_lo[:, 0:4, :], y5, xt_hi[:, 0:4, :].bitcast(F32), ALU.subtract).then_inc(xt_lo_ready, 1)
                split(4)

            def before_experts(l):
                split(1)
                if l == 0:
                    dve.wait_ge(const_made, 8)
                dve.tensor_copy(tri.rearrange("p a c -> p (a c)"), tri_ones).then_inc(dve_link, 1)
                link(dve.tensor_copy(ident_r, ident[:, :]))
                dve.wait_ge(dve_link, seen(dve_link))
                dve.wait_ge(route_sig, seen(route_sig, TT))
                bias = router_b.rearrange("p (o e) -> p o e", o=1).broadcast_to([P, TT, N_EXPERTS])
                link(dve.tensor_tensor(r_sel, r_s, bias, ALU.add))
                four = r_sel.rearrange("p t (g e) -> p (t g) e", g=N_GROUPS)
                for i, (u, v, op) in enumerate(((0, 1, ALU.max), (0, 1, ALU.min), (2, 3, ALU.max), (2, 3, ALU.min))):
                    dve.tensor_tensor(r_two[:, i], four[:, :, u], four[:, :, v], op).then_inc(dve_link, 1)
                dve.wait_ge(dve_link, seen(dve_link, 4))
                dve.tensor_tensor(r_two[:, 4], r_two[:, 0], r_two[:, 2], ALU.max).then_inc(dve_link, 1)
                dve.tensor_tensor(r_two[:, 5], r_two[:, 0], r_two[:, 2], ALU.min).then_inc(dve_link, 1)
                dve.tensor_tensor(r_two[:, 6], r_two[:, 1], r_two[:, 3], ALU.max).then_inc(dve_link, 1)
                dve.wait_ge(dve_link, seen(dve_link, 3))
                link(dve.tensor_tensor(r_two[:, 5], r_two[:, 5], r_two[:, 6], ALU.max))
                link(dve.tensor_tensor(r_two[:, 7], r_two[:, 4], r_two[:, 5], ALU.add))
                score = r_two[:, 7].rearrange("p (t g) -> p t g", t=TT)

                def rank(values, t, n_values, dst):
                    mine = values.rearrange("p (e o) -> p e o", o=1).broadcast_to([P, n_values, n_values])
                    others = values.rearrange("p (o e) -> p o e", o=1).broadcast_to([P, n_values, n_values])
                    g, q = r_gt[:, 0:n_values, 0:n_values], r_eq[:, 0:n_values, 0:n_values]
                    dve.tensor_tensor(g, others, mine, ALU.is_gt).then_inc(dve_link, 1)
                    dve.tensor_tensor(q, others, mine, ALU.is_equal).then_inc(dve_link, 1)
                    dve.wait_ge(dve_link, seen(dve_link, 2))
                    link(dve.tensor_tensor(q, q, before[:, 0:n_values, 0:n_values], ALU.mult))
                    link(dve.tensor_tensor(g, g, q, ALU.add))
                    link(dve.tensor_reduce(dst, g, AX_X, ALU.add))

                for t in range(TT):
                    rank(score[:, t], t, N_GROUPS, r_grp[:, t])
                    link(dve.tensor_scalar(r_grp[:, t], r_grp[:, t], 0.5, FAR, ALU.is_gt, ALU.mult))
                    away = r_grp[:, t].rearrange("p (g o) -> p g o", o=1).broadcast_to([P, N_GROUPS, 4])
                    link(dve.tensor_tensor(r_sel[:, t].rearrange("p (g e) -> p g e", g=N_GROUPS),
                                           r_sel[:, t].rearrange("p (g e) -> p g e", g=N_GROUPS), away, ALU.add))
                    rank(r_sel[:, t], t, N_EXPERTS, r_rank[:, t])
                    link(dve.tensor_scalar(r_rank[:, t], r_rank[:, t], 1.5, None, ALU.is_lt))
                    link(dve.tensor_copy(chosen[:, t], r_rank[:, t]))
                    link(dve.tensor_tensor(r_rank[:, t], r_rank[:, t], r_s[:, t], ALU.mult))
                    link(dve.tensor_reduce(r_sum[:, t:t + 1], r_rank[:, t], AX_X, ALU.add))
                    link(dve.reciprocal(r_sum[:, t:t + 1], r_sum[:, t:t + 1]))
                    ins = dve.tensor_scalar(gates[:, t], r_rank[:, t], r_sum[:, t:t + 1], None, ALU.mult)
                    link(ins)
                link(dve.tensor_copy(gates_r[:, 0], gates[:, :, :]))
                dve.tensor_tensor(gates_r[:, 1], gates[:, :, :], gates_r[:, 0].bitcast(F32), ALU.subtract)\
                    .then_inc(gates_ready, 1)
                split(3)
                low_h()
                split()
                dve.wait_ge(x_high, seen(x_high, TT))
                for t in range(TT):
                    dve.tensor_tensor(xr[:, 1, t], x[:, t, :], xr[:, 0, t].bitcast(F32), ALU.subtract)
                dve.wait_ge(placed, l + 1)
                dve.tensor_scalar(slot_of, h_bank[0][:, 0:TT * N_EXPERTS].rearrange("p (t e) -> p t e", t=TT), ELSEWHERE,
                                  None, ALU.add).then_inc(dve_link, 1)
                link(dve.tensor_reduce(most, h_bank[0][:, TT * N_EXPERTS:(TT + 1) * N_EXPERTS], AX_X, ALU.max))
                dve.wait_ge(dve_link, seen(dve_link))
                dve.tensor_scalar(overflow[:, :], most, SLOTS + 0.5, None, ALU.is_gt).then_inc(overflow_known, 1)
                for e in range(2):
                    pick_slots(l, e, e)
                for t in range(TT):
                    if t == 0:
                        dve.wait_ge(y_half, seen(y_half))
                    else:
                        wait_units()
                    for c in range(2):
                        at = slice(c * 512, (c + 1) * 512)
                        ins = dve.tensor_tensor(ple_gate[:, t, at], y_bank[t][c][:, :], ple_gate[:, t, at], ALU.mult)
                        if c == 0:
                            link(ins)
                    ins.then_inc(tile_taken, 1)
                    dve.wait_ge(tile_taken, seen(tile_taken))
                    link(dve.scalar_tensor_tensor(out=x[:, t, :], in0=x[:, t, :], scalar=ALPHA, in1=ple_gate[:, t, :],
                                                  op0=ALU.mult, op1=ALU.add))

            def pick_slots(l, e, b):
                for t in range(TT):
                    col = slot_of[:, t, e:e + 1] if isinstance(e, int) else slot_of[:, t, bass.ds(e, 1)]
                    ins = dve.tensor_scalar(pick[:, b, t, :], slot_row, col, None, ALU.is_equal)
                ins.then_inc(slots_ready[l], 1)

            def experts(l):
                dve.wait_ge(overflow_known, l + 1)
                before, n_before = dict(seen.n), n[0]
                with dve.If(dve.value_load(overflow[0:1, 0:1], min_val=0, max_val=1) == 0):
                    gathered_experts(l)
                seen.n = dict(before)
                after, n[0] = n[0], n_before
                with dve.Else():
                    gated(moe[l])
                assert n[0] == after

            def gathered_experts(l):
                turn, z = turn_bank[0], (h_bank[1], turn_bank[1])

                def gates_by_slot(e, b):
                    col = turn[:, T + e:T + e + 1] if isinstance(e, int) else turn[:, bass.ds(e + T, 1)]
                    dve.tensor_copy(slot_gate[:, b:b + 1], col).then_inc(turn_taken[l], 1)

                def low_ye():
                    for c in range(2):
                        dve.wait_ge(ye_hi_ready[l], seen(ye_hi_ready[l]))
                        at = slice(c * 512, (c + 1) * 512)
                        dve.tensor_tensor(ye[:, 1, at], z[c][:, :], ye[:, 0, at].bitcast(F32), ALU.subtract)\
                            .then_inc(ye_lo_ready[l], 1)

                def step(e, b, s, prev=True, next_=True, after_next=True):
                    if s == 1 or prev:
                        split()
                    if s == 1 and after_next:
                        pick_slots(l, e + 2, b)
                    split()
                    dve.wait_ge(gate_ready, seen(gate_ready, TT))
                    dve.wait_ge(turn_taken[l], seen(turn_taken[l]))
                    dve.scalar_tensor_tensor(out=h[:, 0], in0=h_bank[0][:, HALF:2 * HALF], scalar=slot_gate[:, b:b + 1],
                                             in1=gate_act[:, 0], op0=ALU.mult, op1=ALU.mult).then_inc(h_ready, TT)
                    split()
                    dve.wait_ge(ht_hi_ready, seen(ht_hi_ready))
                    dve.tensor_tensor(ht_lo[:, :, 0:SLOTS], turn[:, 0:2 * SLOTS].rearrange("p (k c) -> p k c", k=2),
                                      ht_hi[:, :, 0:SLOTS].bitcast(F32), ALU.subtract).then_inc(ht_lo_ready, 1)
                    if s == 0:
                        dve.tensor_copy(pick_t[:, b, :], turn[:, T:2 * T]).then_inc(turn_taken[l], 1)
                        if prev:
                            low_ye()
                    elif next_:
                        gates_by_slot(e + 1, 1 - b)

                dve.wait_ge(first_gates[l], 1)
                gates_by_slot(0, 0)
                for s in range(2):
                    step(0, 0, s, prev=False)
                for s in range(2):
                    step(1, 1, s)
                with seen.loop(SLOT_ROUNDS, [(hi_ready, 12), (gate_ready, 4 * TT), (ht_hi_ready, 4), (turn_taken[l], 4),
                                             (ye_hi_ready[l], 4)]) as i:
                    for b in range(2):
                        for s in range(2):
                            step(2 * i + (2 + b), b, s)
                n[0] += 12 * (SLOT_ROUNDS - 1)
                for s in range(2):
                    step(14, 0, s, after_next=False)
                for s in range(2):
                    step(15, 1, s, next_=False, after_next=False)
                low_ye()
                if l < DEPTH - 1:
                    split()

            split(AHEAD)
            for t in range(TT):
                low_xt(t)
            for l in range(DEPTH):
                gated(ff[l][0], aside=make_tables if l == 0 else None)
                norm(3 * l, 2 * ALPHA, x_ready)
                hybrid(l)
                norm(3 * l + 1, ALPHA, x_ready)
                gated(ff[l][1], aside=s5_parameters if l == DEPTH - 1 else None)
                norm(3 * l + 2, 2 * ALPHA, x_ready)
            for l in range(DEPTH):
                (s5_and_pool, stick_breaking)[l]()
                norm(6 + 2 * l, ALPHA, x_ready)
                before_experts(l)
                experts(l)
                if l < DEPTH - 1:
                    norm(7 + 2 * l, 1.0, x_ready)
                else:
                    norm(7 + 2 * l, 1.0, x_final, split_ahead=1)


def lambda_init(l):
    return 0.8 - 0.6 * math.exp(-0.3 * l)


def constants():
    c = np.zeros((P, C_END), np.float32)
    c[:, C_FREQ:C_FREQ + 32] = np.power(np.float32(10000.0), -np.arange(0, HD, 2, dtype=np.float32) / np.float32(HD))
    c[:, C_TIME:C_TIME + T] = np.arange(T)
    for g in range(2):
        c[:, C_PAR + g] = (np.arange(P) // H5) % 2 == g
    return c


def window_matrices():
    token, time = np.arange(T)[:, None], np.arange(T)[None, :]
    m = [((token <= time) & (token > time - w)) / np.minimum(time + 1, w).astype(np.float32) - (token == time)
         for w in POOL_WINDOWS]
    return np.stack(m).astype(np.float32).reshape(len(POOL_WINDOWS), TT, P, T).transpose(2, 0, 1, 3)


_NAMES = ["x", "positions", "w_in", "w_out", "diff_lambda", "diff_subln_g", "swa_sink", "ffn1_w_in", "ffn1_w_out",
          "ffn2_w_in", "ffn2_w_out", "ln_g", "ln_b", "p_2", "ab_w_in_2", "s5_lambda_re_2", "s5_lambda_im_2",
          "s5_log_dt_2", "s5_b_re_2", "s5_b_im_2", "s5_c_re_2", "s5_c_im_2", "s5_d_2", "s5_w_glu_2", "pool_w_2",
          "pool_scale_2", "ab_w_out_2", "sb_w_qkv_2", "sb_w_out_2", "ln_mix_g_2", "ln_mix_b_2", "ln_ffn_g_2",
          "ln_ffn_b_2", "router_w_2", "router_bias_2", "moe_w1_2", "moe_w3_2", "moe_w2_2", "ple_w_proj_2",
          "ple_w_gate_2"]


def kernel(**inputs):
    import concourse.bacc as bacc
    from concourse.bass_utils import run_bass_kernel_spmd

    nc = bacc.Bacc("TRN2", target_bir_lowering=False, num_devices=1)
    inputs = {**inputs, "constants": constants(), "window_matrices": window_matrices()}
    arrays, aps = {}, {}
    for name in _NAMES + ["constants", "window_matrices"]:
        arrays[name] = np.ascontiguousarray(inputs[name])
        aps[name] = nc.dram_tensor(name, arrays[name].shape, mybir.dt.from_np(arrays[name].dtype), kind="ExternalInput").ap()
    out = nc.dram_tensor("out", (1, T, D), F32, kind="ExternalOutput").ap()
    program(nc, aps, out)
    r = run_bass_kernel_spmd(nc, [arrays], core_ids=[0])
    return r.results[0]["out"]
```

```python
import math
from contextlib import ExitStack, contextmanager

import numpy as np
import concourse.bass as bass
from concourse import mybir

ALU = mybir.AluOpType
ACT = mybir.ActivationFunctionType
F32 = mybir.dt.float32
F32R = mybir.dt.float32r
I32 = mybir.dt.int32
AX_X = mybir.AxisListType.X

P = 128
T = 256
TT = T // P
D = 1024
KD = D // P
DEPTH = 2
D_FF = ((8 * D // 3 + 127) // 128) * 128
HALF = 256
FF_STEPS = D_FF // HALF
UNIT = 2048
RAW = 6
SPLIT = 3
AHEAD = 2
ALPHA = (2.0 * DEPTH) ** 0.25
LN_EPS = 1e-5
RMS_EPS = 1e-5
HD = 64
SCALE = HD ** -0.5
FAR = -1e30
DIFF_HEADS = 4
SWA_Q = 8
WINDOW = 128
N_EXPERTS = 16
D_EXPERT = 512
EXPERT_STEPS = D_EXPERT // HALF
MOE_STEPS = N_EXPERTS * EXPERT_STEPS
N_GROUPS = 4
FF_UNITS = 3 * FF_STEPS
HYBRID_UNITS = 13
S5_UNITS = 9
STICK_UNITS = 16
PLE_UNITS = 5
MOE_UNITS = 3 * MOE_STEPS
SLOT_ROUNDS = (N_EXPERTS - 8) // 4
PLE = 256
G5, P5, H5 = 32, 64, 16
S5_TILES = G5 * P5 // P
POOL_WINDOWS = (2, 4, 8, 16)
SLOTS = P
ELSEWHERE = 4096.0
TWO_PI = 2.0 * math.pi
PI_IN = 3.1415925
ROUND = 1.5 * 2.0 ** 23
TP_HI = 6.28125
TP_MID = math.floor((TWO_PI - TP_HI) * 2.0 ** 21) / 2.0 ** 21
TP_LO = TWO_PI - TP_HI - TP_MID
GELU_C = 2.0 * math.sqrt(2.0 / math.pi)

WORK_AT = 171968

C_FREQ, C_TIME, C_PAR, C_END = 0, 32, 288, 290


class Tally:

    def __init__(self, engine):
        self.engine, self.n, self.term = engine, {}, {}

    def __call__(self, sem, k=1):
        self.n[id(sem)] = self.n.get(id(sem), 0) + k
        return self.n[id(sem)] + self.term.get(id(sem), 0)

    def ahead(self, sem, k):
        return self.n.get(id(sem), 0) + k + self.term.get(id(sem), 0)

    @contextmanager
    def loop(self, rounds, per_round):
        start = {id(s): self.n.get(id(s), 0) for s, _ in per_round}
        before = dict(self.n)
        with self.engine.Fori(0, rounds) as i:
            self.term = {id(s): i * k for s, k in per_round}
            yield i
        for s, k in per_round:
            assert self.n.get(id(s), 0) - start[id(s)] == k, (s, k, self.n.get(id(s), 0) - start[id(s)])
            self.n[id(s)] = start[id(s)] + rounds * k
        for key, n in self.n.items():
            assert key in start or n == before.get(key), "a semaphore waited for, but not named"
        self.term = {}


class Gated:

    def __init__(self, gate, up, down, steps, peeled):
        self.gate_v, self.up_v, self.down_v, self.steps, self.peeled = gate, up, down, steps, peeled
        self.rounds = (steps - 1 - peeled) // 2
        assert peeled + 1 + 2 * self.rounds == steps


class FeedForward(Gated):
    def __init__(self, w_in, w_out):
        v = w_in.rearrange("(u k p) (g j c) -> g u j p k c", p=P, u=2, g=2, c=HALF)
        super().__init__(v[0], v[1], w_out.rearrange("(j k p) c -> j p k c", p=P, k=2), FF_STEPS, 2)
        self.experts = False

    def gate_up(self, i, j, u):
        at = 2 * i + j
        if isinstance(at, int):
            return self.gate_v[u, at], self.up_v[u, at]
        return (self.gate_v[u, bass.ds(at, 1)].rearrange("o p k c -> (o p) k c"),
                self.up_v[u, bass.ds(at, 1)].rearrange("o p k c -> (o p) k c"))

    def down(self, i, j):
        at = 2 * i + j
        if isinstance(at, int):
            return self.down_v[at]
        return self.down_v[bass.ds(at, 1)].rearrange("o p k c -> (o p) k c")


class Experts(Gated):
    def __init__(self, w1, w3, w2):
        ins = [w.rearrange("e (u k p) (j c) -> u j e p k c", p=P, u=2, c=HALF) for w in (w1, w3)]
        super().__init__(*ins, w2.rearrange("e (j k p) c -> j e p k c", p=P, k=2), MOE_STEPS, 1)
        self.experts = True

    def pick(self, v, i, j):
        e, half = i + j // EXPERT_STEPS, j % EXPERT_STEPS
        if isinstance(e, int):
            return v[half, e]
        return v[half, bass.ds(e, 1)].rearrange("o p k c -> (o p) k c")

    def gate_up(self, i, j, u):
        return self.pick(self.gate_v[u], i, j), self.pick(self.up_v[u], i, j)

    def down(self, i, j):
        return self.pick(self.down_v, i, j)


def program(nc, a, out):
    with ExitStack() as ctx:
        def sb(name, shape, dt=F32):
            return ctx.enter_context(nc.sbuf_tensor(name, shape, dt))

        def bank(name):
            return ctx.enter_context(nc.psum_tensor(name, [P, 512], F32))

        def sem(name):
            return ctx.enter_context(nc.semaphore(name))

        raw = [sb(f"raw{i}", [P, UNIT]) for i in range(RAW)]
        hi = [sb(f"w_hi{i}", [P, UNIT], F32R) for i in range(SPLIT)]
        lo = [sb(f"w_lo{i}", [P, UNIT], F32R) for i in range(SPLIT)]
        x = sb("x_rows", [P, TT, D])
        xt_hi = sb("xt_hi", [P, KD, T], F32R)
        xt_lo = sb("xt_lo", [P, KD, T], F32R)
        gate_act = sb("gate_act", [P, TT, HALF])
        h = sb("h", [P, TT, HALF])
        ht_hi = sb("ht_hi", [P, 2, T], F32R)
        ht_lo = sb("ht_lo", [P, 2, T], F32R)
        ln_gb = sb("ln_gb", [P, 2, D])
        ident = sb("ident", [P, P])
        stats = sb("stats", [P, TT, 2, 6])
        moments = sb("moments", [P, TT, 2])
        rstd = sb("rstd", [P, TT, 1])
        minus_half = sb("minus_half", [P, 4])
        cst = sb("cst", [P, C_END])
        rope = sb("rope", [P, 2, TT, HD])
        swa_mask = sb("swa_mask", [P, TT, T])
        causal = sb("causal", [P, T])
        gates = sb("gates", [P, TT, N_EXPERTS])
        small = sb("small", [P, 384])
        params = sb("params", [P, 984])
        pool_w = sb("pool_w", [P, 4, P])
        rw_hi = sb("rw_hi", [P, KD, N_EXPERTS], F32R)
        rw_lo = sb("rw_lo", [P, KD, N_EXPERTS], F32R)
        before = sb("before", [P, N_EXPERTS, N_EXPERTS])
        half_pi = sb("half_pi", [P, 1])
        position = sb("position", [P, TT], I32)
        work = nc.alloc_sbuf_tensor_at("work", [P, 14336], F32, offset=WORK_AT)
        slot_mem = nc.alloc_sbuf_tensor_at("slot_mem", [P, 12256], F32R, offset=WORK_AT)
        overflow = sb("overflow", [P, 1], I32)

        y_bank = [[bank(f"y{t}{c}") for c in range(2)] for t in range(TT)]
        h_bank = [bank(f"h{t}") for t in range(TT)]
        turn_bank = [bank(f"turn{t}") for t in range(TT)]

        unit_loaded = [sem(f"unit_loaded{i}") for i in range(RAW)]
        hi_ready = sem("hi_ready")
        lo_ready = sem("lo_ready")
        unit_used = sem("unit_used")
        const_loaded = sem("const_loaded")
        const_made = sem("const_made")
        gb_loaded = sem("gb_loaded")
        x_loaded = sem("x_loaded")
        first_half = sem("first_half")
        y_half = sem("y_half")
        gate_ready = sem("gate_ready")
        h_ready = sem("h_ready")
        h_turned = sem("h_turned")
        ht_hi_ready = sem("ht_hi_ready")
        ht_lo_ready = sem("ht_lo_ready")
        var_ready = sem("var_ready")
        rstd_ready = sem("rstd_ready")
        x_ready = sem("x_ready")
        x_turned = sem("x_turned")
        xt_hi_ready = sem("xt_hi_ready")
        xt_lo_ready = sem("xt_lo_ready")
        tile_taken = sem("tile_taken")
        dve_link = sem("dve_link")
        act_link = sem("act_link")
        pool_link = sem("pool_link")
        angles = sem("angles")
        sines = sem("sines")
        x_final = sem("x_final")
        stored = sem("stored")
        lam_sums = sem("lam_sums")
        lam_exps = sem("lam_exps")
        row_ready = sem("row_ready")
        row_turned = sem("row_turned")
        col_ready = sem("col_ready")
        scores_ready = sem("scores_ready")
        neg_ready = sem("neg_ready")
        exp_ready = sem("exp_ready")
        prob_ready = sem("prob_ready")
        prob_turned = sem("prob_turned")
        pt_ready = sem("pt_ready")
        pv_done = sem("pv_done")
        swa_out = sem("swa_out")
        squares = sem("squares")
        sub_rstd = sem("sub_rstd")
        mix_ready = sem("mix_ready")
        zeroed = sem("zeroed")
        zm_ready = sem("zm_ready")
        sp_ready = sem("sp_ready")
        arg_ready = sem("arg_ready")
        w_ready = sem("w_ready")
        s5_loaded = sem("s5_loaded")
        s5_act = sem("s5_act")
        s5_dve = sem("s5_dve")
        wide_ready = sem("wide_ready")
        wide_turned = sem("wide_turned")
        wide_copied = sem("wide_copied")
        turns_ready = sem("turns_ready")
        trig_ready = sem("trig_ready")
        bu_ready = sem("bu_ready")
        scan_ready = sem("scan_ready")
        st_ready = sem("st_ready")
        y_part = sem("y_part")
        pooled = sem("pooled")
        pooled_ready = sem("pooled_ready")
        glu_half = sem("glu_half")
        pool_mixed = sem("pool_mixed")
        rw_hi_ready = sem("rw_hi_ready")
        rw_lo_ready = sem("rw_lo_ready")
        routed = sem("routed")
        route_sig = sem("route_sig")
        gates_ready = sem("gates_ready")
        p_loaded = sem("p_loaded")
        ple_sig = sem("ple_sig")

        placed = sem("placed")
        overflow_known = sem("overflow_known")
        x_high = sem("x_high")
        all_half = [sem(f"all_half{l}") for l in range(DEPTH)]
        slots_ready = [sem(f"slots_ready{l}") for l in range(DEPTH)]
        gathered = [sem(f"gathered{l}") for l in range(DEPTH)]
        xe_ready = [sem(f"xe_ready{l}") for l in range(DEPTH)]
        first_gates = [sem(f"first_gates{l}") for l in range(DEPTH)]
        turn_taken = [sem(f"turn_taken{l}") for l in range(DEPTH)]
        last_out = [sem(f"last_out{l}") for l in range(DEPTH)]
        ye_hi_ready = [sem(f"ye_hi_ready{l}") for l in range(DEPTH)]
        ye_lo_ready = [sem(f"ye_lo_ready{l}") for l in range(DEPTH)]

        block = ctx.enter_context(nc.Block())

        ff = [[FeedForward(a["ffn1_w_in"][l], a["ffn1_w_out"][l]), FeedForward(a["ffn2_w_in"][l], a["ffn2_w_out"][l])]
              for l in range(DEPTH)]
        moe = [Experts(a["moe_w1_2"][l], a["moe_w3_2"][l], a["moe_w2_2"][l]) for l in range(DEPTH)]

        def by_rows(w, rows, c0, c1):
            return w[rows[0] * P:rows[1] * P, c0:c1].rearrange("(k p) c -> p k c", p=P)

        @block.sync
        def _(sp):
            seen = Tally(sp)
            n = [0]

            def load(*pieces):
                s = n[0] % RAW
                if n[0] >= RAW:
                    sp.wait_ge(lo_ready, seen(lo_ready))
                k = pieces[0].shape[1]
                dst = raw[s][:, :].rearrange("p (k c) -> p k c", k=k)
                c = UNIT // k // len(pieces)
                for q, src in enumerate(pieces):
                    sp.dma_start(dst[:, :, q * c:(q + 1) * c], src).then_inc(unit_loaded[s], 32 // len(pieces))
                n[0] += 1

            def load_gated(w):
                def step(i, j):
                    load(*w.gate_up(i, j, 0))
                    load(*w.gate_up(i, j, 1))
                    if not isinstance(i, int) or j > 0:
                        load(w.down(i, j - 1))
                for j in range(w.peeled + 1):
                    step(0, j)
                with seen.loop(w.rounds, [(lo_ready, 6)]) as i:
                    step(i, w.peeled + 1)
                    step(i, w.peeled + 2)
                n[0] += 6 * (w.rounds - 1)
                load(w.down(0, w.steps - 1))

            def load_matrix(w, cols, c0=0):
                for c in range(c0, c0 + cols, 512):
                    for u in range(2):
                        load(by_rows(w, (4 * u, 4 * u + 4), c, c + 512))

            for l in range(DEPTH):
                load_gated(ff[l][0])
                load_matrix(a["w_in"][l], 1024)
                load_matrix(a["w_in"][l], 512, 1536)
                load(by_rows(a["w_in"][l], (0, 8), 2048, 2304))
                load_matrix(a["w_in"][l], 512, 1024)
                load_matrix(a["w_out"][l], 1024)
                load_gated(ff[l][1])
            load_matrix(a["ab_w_in_2"][0], 1024)
            load(by_rows(a["s5_w_glu_2"][0], (0, 4), 0, 512))
            load_matrix(a["ab_w_out_2"][0], 1024)
            load_matrix(a["ple_w_gate_2"][0], 1024)
            load(by_rows(a["ple_w_proj_2"][0], (0, 2), 0, 1024))
            load_gated(moe[0])
            load_matrix(a["sb_w_qkv_2"][0], 3072)
            load_matrix(a["sb_w_out_2"][0], 1024)
            load_matrix(a["ple_w_gate_2"][1], 1024)
            load(by_rows(a["ple_w_proj_2"][1], (0, 2), 0, 1024))
            load_gated(moe[1])
            s = n[0] % RAW
            sp.wait_ge(lo_ready, seen(lo_ready))
            sp.dma_start(raw[s][:, 0:P], a["p_2"][0, 0, 0:P, 0:P]).then_inc(unit_loaded[s], 32)
            for t in range(TT):
                sp.wait_ge(x_final, 2 * (t + 1))
                sp.dma_start(out[0].rearrange("(t p) d -> p t d", p=P)[:, t], x[:, t, :]).then_inc(stored, 16)
            sp.wait_ge(stored, 16 * TT)

        def carve(tensor, at, *dims):
            n = int(np.prod(dims))
            v = tensor[:, at:at + n]
            if len(dims) == 1:
                return v
            names = "abcd"[:len(dims)]
            return v.rearrange(f"p ({' '.join(names)}) -> p {' '.join(names)}",
                               **{k: d for k, d in zip(names[1:], dims[1:])})

        freq, time_row = cst[:, C_FREQ:C_FREQ + 32], cst[:, C_TIME:C_TIME + T]
        parity = cst[:, C_PAR:C_PAR + 2]

        qk = carve(work, 0, TT, 1792)
        qz1 = carve(work, 3584, 8, 2, T)
        kt1 = carve(work, 7680, 6, T)
        v1 = carve(work, 9216, TT, 640)
        rot = carve(work, 10496, 2, 512)
        e1 = carve(work, 11520, 2, 2, T)
        p1 = carve(work, 12544, 2, 2, T)
        pt1 = carve(work, 2048, 2, 512)
        mix = carve(work, 0, TT, D)
        qz2 = carve(work, 0, 8, 2, T)
        kt2 = carve(work, 4096, 8, T)
        v2 = carve(work, 6144, TT, D)
        qk_row = carve(work, 8192, 2, TT, 512)
        zm = carve(work, 8192, 2, 2, T)
        sp_ = carve(work, 9216, 2, 2, T)
        soft = carve(work, 10240, 2, 2, T)
        w2 = carve(work, 11264, 2, 2, T)
        wt2 = carve(work, 12288, 2, 512)
        ab_row = carve(work, 2048, TT, D)
        ab_t = carve(work, 0, 8, T)
        bb_t = carve(work, 4096, 2, 4, P)
        c_t = carve(work, 5120, 2, 4, P)
        trig = [carve(work, at, 2, 4, T) for at in (6144, 2048)]
        pool_mat = carve(work, 12288, 4, TT, T)
        th = carve(work, 8192, 2, 4, T)
        m5 = carve(work, 10240, 2, 2, T)
        s5 = carve(work, 11264, 2, 2, T)
        n5 = [carve(work, 12288 + 1024 * b, 2, 2, T) for b in range(2)]
        minus_c = carve(gate_act[:, :, :].rearrange("p t c -> p (t c)"), 0, 4, P)
        b_nat = carve(work, 8192, 2, 16, 16)
        bb_wide = carve(work, 8704, 2, 16, 32)
        c_nat = carve(work, 9728, 2, 4, P5)
        c_wide = carve(work, 10240, 2, 4, P)
        bb_tmp = carve(work, 11264, 2, 16, 16)
        y5 = carve(work, 4 * T, 4, T)
        g1 = rope[:, :, :, :].rearrange("p a t d -> p (a t d)")
        g5 = carve(work, 9344, 4, T)

        lam_in = carve(params, 0, DEPTH, 4, HD)
        sub_g = carve(params, 512, DEPTH, P)
        sink = carve(params, 768, DEPTH, SWA_Q)
        router_w = carve(params, 784, KD, N_EXPERTS)
        router_b = carve(params, 912, N_EXPERTS)
        lam_re, lam_im, log_dt = (carve(params, 928 + 16 * i, S5_TILES) for i in range(3))
        pool_scale = carve(params, 976, 4)
        d_skip = carve(params, 980, 4)
        N_LOADS = 14
        lam = carve(small, 0, DEPTH)
        lam_e = carve(small, 2, DEPTH, 2)
        neg = carve(small, 8, 2, 2)
        sums = carve(small, 12, 2, 2)
        sink_e = carve(small, 16, 2, 2)
        inv = carve(small, 20, 2, 2)
        nmax = carve(small, 24, 2, 2)
        ssq = carve(small, 28, TT, DIFF_HEADS)
        srs = carve(small, 36, TT, DIFF_HEADS)
        neg_sink = carve(small, 44, DEPTH, SWA_Q)
        s5v = [carve(small, 64 + 16 * i, 16) for i in range(20)]
        (dt5, ang5, mag5, k5, r5, sin5, cos5, phi5, abs5, lbr, lbi, den, fre, fim, tmpa, tmpb) = s5v[:16]

        ple_gate = carve(work, 0, TT, D)
        r_s = carve(work, 12288, TT, N_EXPERTS)
        r_sel = carve(work, 12320, TT, N_EXPERTS)
        r_two = carve(work, 12352, 8, TT * N_GROUPS)
        r_grp = carve(work, 12416, TT, N_GROUPS)
        r_rank = carve(work, 12424, TT, N_EXPERTS)
        r_sum = carve(work, 12456, TT)
        r_gt = carve(work, 12544, N_EXPERTS, N_EXPERTS)
        r_eq = carve(work, 12800, N_EXPERTS, N_EXPERTS)

        ye = carve(slot_mem, 0, 2, D)
        xr = carve(slot_mem, 2048, 2, TT, D)
        xe = [[carve(slot_mem, 6144 + 2048 * part, KD, 2 * SLOTS) for part in range(2)], [xt_hi, xt_lo]]
        pick = carve(slot_mem, 10240, 2, TT, 2 * SLOTS)
        pick_t = carve(slot_mem, 11264, 2, T)
        tri = carve(slot_mem, 11776, 2, P)
        ident_r = carve(slot_mem, 12032, P)
        chosen = carve(slot_mem, 12160, TT, N_EXPERTS)
        gates_r = carve(slot_mem, 12192, 2, TT, N_EXPERTS)
        tri_ones = swa_mask[:, 0, :]
        slot_of = carve(small, 64, TT, N_EXPERTS)
        slot_gate = carve(small, 96, 2)
        most = carve(small, 98, 1)
        slot_row = time_row[:, 0:SLOTS]

        @block.gpsimd
        def _(pool):
            seen = Tally(pool)

            def link(ins):
                ins.then_inc(pool_link, 1)
                pool.wait_ge(pool_link, seen(pool_link))

            def load(dst, src, to=const_loaded):
                pool.dma_start(dst, src, allow_slow_non_contiguous=True).then_inc(to, 16)

            def load_ln(g, b):
                load(ln_gb[:, 0, :], g.partition_broadcast(P), gb_loaded)
                load(ln_gb[:, 1, :], b.partition_broadcast(P), gb_loaded)

            load(x[:, :, :], a["x"][0].rearrange("(t p) d -> p t d", p=P), x_loaded)
            pool.memset(ident[:, :], 0.0).then_inc(pool_link, 1)
            pool.wait_ge(pool_link, seen(pool_link))
            pool.affine_select(out=ident[:, :], in_=ident[:, :], compare_op=ALU.not_equal, fill=1.0, base=0,
                               pattern=[[-1, P]], channel_multiplier=1).then_inc(const_made, 1)
            load_ln(a["ln_g"][0, 0], a["ln_b"][0, 0])
            load(cst[:, :], a["constants"])
            load(position[:, :], a["positions"][0].rearrange("(t p) -> p t", p=P))
            load(lam_in, a["diff_lambda"].partition_broadcast(P))
            load(sub_g, a["diff_subln_g"].partition_broadcast(P))
            load(sink, a["swa_sink"].partition_broadcast(P))
            load(router_w, a["router_w_2"].rearrange("(k p) e -> p k e", p=P))
            load(router_b, a["router_bias_2"].partition_broadcast(P))
            load(lam_re, a["s5_lambda_re_2"][0].rearrange("(i g) p -> (g p) i", g=2))
            load(lam_im, a["s5_lambda_im_2"][0].rearrange("(i g) p -> (g p) i", g=2))
            for g in range(2):
                load(log_dt[P5 * g:P5 * g + P5, :],
                     a["s5_log_dt_2"][0].rearrange("(i g) -> g i", g=2)[g].partition_broadcast(P5))
            load(pool_scale, a["pool_scale_2"][0].rearrange("(g d) -> d g", d=P))
            load(d_skip, a["s5_d_2"][0].rearrange("(c g) h -> (g h) c", c=4))
            load(pool_w[:, :, :], a["pool_w_2"][0].rearrange("g c d -> c g d"))
            pool.memset(minus_half[:, :], -0.5).then_inc(const_made, 1)
            pool.memset(half_pi[:, :], math.pi / 2).then_inc(const_made, 1)
            pool.memset(swa_mask[:, :, :], 0.0).then_inc(pool_link, 1)
            pool.memset(causal[:, :], 0.0).then_inc(pool_link, 1)
            pool.memset(before[:, :, :], 1.0).then_inc(pool_link, 1)
            pool.wait_ge(pool_link, seen(pool_link, 3))
            pool.affine_select(out=swa_mask[:, 0, :], in_=swa_mask[:, 0, :], compare_op=ALU.is_ge, fill=FAR,
                               base=WINDOW, pattern=[[-1, T]], channel_multiplier=1).then_inc(const_made, 1)
            pool.affine_select(out=swa_mask[:, 1, :], in_=swa_mask[:, 1, :], compare_op=ALU.is_ge, fill=FAR,
                               base=WINDOW - P, pattern=[[1, T]], channel_multiplier=-1).then_inc(const_made, 1)
            pool.affine_select(out=causal[:, P:T], in_=causal[:, P:T], compare_op=ALU.is_gt, fill=FAR, base=0,
                               pattern=[[-1, P]], channel_multiplier=1).then_inc(const_made, 1)
            pool.affine_select(out=before[:, :, :], in_=before[:, :, :], compare_op=ALU.is_gt, fill=0.0, base=0,
                               pattern=[[1, N_EXPERTS], [-1, N_EXPERTS]], channel_multiplier=0).then_inc(const_made, 1)

            pool.memset(qz1, 0.0).then_inc(zeroed, 1)

            used = [0]

            def split_low(units):
                used[0] += units
                n = used[0] + 1
                s, r = n % SPLIT, n % RAW
                pool.wait_ge(hi_ready, n + 1)
                pool.wait_ge(lo_ready, n)
                pool.tensor_tensor(lo[s][:, :], raw[r][:, :], hi[s][:, :].bitcast(F32), ALU.subtract)\
                    .then_inc(lo_ready, 1)

            def ln_rstd(eps, units=None):
                if units is not None:
                    split_low(units)
                pool.wait_ge(const_made, 7)
                for t in range(TT):
                    pool.wait_ge(var_ready, seen(var_ready))
                    link(pool.tensor_scalar(rstd[:, t], moments[:, t, 1:2], eps, None, ALU.add))
                    pool.tensor_tensor(rstd[:, t], rstd[:, t], minus_half[:, 0:1], ALU.pow).then_inc(rstd_ready, 1)

            def next_ln(g, b):
                pool.wait_ge(x_ready, seen(x_ready, 2 * TT))
                load_ln(g, b)

            for l in range(DEPTH):
                ln_rstd(4 * LN_EPS, FF_UNITS)
                next_ln(a["ln_g"][l, 1], a["ln_b"][l, 1])
                pool.wait_ge(squares, seen(squares, TT))
                link(pool.tensor_scalar(srs, ssq, 1.0 / P, RMS_EPS, ALU.mult, ALU.add))
                pool.tensor_tensor(srs, srs, minus_half[:, 0:1].broadcast_to([P, TT, DIFF_HEADS]), ALU.pow)\
                    .then_inc(sub_rstd, 1)
                ln_rstd(LN_EPS, HYBRID_UNITS)
                next_ln(a["ln_g"][l, 2], a["ln_b"][l, 2])
                if l == DEPTH - 1:
                    link(pool.memset(tri_ones, 1.0))
                    link(pool.affine_select(out=tri_ones[:, 0:P], in_=tri_ones[:, 0:P], compare_op=ALU.is_ge, fill=0.0,
                                            base=0, pattern=[[1, P]], channel_multiplier=-1))
                    pool.affine_select(out=tri_ones[:, 0:P], in_=tri_ones[:, 0:P], compare_op=ALU.not_equal,
                                       fill=-ELSEWHERE, base=0, pattern=[[-1, P]], channel_multiplier=1)\
                        .then_inc(const_made, 1)
                    for i, n in enumerate(("re", "im")):
                        load(b_nat[:, i], a[f"s5_b_{n}_2"][0].rearrange("(i g) p h -> (g p) i h", g=2), s5_loaded)
                        load(c_nat[:, i], a[f"s5_c_{n}_2"][0].rearrange("(c g) h p -> (g h) c p", c=4), s5_loaded)
                    load(pool_mat, a["window_matrices"], s5_loaded)
                ln_rstd(4 * LN_EPS, FF_UNITS)
                if l < DEPTH - 1:
                    next_ln(a["ln_g"][l + 1, 0], a["ln_b"][l + 1, 0])
                    pool.memset(qz1, 0.0).then_inc(zeroed, 1)
                else:
                    next_ln(a["ln_mix_g_2"][0], a["ln_mix_b_2"][0])

            def load_p(l):
                load(h[:, :, :], a["p_2"][l, 0].rearrange("(t p) c -> p t c", p=P), p_loaded)

            load_p(0)
            for i in range(S5_TILES):
                q, b = i % 4, i % 2
                pool.wait_ge(scan_ready, seen(scan_ready))
                if i >= 2:
                    pool.wait_ge(y_part, seen(y_part))
                for j in range(2):
                    pool.tensor_tensor(n5[b][:, j], s5[:, b], trig[i // 4 % 2][:, j, q:q + 1, :].broadcast_to([P, 2, T]),
                                       ALU.mult).then_inc(st_ready, 1)

            ln_rstd(LN_EPS, S5_UNITS)
            next_ln(a["ln_ffn_g_2"][0], a["ln_ffn_b_2"][0])
            ln_rstd(LN_EPS, PLE_UNITS + MOE_UNITS)
            next_ln(a["ln_mix_g_2"][1], a["ln_mix_b_2"][1])
            pool.memset(qz2, 0.0).then_inc(zeroed, 1)
            load_p(1)
            ln_rstd(LN_EPS, STICK_UNITS)
            next_ln(a["ln_ffn_g_2"][1], a["ln_ffn_b_2"][1])
            ln_rstd(LN_EPS)
            pool.wait_ge(gb_loaded, 2 * 16 * 10)

        def mm3(pe, dst, left, right, start, stop):
            pe.matmul(dst, left[0], right[0], start=start, stop=False)
            pe.matmul(dst, left[0], right[1], start=False, stop=False)
            return pe.matmul(dst, left[1], right[0], start=False, stop=stop)

        @block.tensor
        def _(pe):
            seen = Tally(pe)
            n = [0]

            def unit(k):
                s = n[0] % SPLIT
                n[0] += 1
                pe.wait_ge(lo_ready, seen(lo_ready))
                return [w[s][:, :].rearrange("p (k c) -> p k c", k=k) for w in (hi, lo)]

            def xt_part(k, t):
                return xt_hi[:, k, t * P:(t + 1) * P], xt_lo[:, k, t * P:(t + 1) * P]

            def tile(banks, parts=2, half=None, late=None):
                if late is not None:
                    w = []
                    for t in range(TT):
                        if t == 1:
                            pe.wait_ge(xt_lo_ready, seen(xt_lo_ready, 2))
                        for u in range(2):
                            if t == 0 and u == 1:
                                late()
                            if t == 0:
                                w.append(unit(4))
                            for k in range(4):
                                mm = mm3(pe, banks[t][:, :], xt_part(4 * u + k, t), (w[u][0][:, k], w[u][1][:, k]),
                                         u == 0 and k == 0, u == 1 and k == 3)
                            if t == 1:
                                mm.then_inc(unit_used, 1)
                        if t == 0 and half is not None:
                            mm.then_inc(half, 1)
                    return
                for u in range(parts):
                    w = unit(KD // parts)
                    width = UNIT // (KD // parts)
                    for t in range(TT):
                        for k in range(KD // parts):
                            mm = mm3(pe, banks[t][:, 0:width], xt_part(u * (KD // parts) + k, t), (w[0][:, k], w[1][:, k]),
                                     u == 0 and k == 0, u == parts - 1 and k == KD // parts - 1)
                        if t == 0 and u == parts - 1 and half is not None:
                            mm.then_inc(half, 1)
                    mm.then_inc(unit_used, 1)

            def matrix(late=None):
                tile([y_bank[t][0] for t in range(TT)], half=y_half, late=late)
                tile([y_bank[t][1] for t in range(TT)], half=y_half)

            def turn_h(p=False):
                if p:
                    pe.wait_ge(p_loaded, seen(p_loaded, 16))
                else:
                    pe.wait_ge(h_ready, seen(h_ready, TT))
                for k in range(2):
                    for t in range(TT):
                        mm = pe.transpose(turn_bank[0][:, k * T + t * P:k * T + (t + 1) * P], h[:, t, k * P:(k + 1) * P],
                                          ident[:, :])
                mm.then_inc(h_turned, 1)

            def down(first, last):
                w = unit(2)
                pe.wait_ge(ht_lo_ready, seen(ht_lo_ready))
                for t in range(TT):
                    for c in range(2):
                        for k in range(2):
                            left = ht_hi[:, k, t * P:(t + 1) * P], ht_lo[:, k, t * P:(t + 1) * P]
                            right = [v[:, k, c * 512:(c + 1) * 512] for v in w]
                            mm = mm3(pe, y_bank[t][c][:, :], left, right, first and k == 0, last and k == 1)
                        if t == 0 and last:
                            mm.then_inc(y_half, 1)
                mm.then_inc(unit_used, 1)

            def gated(w, half=first_half, late=None):
                def step(j):
                    tile(h_bank, half=half, late=late if j == 0 else None)
                    if j > 0:
                        down(j == 1, False)
                    turn_h()
                for j in range(w.peeled + 1):
                    step(j)
                with seen.loop(w.rounds, [(lo_ready, 6), (h_ready, 2 * TT), (ht_lo_ready, 2)]):
                    step(w.peeled + 1)
                    step(w.peeled + 2)
                n[0] += 6 * (w.rounds - 1)
                down(False, True)

            def turn_to_xt(src, ready, also=None):
                def turn(t):
                    if also is not None:
                        pe.wait_ge(also, seen(also))
                    for b in range(2):
                        if ready is x_ready or ready is not None and b == 0:
                            pe.wait_ge(ready, seen(ready))
                        for k in range(4):
                            mm = pe.transpose(turn_bank[b][:, k * P:(k + 1) * P],
                                              src[:, t, (4 * b + k) * P:(4 * b + k + 1) * P], ident[:, :])
                        mm.then_inc(x_turned, 1)
                turn(0)
                pe.wait_ge(xt_lo_ready, seen(xt_lo_ready, 2))
                return lambda: turn(1)

            def turn_rows(get, pairs, b0=0):
                for r in range(pairs):
                    b = (b0 + r) % 2
                    if r >= 2:
                        pe.wait_ge(col_ready, seen(col_ready))
                    for m in range(2):
                        for t in range(TT):
                            mm = pe.transpose(turn_bank[b][:, m * T + t * P:m * T + (t + 1) * P], get(2 * r + m, t),
                                              ident[:, :])
                    mm.then_inc(row_turned, 1)
                pe.wait_ge(col_ready, seen(col_ready, min(2, pairs)))

            def items(count, lag, scores, turn, pv):
                for i in range(count + lag + 1):
                    if i < count:
                        scores(i)
                    if lag <= i < count + lag:
                        turn(i - lag)
                    if i >= lag + 1:
                        pv(i - lag - 1)

            def hybrid(l, late):
                for j in range(5):
                    if j >= 2:
                        pe.wait_ge(tile_taken, seen(tile_taken, TT))
                    tile([y_bank[t][j % 2] for t in range(TT)], parts=1 if j == 3 else 2, late=late if j == 0 else None)
                pe.wait_ge(tile_taken, seen(tile_taken, 2 * TT))
                pe.wait_ge(row_ready, seen(row_ready, TT))
                turn_rows(lambda m, t: qk[:, t, m * P:(m + 1) * P], 7)

                def scores(i):
                    t = i % 2
                    k_tile = i // 2 if i < 8 else 4 + (i - 8) // 4
                    if i >= 2:
                        pe.wait_ge(exp_ready, seen(exp_ready))
                    for c in range(2):
                        mm = pe.matmul(h_bank[i % 2][:, c * T:(c + 1) * T], qz1[:, i // 2, c, t * P:(t + 1) * P],
                                       kt1[:, k_tile, :], start=True, stop=True)
                    mm.then_inc(scores_ready, 1)

                def turn(i):
                    pe.wait_ge(prob_ready, seen(prob_ready))
                    for c in range(1 if i < 8 else 2):
                        for kt_ in range(2):
                            mm = pe.transpose(turn_bank[i % 2][:, c * T + kt_ * P:c * T + (kt_ + 1) * P],
                                              p1[:, i % 2, c, kt_ * P:(kt_ + 1) * P], ident[:, :])
                    mm.then_inc(prob_turned, 1)

                def pv(i):
                    pe.wait_ge(pt_ready, seen(pt_ready))
                    t = i % 2
                    for c in range(1 if i < 8 else 2):
                        if i < 8:
                            dst = y_bank[t][0][:, (i // 2) * P:(i // 2 + 1) * P]
                            cols = slice((i // 2) * P, (i // 2 + 1) * P)
                        else:
                            head = 2 * ((i - 8) // 2) + c
                            dst = y_bank[t][1][:, head * HD:(head + 1) * HD]
                            kv = head // (SWA_Q // 2)
                            cols = slice(512 + kv * HD, 512 + (kv + 1) * HD)
                        for kt_ in range(2):
                            mm = pe.matmul(dst, pt1[:, i % 2, c * T + kt_ * P:c * T + (kt_ + 1) * P], v1[:, kt_, cols],
                                           start=kt_ == 0, stop=kt_ == 1)
                    mm.then_inc(pv_done, 1)

                items(16, 2, scores, turn, pv)
                seen(exp_ready, 2)
                matrix(late=turn_to_xt(mix, mix_ready, swa_out))

            def stick_breaking(late):
                for j in range(6):
                    tile([y_bank[t][j % 2] for t in range(TT)], late=late if j == 0 else None)
                    if 1 <= j <= 4:
                        pe.wait_ge(row_ready, seen(row_ready, TT))
                        turn_rows(lambda m, t: qk_row[:, (j - 1) % 2, t, m * P:(m + 1) * P], 2)
                pe.wait_ge(tile_taken, seen(tile_taken, 2 * TT))
                banks = [y_bank[t][c] for t in range(TT) for c in range(2)]

                def scores(i):
                    t = i % 2
                    if i >= 2:
                        pe.wait_ge(zm_ready, seen(zm_ready))
                    for c in range(2):
                        mm = pe.matmul(h_bank[i % 2][:, c * T:c * T + (t + 1) * P], qz2[:, i // 2, c, t * P:(t + 1) * P],
                                       kt2[:, i // 2, 0:(t + 1) * P], start=True, stop=True)
                    mm.then_inc(scores_ready, 1)

                def turn(i):
                    pe.wait_ge(w_ready, seen(w_ready))
                    for c in range(2):
                        for k in range(i % 2 + 1):
                            mm = pe.transpose(turn_bank[i % 2][:, c * T + k * P:c * T + (k + 1) * P],
                                              w2[:, i % 2, c, k * P:(k + 1) * P], ident[:, :])
                    mm.then_inc(prob_turned, 1)

                def pv(i):
                    pe.wait_ge(pt_ready, seen(pt_ready))
                    pair, t = i // 2, i % 2
                    for c in range(2):
                        head = 2 * pair + c
                        at = (pair % 2) * T + t * P
                        for k in range(t + 1):
                            mm = pe.matmul(banks[pair // 2][HD * c:HD * c + HD, at:at + P],
                                           v2[:, k, head * HD:(head + 1) * HD],
                                           wt2[:, i % 2, c * T + k * P:c * T + (k + 1) * P], start=k == 0, stop=k == t)
                    mm.then_inc(pv_done, 1)

                items(16, 2, scores, turn, pv)
                pe.wait_ge(zm_ready, seen(zm_ready, 2))
                pe.wait_ge(xt_lo_ready, seen(xt_lo_ready, 4))
                matrix()

            def s5_and_pool(late):
                tile([y_bank[t][0] for t in range(TT)], late=late)
                pe.wait_ge(wide_ready, 4)
                for r in range(4):
                    src = (bb_wide, c_wide)[r // 2]
                    if r >= 2:
                        pe.wait_ge(wide_copied, seen(wide_copied))
                    for c in range(4):
                        if r < 2:
                            block = bb_wide[:, r % 2, 4 * c:4 * c + 4, :].rearrange("p i h -> p (i h)")
                        else:
                            block = c_wide[:, r % 2, c, :]
                        mm = pe.transpose(turn_bank[r % 2][:, c * P:(c + 1) * P], block, ident[:, :])
                    mm.then_inc(wide_turned, 1)
                pe.wait_ge(wide_copied, seen(wide_copied, 2))
                tile([y_bank[t][1] for t in range(TT)])
                pe.wait_ge(row_ready, seen(row_ready, TT))
                turn_rows(lambda m, t: ab_row[:, t, m * P:(m + 1) * P], 2)
                pe.wait_ge(row_ready, seen(row_ready, TT))
                pe.wait_ge(s5_loaded, 16 * 5)
                for g in range(4):
                    for k in range(TT):
                        mm = pe.matmul(y_bank[1][g // 2][:, (g % 2) * T:(g % 2 + 1) * T],
                                       ab_row[:, k, (4 + g) * P:(5 + g) * P], pool_mat[:, g, k, :], start=k == 0,
                                       stop=k == TT - 1)
                mm.then_inc(pooled, 1)

                def inputs(i):
                    c, q = i // 4, i % 4
                    if i >= 2:
                        pe.wait_ge(scan_ready, seen(scan_ready))
                    for ri in range(2):
                        mm = pe.matmul(h_bank[i % 2][:, ri * T:(ri + 1) * T], bb_t[32 * q:32 * q + 32, ri, c, :],
                                       ab_t[32 * q:32 * q + 32, c, :], start=True, stop=True)
                    mm.then_inc(bu_ready, 1)

                def outputs(i):
                    c, q = i // 4, i % 4
                    pe.wait_ge(st_ready, seen(st_ready, 2))
                    n = n5[i % 2]
                    terms = ((c_t[:, 0], n[:, 0, 0]), (minus_c, n[:, 1, 1]), (c_t[:, 1], n[:, 0, 1]), (c_t[:, 1], n[:, 1, 0]))
                    for at, (left, right) in enumerate(terms):
                        mm = pe.matmul(y_bank[c // 2][c % 2][32 * q:32 * q + 32, 0:T],
                                       left[:, c, 32 * q:32 * q + 32], right, start=at == 0, stop=at == 3)
                    mm.then_inc(y_part, 1)

                for i in range(S5_TILES + 2):
                    if i < S5_TILES:
                        inputs(i)
                    if i >= 2:
                        outputs(i - 2)
                    if i == 1:
                        pe.wait_ge(pooled_ready, 2)
                        for g in range(4):
                            mm = pe.matmul(turn_bank[g // 2][:, (g % 2) * T:(g % 2 + 1) * T], pool_w[:, g, :],
                                           ab_t[:, 4 + g, :], start=True, stop=True)
                        mm.then_inc(pool_mixed, 1)
                w = unit(4)
                pe.wait_ge(xt_lo_ready, seen(xt_lo_ready, 5))
                for m in range(4):
                    for k in range(4):
                        mm = mm3(pe, h_bank[m // 2][:, (m % 2) * T:(m % 2 + 1) * T],
                                 [v[:, k, m * P:(m + 1) * P] for v in w], (xt_hi[:, k, :], xt_lo[:, k, :]), k == 0, k == 3)
                    if m == 1:
                        mm.then_inc(glu_half, 1)
                mm.then_inc(unit_used, 1)
                pe.wait_ge(xt_lo_ready, seen(xt_lo_ready, 2))
                matrix()

            def before_experts(late):
                pe.wait_ge(rw_lo_ready, 1)
                for t in range(TT):
                    if t == 1:
                        late()
                        pe.wait_ge(xt_lo_ready, seen(xt_lo_ready, 2))
                    for k in range(KD):
                        mm = mm3(pe, h_bank[t][:, 0:N_EXPERTS], xt_part(k, t), (rw_hi[:, k, :], rw_lo[:, k, :]),
                                 k == 0, k == KD - 1)
                    mm.then_inc(routed, 1)
                for j in range(2):
                    tile([y_bank[t][j] for t in range(TT)])
                pe.wait_ge(gates_ready, seen(gates_ready))
                products = ((0, tri[:, 0], 0, True, True), (1, tri[:, 1], 0, True, False), (1, tri[:, 0], 1, False, True),
                            (2, tri[:, 1], 0, True, False), (2, tri[:, 1], 1, False, True))
                for at, left, t, start, stop in products:
                    mm = pe.matmul(h_bank[0][:, at * N_EXPERTS:(at + 1) * N_EXPERTS], left, chosen[:, t], start=start,
                                   stop=stop)
                mm.then_inc(placed, 1)
                turn_h(p=True)
                pe.wait_ge(ple_sig, seen(ple_sig, 2 * TT))
                down(True, True)

            def experts(l):
                pe.wait_ge(overflow_known, l + 1)
                before, n_before = dict(seen.n), n[0]
                with pe.If(pe.value_load(overflow[0:1, 0:1], min_val=0, max_val=1) == 0):
                    gathered_experts(l)
                seen.n = dict(before)
                after, n[0] = n[0], n_before
                with pe.Else():
                    pe.wait_ge(tile_taken, seen(tile_taken, TT))
                    gated(moe[l], all_half[l])
                assert n[0] == after

            def gathered_experts(l):
                turn, into_h, z = turn_bank[0], h_bank[0], (h_bank[1], turn_bank[1])

                def gather(k, pair, dst):
                    for part in range(2):
                        for t in range(TT):
                            mm = pe.matmul(dst[:, part * 2 * SLOTS:(part + 1) * 2 * SLOTS],
                                           xr[:, part, t, k * P:(k + 1) * P], pick[:, pair, t, :],
                                           start=t == 0, stop=t == TT - 1)
                    mm.then_inc(gathered[l], 1)

                def picked(pair, b, t):
                    return pick[:, pair, t, b * SLOTS:(b + 1) * SLOTS]

                def gates_by_slot(pair, b):
                    for t in range(TT):
                        for part in range(2):
                            mm = pe.matmul(turn[:, T:T + N_EXPERTS], picked(pair, b, t), gates_r[:, part, t, :],
                                           start=t == 0 and part == 0, stop=t == TT - 1 and part == 1)
                    return mm

                def gate_up(pair, b, u):
                    w = unit(4)
                    for k in range(4):
                        left = [v[:, 4 * u + k, b * SLOTS:(b + 1) * SLOTS] for v in xe[pair]]
                        mm = mm3(pe, into_h[:, :], left, (w[0][:, k], w[1][:, k]), u == 0 and k == 0, u == 1 and k == 3)
                    mm.then_inc(unit_used, 1)

                def down_slots(first, done):
                    w = unit(2)
                    pe.wait_ge(ht_lo_ready, seen(ht_lo_ready))
                    for c in range(2):
                        for k in range(2):
                            mm = mm3(pe, z[c][:, :], (ht_hi[:, k, 0:SLOTS], ht_lo[:, k, 0:SLOTS]),
                                     [v[:, k, c * 512:(c + 1) * 512] for v in w], first and k == 0, not first and k == 1)
                    mm.then_inc(done, 1)

                def scatter(b, first, last):
                    pe.wait_ge(ye_lo_ready[l], seen(ye_lo_ready[l], 2))
                    if first:
                        pe.wait_ge(tile_taken, seen(tile_taken, TT))
                    for t in range(TT):
                        for c in range(2):
                            for part in range(2):
                                mm = pe.matmul(y_bank[t][c][:, :], pick_t[:, b, t * P:(t + 1) * P],
                                               ye[:, part, c * 512:(c + 1) * 512], start=first and part == 0,
                                               stop=last and part == 1)
                            if t == 0 and last:
                                mm.then_inc(y_half, 1)
                    if last:
                        mm.then_inc(unit_used, 1)

                def step(pair, b, s, prev=True, next_=True):
                    gate_up(pair, b, 0)
                    pe.wait_ge(turn_taken[l], seen(turn_taken[l]))
                    k = 4 * b + 2 * s
                    if next_:
                        if k == 0:
                            pe.wait_ge(slots_ready[l], seen(slots_ready[l]))
                        gather(k, 1 - pair, turn)
                    gate_up(pair, b, 1)
                    if next_:
                        pe.wait_ge(xe_ready[l], seen(xe_ready[l]))
                        gather(k + 1, 1 - pair, turn)
                    if s == 1:
                        if prev:
                            scatter(1 - b, prev == "first", False)
                        down_slots(True, unit_used)
                    elif prev:
                        down_slots(False, unit_used)
                    pe.wait_ge(h_ready, seen(h_ready, TT))
                    if next_:
                        pe.wait_ge(xe_ready[l], seen(xe_ready[l]))
                    for k in range(2):
                        mm = pe.transpose(turn[:, k * P:(k + 1) * P], h[:, 0, k * P:(k + 1) * P], ident[:, :])
                    if s == 0:
                        for t in range(TT):
                            mm = pe.matmul(turn[:, T + t * P:T + (t + 1) * P], picked(pair, b, t), ident_r, start=True,
                                           stop=True)
                    elif b == 0:
                        mm = gates_by_slot(pair, 1)
                    elif next_:
                        mm = gates_by_slot(1 - pair, 0)
                    mm.then_inc(h_turned, 1)

                def pair_of_experts(pair, prev, next_=True):
                    for b in range(2):
                        for s in range(2):
                            step(pair, b, s, prev or ("first" if b == 1 else False), next_)

                pe.wait_ge(slots_ready[l], seen(slots_ready[l]))
                for k in range(KD):
                    if k >= 4:
                        pe.wait_ge(xe_ready[l], seen(xe_ready[l]))
                    gather(k, 0, ((turn, into_h) + z)[k % 4])
                pe.wait_ge(xe_ready[l], seen(xe_ready[l], 4))
                gates_by_slot(0, 0).then_inc(first_gates[l], 1)
                pair_of_experts(0, prev=False)
                with seen.loop(SLOT_ROUNDS, [(lo_ready, 24), (h_ready, 8 * TT), (ht_lo_ready, 8), (slots_ready[l], 2),
                                             (xe_ready[l], 16), (turn_taken[l], 8), (ye_lo_ready[l], 8)]):
                    pair_of_experts(1, prev=True)
                    pair_of_experts(0, prev=True)
                n[0] += 24 * (SLOT_ROUNDS - 1)
                pair_of_experts(1, prev=True)
                pair_of_experts(0, prev=True)
                pair_of_experts(1, prev=True, next_=False)
                down_slots(False, last_out[l])
                scatter(1, False, True)

            pe.wait_ge(const_made, 1)
            pe.wait_ge(x_loaded, 16)
            late = turn_to_xt(x, None)
            for l in range(DEPTH):
                gated(ff[l][0], late=late)
                hybrid(l, turn_to_xt(x, x_ready))
                gated(ff[l][1], late=turn_to_xt(x, x_ready))
                late = turn_to_xt(x, x_ready)
            for l in range(DEPTH):
                (s5_and_pool, stick_breaking)[l](late)
                before_experts(turn_to_xt(x, x_ready))
                experts(l)
                if l < DEPTH - 1:
                    late = turn_to_xt(x, x_ready)

        @block.scalar
        def _(act):
            seen = Tally(act)
            n = [0]

            def link(ins):
                ins.then_inc(act_link, 1)
                act.wait_ge(act_link, seen(act_link))

            early = [0]

            def split_early():
                split()
                early[0] = 1

            def split(times=1):
                times, early[0] = times - early[0], 0
                for _ in range(times):
                    s, r = n[0] % SPLIT, n[0] % RAW
                    act.wait_ge(unit_loaded[r], seen(unit_loaded[r], 32))
                    if n[0] >= SPLIT:
                        act.wait_ge(unit_used, seen(unit_used))
                    act.activation(hi[s][:, :], raw[r][:, :], ACT.Copy).then_inc(hi_ready, 1)
                    n[0] += 1

            def wait_units():
                act.wait_ge(unit_used, n[0] - AHEAD)

            def gated(w, half=first_half, aside=()):
                def silu(t):
                    act.activation(gate_act[:, t], h_bank[t][:, 0:HALF], ACT.Silu).then_inc(gate_ready, 1)

                def step(j):
                    split(1 if j == 0 else 2)
                    act.wait_ge(half, seen(half))
                    silu(0)
                    act.wait_ge(unit_used, seen.ahead(unit_used, 2 if j == 0 else 1))
                    silu(1)
                    split()
                    act.wait_ge(h_turned, seen(h_turned))
                    act.activation(ht_hi[:, :, :].rearrange("p k t -> p (k t)"), turn_bank[0][:, :], ACT.Copy)\
                        .then_inc(ht_hi_ready, 1)
                for j in range(w.peeled + 1):
                    step(j)
                    if 0 < j <= len(aside):
                        aside[j - 1]()
                with seen.loop(w.rounds, [(s, 32) for s in unit_loaded] + [(unit_used, 6), (half, 2), (h_turned, 2)]):
                    step(1)
                    step(1)
                n[0] += 6 * (w.rounds - 1)
                if w is not moe[-1]:
                    split()

            def turned_to_xt(after_norm=True):
                for t in range(TT):
                    for b in range(2):
                        act.wait_ge(x_turned, seen(x_turned))
                        act.activation(xt_hi[:, 4 * b:4 * b + 4, t * P:(t + 1) * P],
                                       turn_bank[b][:, :].rearrange("p (k t) -> p k t", k=4), ACT.Copy)\
                            .then_inc(xt_hi_ready, 1)
                    if t == 0 and after_norm:
                        split_early()
                    elif t == 0 and n[0] < AHEAD:
                        split()

            def turned_rows(dsts):
                for r, dst in enumerate(dsts):
                    act.wait_ge(row_turned, seen(row_turned))
                    src = turn_bank[r % 2][:, :].rearrange("p (m t) -> p m t", m=2)
                    if len(dst.shape) == 3:
                        ins = act.activation(dst, src, ACT.Copy)
                    else:
                        for c in range(2):
                            rows = slice(HD * c, HD * c + HD)
                            ins = act.activation(dst[rows, :, c], src[rows], ACT.Copy)
                    ins.then_inc(col_ready, 1)

            def make_lambda():
                act.wait_ge(const_loaded, 16 * N_LOADS)
                act.wait_ge(const_made, 7)
                act.wait_ge(lam_sums, 1)
                act.activation(lam_e, lam_e, ACT.Exp).then_inc(lam_exps, 1)

            def make_rope():
                act.wait_ge(angles, seen(angles))
                act.activation(rope[:, 1], rope[:, 0], ACT.Sin).then_inc(act_link, 1)
                link(act.activation(rot[:, 0, 0:TT * HD].rearrange("p (t d) -> p t d", t=TT), rope[:, 0], ACT.Abs))
                act.wait_ge(act_link, seen(act_link))
                act.activation(rope[:, 0], rot[:, 0, 0:TT * HD].rearrange("p (t d) -> p t d", t=TT), ACT.Sin,
                               bias=half_pi[:, 0:1], scale=-1.0).then_inc(sines, 1)

            def hybrid(l):
                split(9)
                act.wait_ge(zeroed, l + 1)
                turned_rows([qz1[:, 0:2], qz1[:, 2:4], kt1[:, 0:2], kt1[:, 2:4], qz1[:, 4:6], qz1[:, 6:8], kt1[:, 4:6]])

                def exps(i):
                    b = i % 2
                    act.wait_ge(neg_ready, seen(neg_ready))
                    for c in range(2):
                        src = h_bank[b][:, c * T:(c + 1) * T] if i < 8 else e1[:, b, c]
                        ins = act.activation(e1[:, b, c], src, ACT.Exp, bias=neg[:, b, c:c + 1], scale=SCALE,
                                             accum_out=sums[:, b, c:c + 1])
                    if i >= 8:
                        ins = act.activation(sink_e[:, b], sink_e[:, b], ACT.Exp)
                    ins.then_inc(exp_ready, 1)

                def copies(i):
                    act.wait_ge(prob_turned, seen(prob_turned))
                    width = T if i < 8 else 2 * T
                    act.activation(pt1[:, i % 2, 0:width], turn_bank[i % 2][:, 0:width], ACT.Copy).then_inc(pt_ready, 1)

                for i in range(18):
                    if i < 16:
                        exps(i)
                    if i >= 2:
                        copies(i - 2)
                    if i in (11, 12):
                        if i == 11:
                            act.wait_ge(pv_done, seen(pv_done, 8))
                        t = i - 11
                        for d in range(DIFF_HEADS):
                            ins = act.activation(rot[:, t, d * P:(d + 1) * P], y_bank[t][0][:, d * P:(d + 1) * P],
                                                 ACT.Square, accum_out=ssq[:, t, d:d + 1])
                        ins.then_inc(squares, 1)
                act.wait_ge(pv_done, seen(pv_done, 8))
                for t in range(TT):
                    act.activation(mix[:, t, 512:D], y_bank[t][1][:, :], ACT.Copy).then_inc(swa_out, 1)
                turned_to_xt(after_norm=False)
                split(4)

            def stick_breaking():
                for j in range(6):
                    split(2)
                    if 1 <= j <= 4:
                        dst = (qz2, kt2)[(j - 1) // 2]
                        k = 4 * ((j - 1) % 2)
                        if j == 1:
                            act.wait_ge(zeroed, DEPTH + 1)
                        turned_rows([dst[:, k + 2 * r:k + 2 * r + 2] for r in range(2)])

                def logs(i):
                    b, n_keys = i % 2, (i % 2 + 1) * P
                    act.wait_ge(zm_ready, seen(zm_ready))
                    v = sp_[:, b, :, 0:n_keys]
                    link(act.activation(v, zm[:, b, :, 0:n_keys], ACT.Abs))
                    link(act.activation(v, v, ACT.Exp, scale=-1.0))
                    act.activation(v, v, ACT.Ln, bias=1.0).then_inc(sp_ready, 1)

                def weights(i):
                    b, n_keys = i % 2, (i % 2 + 1) * P
                    act.wait_ge(arg_ready, seen(arg_ready))
                    act.activation(w2[:, b, :, 0:n_keys], zm[:, b, :, 0:n_keys], ACT.Exp).then_inc(w_ready, 1)

                def copies(i):
                    act.wait_ge(prob_turned, seen(prob_turned))
                    for c in range(2):
                        at = slice(c * T, c * T + (i % 2 + 1) * P)
                        ins = act.activation(wt2[:, i % 2, at], turn_bank[i % 2][:, at], ACT.Copy)
                    ins.then_inc(pt_ready, 1)

                for i in range(18):
                    if i < 16:
                        logs(i)
                    if 1 <= i < 17:
                        weights(i - 1)
                    if i >= 2:
                        copies(i - 2)
                act.wait_ge(pv_done, seen(pv_done, 16))
                for b in range(4):
                    act.activation(xt_hi[:, 2 * b:2 * b + 2, :],
                                   y_bank[b // 2][b % 2][:, :].rearrange("p (k t) -> p k t", k=2), ACT.Copy)\
                        .then_inc(xt_hi_ready, 1)
                split(4)

            def s5_parameters():
                act.activation(rw_hi[:, :, :], router_w, ACT.Copy).then_inc(rw_hi_ready, 1)
                act.activation(dt5, log_dt, ACT.Exp).then_inc(s5_act, 1)
                act.wait_ge(s5_dve, seen(s5_dve))
                act.activation(mag5, tmpa, ACT.Exp).then_inc(s5_act, 1)
                act.wait_ge(s5_dve, seen(s5_dve))
                act.activation(sin5, r5, ACT.Sin).then_inc(s5_act, 1)
                link(act.activation(abs5, r5, ACT.Abs))
                act.activation(cos5, abs5, ACT.Sin, bias=half_pi[:, 0:1], scale=-1.0).then_inc(s5_act, 1)

            def s5_and_pool():
                split()
                for r in range(4):
                    act.wait_ge(wide_turned, seen(wide_turned))
                    dst = (bb_t, c_t)[r // 2][:, r % 2]
                    if r == 2:
                        act.activation(minus_c, turn_bank[0][:, :].rearrange("p (c m) -> p c m", c=4), ACT.Copy, scale=-1.0)
                    act.activation(dst, turn_bank[r % 2][:, :].rearrange("p (c m) -> p c m", c=4), ACT.Copy,
                                   scale=-1.0 if r == 3 else 1.0).then_inc(wide_copied, 1)

                def sines_of(c):
                    act.wait_ge(turns_ready, seen(turns_ready))
                    if c >= 2:
                        act.wait_ge(st_ready, 8 * (c - 1))
                    act.activation(trig[c % 2][:, 1], th[:, 0], ACT.Sin, scale=6.283185).then_inc(act_link, 1)
                    link(act.activation(th[:, 1], th[:, 0], ACT.Abs))
                    act.wait_ge(act_link, seen(act_link))
                    act.activation(trig[c % 2][:, 0], th[:, 1], ACT.Sin, bias=half_pi[:, 0:1], scale=-6.283185)\
                        .then_inc(trig_ready, 1)

                split()
                sines_of(0)
                split(2)
                turned_rows([ab_t[:, 2 * r:2 * r + 2, :] for r in range(2)])
                act.wait_ge(pooled, 1)
                for b in range(2):
                    act.activation(ab_t[:, 4 + 2 * b:6 + 2 * b, :], y_bank[1][b][:, :].rearrange("p (g t) -> p g t", g=2),
                                   ACT.Copy).then_inc(pooled_ready, 1)
                sines_of(1)
                act.wait_ge(pool_mixed, 1)
                for g in range(4):
                    ins = act.activation(xt_hi[:, 4 + g, :], turn_bank[g // 2][:, (g % 2) * T:(g % 2 + 1) * T], ACT.Copy,
                                         scale=pool_scale[:, g:g + 1])
                ins.then_inc(xt_hi_ready, 1)
                sines_of(2)

                def square(c):
                    act.wait_ge(s5_dve, seen(s5_dve))
                    act.activation(g1, y5[:, c], ACT.Square).then_inc(s5_act, 1)

                def rest(c):
                    act.wait_ge(s5_dve, seen(s5_dve))
                    act.activation(g1, g1, ACT.Sigmoid, scale=GELU_C).then_inc(s5_act, 1)
                    act.wait_ge(s5_dve, seen(s5_dve))
                    act.activation(xt_hi[:, c, :], y5[:, c], ACT.Copy).then_inc(xt_hi_ready, 1)

                square(0)
                sines_of(3)
                rest(0)
                for c in range(1, 4):
                    square(c)
                    rest(c)
                split()
                for b in range(2):
                    if b == 0:
                        act.wait_ge(glu_half, 1)
                    else:
                        wait_units()
                    act.activation(g5[:, 2 * b:2 * b + 2, :], h_bank[b][:, :].rearrange("p (m t) -> p m t", m=2),
                                   ACT.Sigmoid).then_inc(s5_act, 1)
                for b in range(2):
                    act.wait_ge(s5_dve, seen(s5_dve))
                    act.activation(xt_hi[:, 2 * b:2 * b + 2, :], y5[:, 2 * b:2 * b + 2], ACT.Copy).then_inc(xt_hi_ready, 1)
                split(4)

            def before_experts(l):
                for t in range(TT):
                    act.wait_ge(routed, seen(routed))
                    act.activation(r_s[:, t], h_bank[t][:, 0:N_EXPERTS], ACT.Sigmoid).then_inc(route_sig, 1)
                for t in range(TT):
                    act.activation(xr[:, 0, t], x[:, t, :], ACT.Copy).then_inc(x_high, 1)
                for j in range(2):
                    split(2)
                    wait_units()
                    for t in range(TT):
                        act.activation(ple_gate[:, t, j * 512:(j + 1) * 512], y_bank[t][j][:, :], ACT.Sigmoid)\
                            .then_inc(ple_sig, 1)
                act.preload_act_table(ACT.Silu)
                act.wait_ge(h_turned, seen(h_turned))
                act.activation(ht_hi[:, :, :].rearrange("p k t -> p (k t)"), turn_bank[0][:, :], ACT.Copy)\
                    .then_inc(ht_hi_ready, 1)
                split()

            def experts(l):
                act.wait_ge(overflow_known, l + 1)
                before, n_before = dict(seen.n), n[0]
                with act.If(act.value_load(overflow[0:1, 0:1], min_val=0, max_val=1) == 0):
                    gathered_experts(l)
                seen.n = dict(before)
                after, n[0] = n[0], n_before
                with act.Else():
                    gated(moe[l], all_half[l])
                assert n[0] == after

            def gathered_experts(l):
                z = h_bank[1], turn_bank[1]

                def copy_xe(pair, k, src):
                    act.wait_ge(gathered[l], seen(gathered[l]))
                    for part in range(2):
                        ins = act.activation(xe[pair][part][:, k, :], src[:, part * 2 * SLOTS:(part + 1) * 2 * SLOTS],
                                             ACT.Copy)
                    ins.then_inc(xe_ready[l], 1)

                def high_ye():
                    for c in range(2):
                        act.activation(ye[:, 0, c * 512:(c + 1) * 512], z[c][:, :], ACT.Copy).then_inc(ye_hi_ready[l], 1)

                def step(pair, b, s, prev=True, next_=True):
                    if s == 1 or prev:
                        split()
                    if next_:
                        copy_xe(1 - pair, 4 * b + 2 * s, turn_bank[0])
                    split()
                    act.wait_ge(unit_used, seen.ahead(unit_used, 1 if s == 1 or prev else 2))
                    act.activation(gate_act[:, 0], h_bank[0][:, 0:HALF], ACT.Silu).then_inc(gate_ready, TT)
                    if next_:
                        copy_xe(1 - pair, 4 * b + 2 * s + 1, turn_bank[0])
                    split()
                    act.wait_ge(h_turned, seen(h_turned))
                    act.activation(ht_hi[:, :, 0:SLOTS], turn_bank[0][:, 0:2 * SLOTS].rearrange("p (k c) -> p k c", k=2),
                                   ACT.Copy).then_inc(ht_hi_ready, 1)
                    if s == 0 and prev:
                        high_ye()

                def pair_of_experts(pair, prev=True, next_=True):
                    for b in range(2):
                        for s in range(2):
                            step(pair, b, s, prev or b == 1, next_)

                for k in range(KD):
                    copy_xe(0, k, ((turn_bank[0], h_bank[0]) + z)[k % 4])
                pair_of_experts(0, prev=False)
                with seen.loop(SLOT_ROUNDS, [(s, 128) for s in unit_loaded] + [(unit_used, 24), (h_turned, 8),
                                                                               (gathered[l], 16)]):
                    pair_of_experts(1)
                    pair_of_experts(0)
                n[0] += 24 * (SLOT_ROUNDS - 1)
                pair_of_experts(1)
                pair_of_experts(0)
                pair_of_experts(1, next_=False)
                act.wait_ge(last_out[l], 1)
                high_ye()
                if l < DEPTH - 1:
                    split()

            split()
            turned_to_xt(after_norm=False)
            for l in range(DEPTH):
                gated(ff[l][0], aside=(make_lambda, make_rope) if l == 0 else ())
                act.preload_act_table(ACT.Exp)
                turned_to_xt()
                hybrid(l)
                act.preload_act_table(ACT.Silu)
                turned_to_xt()
                gated(ff[l][1], aside=(s5_parameters,) if l == DEPTH - 1 else ())
                turned_to_xt()
            for l in range(DEPTH):
                (s5_and_pool, stick_breaking)[l]()
                act.preload_act_table(ACT.Sigmoid)
                turned_to_xt()
                before_experts(l)
                experts(l)
                if l < DEPTH - 1:
                    act.preload_act_table_set("natural_log_exp_and_others")
                    turned_to_xt()

        @block.vector
        def _(dve):
            seen = Tally(dve)
            n = [0]

            def link(ins):
                ins.then_inc(dve_link, 1)
                dve.wait_ge(dve_link, seen(dve_link))

            early = [0]

            def split_early():
                dve.wait_ge(lo_ready, n[0])
                split()
                early[0] = 1

            def split(times=1):
                times, early[0] = times - early[0], 0
                for _ in range(times):
                    s, r = n[0] % SPLIT, n[0] % RAW
                    dve.wait_ge(hi_ready, seen(hi_ready))
                    dve.tensor_tensor(lo[s][:, :], raw[r][:, :], hi[s][:, :].bitcast(F32), ALU.subtract)\
                        .then_inc(lo_ready, 1)
                    n[0] += 1

            def leave_split():
                seen(hi_ready)
                n[0] += 1

            def wait_units():
                dve.wait_ge(unit_used, n[0] - AHEAD)

            def low_h():
                dve.wait_ge(ht_hi_ready, seen(ht_hi_ready))
                dve.tensor_tensor(ht_lo[:, :, :].rearrange("p k t -> p (k t)"), turn_bank[0][:, :],
                                  ht_hi[:, :, :].bitcast(F32).rearrange("p k t -> p (k t)"), ALU.subtract)\
                    .then_inc(ht_lo_ready, 1)

            def gated(w, aside=()):
                def step(i, j):
                    split(1 if j == 0 else 2)
                    for t in range(TT):
                        dve.wait_ge(gate_ready, seen(gate_ready))
                        up = h_bank[t][:, HALF:2 * HALF]
                        if w.experts:
                            e = i + j // EXPERT_STEPS
                            g = gates[:, t, e:e + 1] if isinstance(e, int) else gates[:, t, bass.ds(e, 1)]
                            ins = dve.scalar_tensor_tensor(out=h[:, t], in0=up, scalar=g, in1=gate_act[:, t],
                                                           op0=ALU.mult, op1=ALU.mult)
                        else:
                            ins = dve.tensor_tensor(h[:, t], up, gate_act[:, t], ALU.mult)
                        ins.then_inc(h_ready, 1)
                    split()
                    low_h()
                for j in range(w.peeled + 1):
                    step(0, j)
                    if 0 < j <= len(aside):
                        aside[j - 1]()
                with seen.loop(w.rounds, [(hi_ready, 6), (gate_ready, 2 * TT), (ht_hi_ready, 2)]) as i:
                    step(i, w.peeled + 1)
                    step(i, w.peeled + 2)
                n[0] += 6 * (w.rounds - 1)
                if w is not moe[-1]:
                    leave_split()

            def norm(k, coef, done, split_ahead=AHEAD):
                def residual(t, c):
                    v = x[:, t, c * 512:(c + 1) * 512]
                    dve.scalar_tensor_tensor(out=v, in0=v, scalar=coef, in1=y_bank[t][c][:, :],
                                             op0=ALU.mult, op1=ALU.add).then_inc(dve_link, 1)

                def statistics(t, c, links):
                    if links:
                        dve.wait_ge(dve_link, seen(dve_link, links))
                    dve.bn_stats(stats[:, t, c, :], x[:, t, c * 512:(c + 1) * 512]).then_inc(dve_link, 1)

                def variance(t, links):
                    dve.wait_ge(dve_link, seen(dve_link, links))
                    dve.bn_aggr(moments[:, t, :], stats[:, t].rearrange("p c s -> p (c s)")).then_inc(var_ready, 1)
                    dve.wait_ge(var_ready, seen(var_ready))

                def scaled(t, meanwhile=None):
                    link(dve.scalar_tensor_tensor(out=x[:, t, :], in0=x[:, t, :], scalar=moments[:, t, 0:1],
                                                  in1=ln_gb[:, 0, :], op0=ALU.subtract, op1=ALU.mult))
                    if meanwhile is not None:
                        meanwhile()
                    dve.wait_ge(rstd_ready, seen(rstd_ready))
                    for c in range(2):
                        v = x[:, t, c * 512:(c + 1) * 512]
                        dve.scalar_tensor_tensor(out=v, in0=v, scalar=rstd[:, t, 0:1], in1=ln_gb[:, 1, c * 512:(c + 1) * 512],
                                                 op0=ALU.mult, op1=ALU.add).then_inc(done, 1)

                for c in range(2):
                    dve.wait_ge(y_half, seen(y_half))
                    residual(0, c)
                    statistics(0, c, 1 + c)
                variance(0, 1)
                dve.wait_ge(gb_loaded, 32 * (k + 1))

                def begin_second():
                    dve.wait_ge(unit_used, n[0] - split_ahead)
                    residual(1, 0)

                scaled(0, begin_second)
                residual(1, 1)
                for c in range(2):
                    statistics(1, c, 2 - 2 * c)
                variance(1, 2)
                if done is x_ready:
                    low_xt(0)
                scaled(1)
                if done is x_ready:
                    split_early()
                    low_xt(1)

            def low_xt(t):
                for b in range(2):
                    dve.wait_ge(xt_hi_ready, seen(xt_hi_ready))
                    at = (slice(None), slice(4 * b, 4 * b + 4), slice(t * P, (t + 1) * P))
                    dve.tensor_tensor(xt_lo[at], turn_bank[b][:, :].rearrange("p (k t) -> p k t", k=4),
                                      xt_hi[at].bitcast(F32), ALU.subtract).then_inc(xt_lo_ready, 1)

            def reduce_angle(dst, src, whole):
                link(dve.tensor_scalar(whole, src, 1.0 / TWO_PI, ROUND, ALU.mult, ALU.add))
                link(dve.tensor_scalar(whole, whole, ROUND, None, ALU.subtract))
                for part, first in ((TP_HI, src), (TP_MID, dst), (TP_LO, dst)):
                    link(dve.scalar_tensor_tensor(out=dst, in0=whole, scalar=-part, in1=first, op0=ALU.mult, op1=ALU.add))
                return dve.tensor_scalar(dst, dst, PI_IN, -PI_IN, ALU.min, ALU.max)

            def make_lambda():
                dve.wait_ge(const_loaded, 16 * N_LOADS)
                prod = rot[:, 0, 0:DEPTH * 2 * HD].rearrange("p (l i d) -> p l i d", l=DEPTH, i=2)
                for l in range(DEPTH):
                    v = lam_in[:, l].rearrange("p (i j) d -> p j i d", j=2)
                    link(dve.tensor_tensor(prod[:, l], v[:, 0], v[:, 1], ALU.mult))
                dve.tensor_reduce(lam_e, prod, AX_X, ALU.add).then_inc(lam_sums, 1)
                dve.wait_ge(lam_exps, 1)
                for l in range(DEPTH):
                    link(dve.tensor_tensor(lam[:, l:l + 1], lam_e[:, l, 0:1], lam_e[:, l, 1:2], ALU.subtract))
                    link(dve.tensor_scalar(lam[:, l:l + 1], lam[:, l:l + 1], lambda_init(l), None, ALU.add))
                    link(dve.tensor_scalar(sub_g[:, l], sub_g[:, l], 1.0 - lambda_init(l), None, ALU.mult))
                link(dve.tensor_scalar(neg_sink, sink, -1.0, None, ALU.mult))

            def make_angles():
                pos = small[:, 52:54]
                link(dve.tensor_copy(pos, position[:, :]))
                ang = rot[:, 1, 0:TT * 32].rearrange("p (t f) -> p t f", t=TT)
                whole = rot[:, 1, 64:64 + TT * 32].rearrange("p (t f) -> p t f", t=TT)
                red = rot[:, 1, 128:128 + TT * 32].rearrange("p (t f) -> p t f", t=TT)
                for t in range(TT):
                    link(dve.tensor_scalar(ang[:, t], freq, pos[:, t:t + 1], None, ALU.mult))
                link(reduce_angle(red, ang, whole))
                link(dve.tensor_copy(rope[:, 0, :, 0:32], red))
                dve.tensor_copy(rope[:, 0, :, 32:64], red).then_inc(angles, 1)
                dve.wait_ge(sines, 1)
                link(dve.tensor_scalar(rope[:, 1, :, 0:32], rope[:, 1, :, 0:32], -1.0, None, ALU.mult))

            def rotate(t, src, heads, dsts, done):
                cos = rope[:, 0, t:t + 1, :].broadcast_to([P, heads, HD])
                sin = rope[:, 1, t:t + 1, :].broadcast_to([P, heads, HD])
                by_cos = rot[:, 0, 0:heads * HD].rearrange("p (h d) -> p h d", h=heads)
                by_sin = rot[:, 1, 0:heads * HD].rearrange("p (h d) -> p h d", h=heads)
                dve.tensor_tensor(by_sin[:, :, 0:32], src[:, :, 32:64], sin[:, :, 0:32], ALU.mult).then_inc(dve_link, 1)
                dve.tensor_tensor(by_sin[:, :, 32:64], src[:, :, 0:32], sin[:, :, 32:64], ALU.mult).then_inc(dve_link, 1)
                dve.tensor_tensor(by_cos, src, cos, ALU.mult).then_inc(tile_taken, 1)
                dve.wait_ge(dve_link, seen(dve_link, 2))
                dve.wait_ge(tile_taken, seen(tile_taken))
                for dst in dsts:
                    ins = dve.tensor_tensor(dst, by_cos, by_sin, ALU.add)
                ins.then_inc(done, 1)
                if done is dve_link:
                    dve.wait_ge(dve_link, seen(dve_link))

            def hybrid(l):
                for j in range(5):
                    split(1 if j == 3 else 2)
                    wait_units()
                    for t in range(TT):
                        bank_ = y_bank[t][j % 2]
                        if j < 3:
                            rotate(t, bank_[:, :].rearrange("p (h d) -> p h d", h=8), 8,
                                   [qk[:, t, j * 512:(j + 1) * 512].rearrange("p (h d) -> p h d", h=8)], dve_link)
                        elif j == 3:
                            link(dve.tensor_copy(v1[:, t, 512:640], bank_[:, P:2 * P]))
                            twice = qk[:, t, 1536:1792].rearrange("p (h two d) -> p two h d", h=2, two=2)
                            rotate(t, bank_[:, 0:P].rearrange("p (h d) -> p h d", h=2), 2, [twice[:, 0], twice[:, 1]],
                                   row_ready)
                        else:
                            dve.tensor_copy(v1[:, t, 0:512], bank_[:, :]).then_inc(tile_taken, 1)
                            dve.wait_ge(tile_taken, seen(tile_taken))

                def maxima(i):
                    b = i % 2
                    dve.wait_ge(scores_ready, seen(scores_ready))
                    if i >= 2:
                        dve.wait_ge(prob_ready, 16 * l + i - 1)
                    s = h_bank[b][:, :].rearrange("p (c k) -> p c k", c=2)
                    if i >= 8:
                        pair, t = (i - 8) // 2, i % 2
                        mask = swa_mask[:, t:t + 1, :].broadcast_to([P, 2, T])
                        link(dve.tensor_tensor(e1[:, b], s, mask, ALU.add))
                        s = e1[:, b]
                    link(dve.tensor_reduce(nmax[:, b], s, AX_X, ALU.max, negate=True))
                    if i < 8:
                        dve.tensor_scalar(neg[:, b], nmax[:, b], SCALE, None, ALU.mult).then_inc(neg_ready, 1)
                    else:
                        two = slice(2 * pair, 2 * pair + 2)
                        link(dve.scalar_tensor_tensor(out=neg[:, b], in0=nmax[:, b], scalar=SCALE,
                                                      in1=neg_sink[:, l, two], op0=ALU.mult, op1=ALU.min))
                        dve.tensor_tensor(sink_e[:, b], sink[:, l, two], neg[:, b], ALU.add).then_inc(neg_ready, 1)

                def probs(i):
                    b = i % 2
                    dve.wait_ge(exp_ready, seen(exp_ready))
                    if i >= 2:
                        dve.wait_ge(prob_turned, 16 * l + i - 1)
                    if i < 8:
                        link(dve.reciprocal(inv[:, b], sums[:, b]))
                        link(dve.tensor_scalar(p1[:, b, 1], e1[:, b, 1], inv[:, b, 1:2], lam[:, l:l + 1], ALU.mult, ALU.mult))
                        dve.scalar_tensor_tensor(out=p1[:, b, 0], in0=e1[:, b, 0], scalar=inv[:, b, 0:1], in1=p1[:, b, 1],
                                                 op0=ALU.mult, op1=ALU.subtract).then_inc(prob_ready, 1)
                    else:
                        link(dve.tensor_tensor(sums[:, b], sums[:, b], sink_e[:, b], ALU.add))
                        link(dve.reciprocal(inv[:, b], sums[:, b]))
                        for c in range(2):
                            ins = dve.tensor_scalar(p1[:, b, c], e1[:, b, c], inv[:, b, c:c + 1], None, ALU.mult)
                        ins.then_inc(prob_ready, 1)

                for i in range(17):
                    if i < 16:
                        maxima(i)
                    if i >= 1:
                        probs(i - 1)
                    if i in (14, 15):
                        if i == 14:
                            dve.wait_ge(sub_rstd, seen(sub_rstd))
                        t = i - 14
                        for d in range(DIFF_HEADS):
                            at = slice(d * P, (d + 1) * P)
                            ins = dve.scalar_tensor_tensor(out=mix[:, t, at], in0=y_bank[t][0][:, at],
                                                           scalar=srs[:, t, d:d + 1], in1=sub_g[:, l], op0=ALU.mult,
                                                           op1=ALU.mult)
                        ins.then_inc(mix_ready, 1)
                for t in range(TT):
                    low_xt(t)
                split(3)
                leave_split()

            def stick_breaking():
                for j in range(6):
                    split(2)
                    wait_units()
                    for t in range(TT):
                        if j < 4:
                            dve.tensor_copy(qk_row[:, j % 2, t], y_bank[t][j % 2][:, :]).then_inc(row_ready, 1)
                        else:
                            dve.tensor_copy(v2[:, t, (j - 4) * 512:(j - 3) * 512], y_bank[t][j % 2][:, :])\
                                .then_inc(tile_taken, 1)
                seen(tile_taken, 2 * TT)

                def masked(i):
                    b, n_keys = i % 2, (i % 2 + 1) * P
                    if i >= 2:
                        dve.wait_ge(w_ready, seen(w_ready))
                    dve.wait_ge(scores_ready, seen(scores_ready))
                    mask = causal[:, T - n_keys:T].rearrange("p (o k) -> p o k", o=1).broadcast_to([P, 2, n_keys])
                    s = h_bank[b][:, :].rearrange("p (c k) -> p c k", c=2)[:, :, 0:n_keys]
                    dve.scalar_tensor_tensor(out=zm[:, b, :, 0:n_keys], in0=s, scalar=SCALE, in1=mask,
                                             op0=ALU.mult, op1=ALU.add).then_inc(zm_ready, 1)

                def exponents(i):
                    b, n_keys = i % 2, (i % 2 + 1) * P
                    dve.wait_ge(sp_ready, seen(sp_ready))
                    if i >= 2:
                        dve.wait_ge(prob_turned, 16 * DEPTH + i - 1)
                    z, keep = zm[:, b, :, 0:n_keys], soft[:, b, :, 0:n_keys]
                    link(dve.scalar_tensor_tensor(out=keep, in0=z, scalar=0.0, in1=sp_[:, b, :, 0:n_keys],
                                                  op0=ALU.max, op1=ALU.add))
                    for c in range(2):
                        dve.tensor_tensor_scan(w2[:, b, c, 0:n_keys][:, ::-1], before[:, 1, 0:1].broadcast_to([P, n_keys]),
                                               soft[:, b, c, 0:n_keys][:, ::-1], 0.0, ALU.mult, ALU.add).then_inc(dve_link, 1)
                    dve.wait_ge(dve_link, seen(dve_link, 2))
                    dve.tensor_tensor(z, z, w2[:, b, :, 0:n_keys], ALU.subtract).then_inc(arg_ready, 1)

                for i in range(17):
                    if i < 16:
                        masked(i)
                    if i >= 1:
                        exponents(i - 1)
                for b in range(4):
                    dve.wait_ge(xt_hi_ready, seen(xt_hi_ready))
                    dve.tensor_tensor(xt_lo[:, 2 * b:2 * b + 2, :],
                                      y_bank[b // 2][b % 2][:, :].rearrange("p (k t) -> p k t", k=2),
                                      xt_hi[:, 2 * b:2 * b + 2, :].bitcast(F32), ALU.subtract).then_inc(xt_lo_ready, 1)
                split(3)
                leave_split()

            def s5_parameters():
                dve.wait_ge(rw_hi_ready, 1)
                dve.tensor_tensor(rw_lo[:, :, :], router_w, rw_hi[:, :, :].bitcast(F32), ALU.subtract)\
                    .then_inc(rw_lo_ready, 1)
                dve.wait_ge(s5_act, seen(s5_act))
                link(dve.tensor_tensor(ang5, lam_im, dt5, ALU.mult))
                dve.tensor_tensor(tmpa, lam_re, dt5, ALU.mult).then_inc(s5_dve, 1)
                reduce_angle(r5, ang5, k5).then_inc(s5_dve, 1)
                dve.wait_ge(s5_dve, 2)
                link(dve.tensor_scalar(phi5, r5, 1.0 / TWO_PI, None, ALU.mult))
                link(dve.tensor_tensor(den, lam_re, lam_re, ALU.mult))
                link(dve.tensor_tensor(tmpb, lam_im, lam_im, ALU.mult))
                link(dve.tensor_tensor(den, den, tmpb, ALU.add))
                link(dve.reciprocal(den, den))
                dve.wait_ge(s5_act, seen(s5_act, 3))
                link(dve.tensor_tensor(lbr, mag5, cos5, ALU.mult))
                link(dve.tensor_tensor(lbi, mag5, sin5, ALU.mult))
                link(dve.tensor_scalar(lbr, lbr, 1.0, None, ALU.subtract))
                for f, (u, v), op in ((fre, (lam_re, lam_im), ALU.add), (fim, (lam_im, lam_re), ALU.subtract)):
                    link(dve.tensor_tensor(tmpa, lbr, u, ALU.mult))
                    link(dve.tensor_tensor(tmpb, lbi, v, ALU.mult))
                    first, second = (tmpa, tmpb) if op is ALU.add else (tmpb, tmpa)
                    link(dve.tensor_tensor(f, first, second, op))
                    link(dve.tensor_tensor(f, f, den, ALU.mult))

            def s5_matrices():
                dve.wait_ge(s5_loaded, 16 * 5)
                link(dve.memset(bb_wide, 0.0))
                f_re = fre.rearrange("p (i o) -> p i o", o=1).broadcast_to([P, 16, 16])
                f_im = fim.rearrange("p (i o) -> p i o", o=1).broadcast_to([P, 16, 16])
                for ri in range(2):
                    link(dve.tensor_tensor(bb_tmp[:, 0], b_nat[:, ri], f_re, ALU.mult))
                    link(dve.tensor_tensor(bb_tmp[:, 1], b_nat[:, 1 - ri], f_im, ALU.mult))
                    for g in range(2):
                        r = slice(P5 * g, P5 * g + P5)
                        link(dve.tensor_tensor(bb_wide[r, ri, :, 16 * g:16 * g + 16], bb_tmp[r, 0], bb_tmp[r, 1],
                                               ALU.subtract if ri == 0 else ALU.add))
                    for g in range(2):
                        ins = dve.tensor_scalar(c_wide[:, ri, :, P5 * g:P5 * g + P5], c_nat[:, ri], parity[:, g:g + 1],
                                                None, ALU.mult)
                        ins.then_inc(wide_ready, 1)

            def s5_and_pool():
                def angles_of(c):
                    phi = phi5[:, 4 * c:4 * c + 4].rearrange("p (i o) -> p i o", o=1).broadcast_to([P, 4, T])
                    time = time_row.rearrange("p (o t) -> p o t", o=1).broadcast_to([P, 4, T])
                    link(dve.tensor_tensor(th[:, 0], phi, time, ALU.mult))
                    link(dve.tensor_scalar(th[:, 1], th[:, 0], ROUND, ROUND, ALU.add, ALU.subtract))
                    dve.tensor_tensor(th[:, 0], th[:, 0], th[:, 1], ALU.subtract).then_inc(turns_ready, 1)

                for j in range(2):
                    split(2)
                    if j == 0:
                        dve.wait_ge(wide_turned, 4)
                        angles_of(0)
                    wait_units()
                    for t in range(TT):
                        dve.tensor_copy(ab_row[:, t, j * 512:(j + 1) * 512], y_bank[t][j][:, :]).then_inc(row_ready, 1)
                def gelu(c, part):
                    if part == 0:
                        dve.wait_ge(y_part, 4 * (c + 1))
                        dve.scalar_tensor_tensor(out=y5[:, c], in0=ab_t[:, c], scalar=d_skip[:, c:c + 1],
                                                 in1=y_bank[c // 2][c % 2][:, 0:T],
                                                 op0=ALU.mult, op1=ALU.add).then_inc(s5_dve, 1)
                    elif part == 1:
                        dve.wait_ge(s5_act, seen(s5_act))
                        link(dve.tensor_scalar(g1, g1, 0.044715, 1.0, ALU.mult, ALU.add))
                        dve.tensor_tensor(g1, g1, y5[:, c], ALU.mult).then_inc(s5_dve, 1)
                    elif part == 2:
                        dve.wait_ge(s5_act, seen(s5_act))
                        dve.tensor_tensor(y5[:, c], y5[:, c], g1, ALU.mult).then_inc(s5_dve, 1)
                    else:
                        dve.wait_ge(xt_hi_ready, seen(xt_hi_ready))
                        dve.tensor_tensor(xt_lo[:, c, :], y5[:, c], xt_hi[:, c, :].bitcast(F32), ALU.subtract)\
                            .then_inc(xt_lo_ready, 1)

                for c in range(4):
                    dve.wait_ge(trig_ready, c + 1)
                    if c < 3:
                        angles_of(c + 1)
                    if c == 1:
                        dve.wait_ge(xt_hi_ready, seen(xt_hi_ready))
                        for g in range(4):
                            ins = dve.scalar_tensor_tensor(out=xt_lo[:, 4 + g, :],
                                                           in0=turn_bank[g // 2][:, (g % 2) * T:(g % 2 + 1) * T],
                                                           scalar=pool_scale[:, g:g + 1], in1=xt_hi[:, 4 + g, :].bitcast(F32),
                                                           op0=ALU.mult, op1=ALU.subtract)
                        ins.then_inc(xt_lo_ready, 1)
                    for q in range(4):
                        i = 4 * c + q
                        dve.wait_ge(bu_ready, seen(bu_ready))
                        if i > 0:
                            dve.wait_ge(scan_ready, i)
                        bu = h_bank[i % 2][:, :].rearrange("p (c t) -> p c t", c=2)
                        for j in range(2):
                            dve.tensor_tensor(m5[:, j], bu, trig[c % 2][:, j, q:q + 1, :].broadcast_to([P, 2, T]), ALU.mult)\
                                .then_inc(dve_link, 1)
                        dve.wait_ge(dve_link, seen(dve_link, 2))
                        dve.tensor_tensor(m5[:, 0, 0], m5[:, 0, 0], m5[:, 1, 1], ALU.add).then_inc(dve_link, 1)
                        dve.tensor_tensor(m5[:, 0, 1], m5[:, 0, 1], m5[:, 1, 0], ALU.subtract).then_inc(dve_link, 1)
                        dve.wait_ge(dve_link, seen(dve_link, 2))
                        if i >= 2:
                            dve.wait_ge(st_ready, 2 * (i - 1))
                        for ri in range(2):
                            ins = dve.tensor_tensor_scan(s5[:, i % 2, ri], mag5[:, i:i + 1].broadcast_to([P, T]),
                                                         m5[:, 0, ri], 0.0, ALU.mult, ALU.add)
                        ins.then_inc(scan_ready, 1)
                        if c >= 1 and q >= 2:
                            gelu(c - 1, q - 2)
                        if c >= 2 and q < 2:
                            gelu(c - 2, q + 2)
                for c, part in ((2, 2), (3, 0), (2, 3), (3, 1), (3, 2), (3, 3)):
                    gelu(c, part)
                split()
                for b in range(2):
                    two = slice(2 * b, 2 * b + 2)
                    dve.wait_ge(s5_act, seen(s5_act))
                    dve.tensor_tensor(y5[:, two], y5[:, two], g5[:, two], ALU.mult).then_inc(s5_dve, 1)
                for b in range(2):
                    two = slice(2 * b, 2 * b + 2)
                    dve.wait_ge(xt_hi_ready, seen(xt_hi_ready))
                    dve.tensor_tensor(xt_lo[:, two, :], y5[:, two], xt_hi[:, two, :].bitcast(F32), ALU.subtract)\
                        .then_inc(xt_lo_ready, 1)
                split(3)
                leave_split()

            def before_experts(l):
                split(1)
                if l == 0:
                    dve.wait_ge(const_made, 8)
                dve.tensor_copy(tri.rearrange("p a c -> p (a c)"), tri_ones).then_inc(dve_link, 1)
                link(dve.tensor_copy(ident_r, ident[:, :]))
                dve.wait_ge(dve_link, seen(dve_link))
                dve.wait_ge(route_sig, seen(route_sig, TT))
                bias = router_b.rearrange("p (o e) -> p o e", o=1).broadcast_to([P, TT, N_EXPERTS])
                link(dve.tensor_tensor(r_sel, r_s, bias, ALU.add))
                four = r_sel.rearrange("p t (g e) -> p (t g) e", g=N_GROUPS)
                for i, (u, v, op) in enumerate(((0, 1, ALU.max), (0, 1, ALU.min), (2, 3, ALU.max), (2, 3, ALU.min))):
                    dve.tensor_tensor(r_two[:, i], four[:, :, u], four[:, :, v], op).then_inc(dve_link, 1)
                dve.wait_ge(dve_link, seen(dve_link, 4))
                dve.tensor_tensor(r_two[:, 4], r_two[:, 0], r_two[:, 2], ALU.max).then_inc(dve_link, 1)
                dve.tensor_tensor(r_two[:, 5], r_two[:, 0], r_two[:, 2], ALU.min).then_inc(dve_link, 1)
                dve.tensor_tensor(r_two[:, 6], r_two[:, 1], r_two[:, 3], ALU.max).then_inc(dve_link, 1)
                dve.wait_ge(dve_link, seen(dve_link, 3))
                link(dve.tensor_tensor(r_two[:, 5], r_two[:, 5], r_two[:, 6], ALU.max))
                link(dve.tensor_tensor(r_two[:, 7], r_two[:, 4], r_two[:, 5], ALU.add))
                score = r_two[:, 7].rearrange("p (t g) -> p t g", t=TT)

                def rank(values, t, n_values, dst):
                    mine = values.rearrange("p (e o) -> p e o", o=1).broadcast_to([P, n_values, n_values])
                    others = values.rearrange("p (o e) -> p o e", o=1).broadcast_to([P, n_values, n_values])
                    g, q = r_gt[:, 0:n_values, 0:n_values], r_eq[:, 0:n_values, 0:n_values]
                    dve.tensor_tensor(g, others, mine, ALU.is_gt).then_inc(dve_link, 1)
                    dve.tensor_tensor(q, others, mine, ALU.is_equal).then_inc(dve_link, 1)
                    dve.wait_ge(dve_link, seen(dve_link, 2))
                    link(dve.tensor_tensor(q, q, before[:, 0:n_values, 0:n_values], ALU.mult))
                    link(dve.tensor_tensor(g, g, q, ALU.add))
                    link(dve.tensor_reduce(dst, g, AX_X, ALU.add))

                for t in range(TT):
                    rank(score[:, t], t, N_GROUPS, r_grp[:, t])
                    link(dve.tensor_scalar(r_grp[:, t], r_grp[:, t], 0.5, FAR, ALU.is_gt, ALU.mult))
                    away = r_grp[:, t].rearrange("p (g o) -> p g o", o=1).broadcast_to([P, N_GROUPS, 4])
                    link(dve.tensor_tensor(r_sel[:, t].rearrange("p (g e) -> p g e", g=N_GROUPS),
                                           r_sel[:, t].rearrange("p (g e) -> p g e", g=N_GROUPS), away, ALU.add))
                    rank(r_sel[:, t], t, N_EXPERTS, r_rank[:, t])
                    link(dve.tensor_scalar(r_rank[:, t], r_rank[:, t], 1.5, None, ALU.is_lt))
                    link(dve.tensor_copy(chosen[:, t], r_rank[:, t]))
                    link(dve.tensor_tensor(r_rank[:, t], r_rank[:, t], r_s[:, t], ALU.mult))
                    link(dve.tensor_reduce(r_sum[:, t:t + 1], r_rank[:, t], AX_X, ALU.add))
                    link(dve.reciprocal(r_sum[:, t:t + 1], r_sum[:, t:t + 1]))
                    ins = dve.tensor_scalar(gates[:, t], r_rank[:, t], r_sum[:, t:t + 1], None, ALU.mult)
                    link(ins)
                link(dve.tensor_copy(gates_r[:, 0], gates[:, :, :]))
                dve.tensor_tensor(gates_r[:, 1], gates[:, :, :], gates_r[:, 0].bitcast(F32), ALU.subtract)\
                    .then_inc(gates_ready, 1)
                for t in range(TT):
                    split()
                    if t == 0:
                        dve.wait_ge(x_high, seen(x_high, TT))
                    dve.tensor_tensor(xr[:, 1, t], x[:, t, :], xr[:, 0, t].bitcast(F32), ALU.subtract)
                split()
                low_h()
                dve.wait_ge(placed, l + 1)
                dve.tensor_scalar(slot_of, h_bank[0][:, 0:TT * N_EXPERTS].rearrange("p (t e) -> p t e", t=TT), ELSEWHERE,
                                  None, ALU.add).then_inc(dve_link, 1)
                link(dve.tensor_reduce(most, h_bank[0][:, TT * N_EXPERTS:(TT + 1) * N_EXPERTS], AX_X, ALU.max))
                dve.wait_ge(dve_link, seen(dve_link))
                dve.tensor_scalar(overflow[:, :], most, SLOTS + 0.5, None, ALU.is_gt).then_inc(overflow_known, 1)
                for pair in range(2):
                    pick_slots(l, 2 * pair, pair)
                split()
                for t in range(TT):
                    if t == 0:
                        dve.wait_ge(y_half, seen(y_half, 2))
                    else:
                        wait_units()
                    for c in range(2):
                        at = slice(c * 512, (c + 1) * 512)
                        ins = dve.tensor_tensor(ple_gate[:, t, at], y_bank[t][c][:, :], ple_gate[:, t, at], ALU.mult)
                        if c == 0:
                            link(ins)
                    ins.then_inc(tile_taken, 1)
                    dve.wait_ge(tile_taken, seen(tile_taken))
                    link(dve.scalar_tensor_tensor(out=x[:, t, :], in0=x[:, t, :], scalar=ALPHA, in1=ple_gate[:, t, :],
                                                  op0=ALU.mult, op1=ALU.add))

            def pick_slots(l, e, pair):
                for b in range(2):
                    for t in range(TT):
                        at = e + b
                        col = slot_of[:, t, at:at + 1] if isinstance(e, int) else slot_of[:, t, bass.ds(at, 1)]
                        ins = dve.tensor_scalar(pick[:, pair, t, b * SLOTS:(b + 1) * SLOTS], slot_row, col, None,
                                                ALU.is_equal)
                ins.then_inc(slots_ready[l], 1)

            def experts(l):
                dve.wait_ge(overflow_known, l + 1)
                before, n_before = dict(seen.n), n[0]
                with dve.If(dve.value_load(overflow[0:1, 0:1], min_val=0, max_val=1) == 0):
                    gathered_experts(l)
                seen.n = dict(before)
                after, n[0] = n[0], n_before
                with dve.Else():
                    gated(moe[l])
                assert n[0] == after

            def gathered_experts(l):
                turn, z = turn_bank[0], (h_bank[1], turn_bank[1])

                def gates_by_slot(e, b):
                    col = turn[:, T + e:T + e + 1] if isinstance(e, int) else turn[:, bass.ds(e + T, 1)]
                    dve.tensor_copy(slot_gate[:, b:b + 1], col).then_inc(turn_taken[l], 1)

                def low_ye():
                    for c in range(2):
                        dve.wait_ge(ye_hi_ready[l], seen(ye_hi_ready[l]))
                        at = slice(c * 512, (c + 1) * 512)
                        dve.tensor_tensor(ye[:, 1, at], z[c][:, :], ye[:, 0, at].bitcast(F32), ALU.subtract)\
                            .then_inc(ye_lo_ready[l], 1)

                def step(e, pair, b, s, prev=True, next_=True, after_next=True):
                    if s == 1 or prev:
                        split()
                    if b == 1 and s == 1 and after_next:
                        pick_slots(l, e + 3, pair)
                    split()
                    dve.wait_ge(gate_ready, seen(gate_ready, TT))
                    dve.wait_ge(turn_taken[l], seen(turn_taken[l]))
                    dve.scalar_tensor_tensor(out=h[:, 0], in0=h_bank[0][:, HALF:2 * HALF], scalar=slot_gate[:, b:b + 1],
                                             in1=gate_act[:, 0], op0=ALU.mult, op1=ALU.mult).then_inc(h_ready, TT)
                    split()
                    dve.wait_ge(ht_hi_ready, seen(ht_hi_ready))
                    dve.tensor_tensor(ht_lo[:, :, 0:SLOTS], turn[:, 0:2 * SLOTS].rearrange("p (k c) -> p k c", k=2),
                                      ht_hi[:, :, 0:SLOTS].bitcast(F32), ALU.subtract).then_inc(ht_lo_ready, 1)
                    if s == 0:
                        dve.tensor_copy(pick_t[:, b, :], turn[:, T:2 * T]).then_inc(turn_taken[l], 1)
                        if prev:
                            low_ye()
                    elif b == 0 or next_:
                        gates_by_slot(e + 1, 1 - b)

                def pair_of_experts(e, pair, prev=True, next_=True, after_next=True):
                    for b in range(2):
                        for s in range(2):
                            step(e + b, pair, b, s, prev or b == 1, next_, after_next)

                dve.wait_ge(first_gates[l], 1)
                gates_by_slot(0, 0)
                pair_of_experts(0, 0, prev=False)
                with seen.loop(SLOT_ROUNDS, [(hi_ready, 24), (gate_ready, 8 * TT), (ht_hi_ready, 8), (turn_taken[l], 8),
                                             (ye_hi_ready[l], 8)]) as i:
                    pair_of_experts(4 * i + 2, 1)
                    pair_of_experts(4 * i + 4, 0)
                n[0] += 24 * (SLOT_ROUNDS - 1)
                pair_of_experts(10, 1)
                pair_of_experts(12, 0, after_next=False)
                pair_of_experts(14, 1, next_=False, after_next=False)
                low_ye()
                if l < DEPTH - 1:
                    leave_split()

            for t in range(TT):
                split()
                low_xt(t)
            for l in range(DEPTH):
                gated(ff[l][0], aside=(make_lambda, make_angles) if l == 0 else ())
                norm(3 * l, 2 * ALPHA, x_ready)
                hybrid(l)
                norm(3 * l + 1, ALPHA, x_ready)
                gated(ff[l][1], aside=(s5_parameters, s5_matrices) if l == DEPTH - 1 else ())
                norm(3 * l + 2, 2 * ALPHA, x_ready)
            for l in range(DEPTH):
                (s5_and_pool, stick_breaking)[l]()
                norm(6 + 2 * l, ALPHA, x_ready)
                before_experts(l)
                experts(l)
                if l < DEPTH - 1:
                    norm(7 + 2 * l, 1.0, x_ready)
                else:
                    norm(7 + 2 * l, 1.0, x_final, split_ahead=1)


def lambda_init(l):
    return 0.8 - 0.6 * math.exp(-0.3 * l)


def constants():
    c = np.zeros((P, C_END), np.float32)
    c[:, C_FREQ:C_FREQ + 32] = np.power(np.float32(10000.0), -np.arange(0, HD, 2, dtype=np.float32) / np.float32(HD))
    c[:, C_TIME:C_TIME + T] = np.arange(T)
    for g in range(2):
        c[:, C_PAR + g] = (np.arange(P) // H5) % 2 == g
    return c


def window_matrices():
    token, time = np.arange(T)[:, None], np.arange(T)[None, :]
    m = [((token <= time) & (token > time - w)) / np.minimum(time + 1, w).astype(np.float32) - (token == time)
         for w in POOL_WINDOWS]
    return np.stack(m).astype(np.float32).reshape(len(POOL_WINDOWS), TT, P, T).transpose(2, 0, 1, 3)


_NAMES = ["x", "positions", "w_in", "w_out", "diff_lambda", "diff_subln_g", "swa_sink", "ffn1_w_in", "ffn1_w_out",
          "ffn2_w_in", "ffn2_w_out", "ln_g", "ln_b", "p_2", "ab_w_in_2", "s5_lambda_re_2", "s5_lambda_im_2",
          "s5_log_dt_2", "s5_b_re_2", "s5_b_im_2", "s5_c_re_2", "s5_c_im_2", "s5_d_2", "s5_w_glu_2", "pool_w_2",
          "pool_scale_2", "ab_w_out_2", "sb_w_qkv_2", "sb_w_out_2", "ln_mix_g_2", "ln_mix_b_2", "ln_ffn_g_2",
          "ln_ffn_b_2", "router_w_2", "router_bias_2", "moe_w1_2", "moe_w3_2", "moe_w2_2", "ple_w_proj_2",
          "ple_w_gate_2"]


def kernel(**inputs):
    import concourse.bacc as bacc
    from concourse.bass_utils import run_bass_kernel_spmd

    nc = bacc.Bacc("TRN2", target_bir_lowering=False, num_devices=1)
    inputs = {**inputs, "constants": constants(), "window_matrices": window_matrices()}
    arrays, aps = {}, {}
    for name in _NAMES + ["constants", "window_matrices"]:
        arrays[name] = np.ascontiguousarray(inputs[name])
        aps[name] = nc.dram_tensor(name, arrays[name].shape, mybir.dt.from_np(arrays[name].dtype), kind="ExternalInput").ap()
    out = nc.dram_tensor("out", (1, T, D), F32, kind="ExternalOutput").ap()
    program(nc, aps, out)
    r = run_bass_kernel_spmd(nc, [arrays], core_ids=[0])
    return r.results[0]["out"]
```
